# Optimizing a Trainium2 kernel written in Bass

```python
import jax
import jax.numpy as jnp
from jax import lax
import numpy as np

D_MODEL = 1024
BATCH = 1
SEQ = 1024
DEPTH = 2

GRID_W = 64
CTX_LEN = 256
CHUNK = 64
LN_EPS = 1e-5

GLA_WIDTH = D_MODEL // 2
GLA_HEADS = 4
GLA_DV = GLA_WIDTH // GLA_HEADS
GLA_DK = GLA_DV // 2
GLA_GATE_RANK = 16
GLA_GATE_NORM = 16.0
GLA_SIZES = (GLA_HEADS * GLA_DK, GLA_HEADS * GLA_DK, GLA_WIDTH, GLA_WIDTH, GLA_GATE_RANK, GLA_GATE_RANK)
GLA_COLS = sum(GLA_SIZES)

RWKV_WIDTH = D_MODEL // 2
RWKV_HEAD_DIM = 64
RWKV_HEADS = RWKV_WIDTH // RWKV_HEAD_DIM
RWKV_DECAY_RANK = 64
RWKV_ICLR_RANK = 64
RWKV_DECAY_SCALE = 0.6065306597
RWKV_GN_EPS = 64e-5
RWKV_SIZES = (RWKV_WIDTH, RWKV_WIDTH, RWKV_WIDTH, RWKV_WIDTH, RWKV_DECAY_RANK, RWKV_DECAY_RANK, RWKV_ICLR_RANK, RWKV_ICLR_RANK)
RWKV_COLS = sum(RWKV_SIZES)
EVEN_IN = GLA_COLS + RWKV_COLS
EVEN_OUT = GLA_WIDTH + RWKV_WIDTH

MLSTM_INNER = 2 * D_MODEL
MLSTM_HEADS = 4
MLSTM_DH = MLSTM_INNER // MLSTM_HEADS
QKV_BLOCK = 4
CONV_K = 3

kernel_name = 'hybrid_gla_rwkv7_mlstm_prefix_flow_block'

def split_cols(p, sizes):
    idx = np.cumsum(sizes)[:-1].tolist()
    return jnp.split(p, idx, axis=-1)

def to_heads(t, n_heads):
    b, n, w = t.shape
    return t.reshape(b, n, n_heads, w // n_heads).transpose(0, 2, 1, 3)

def from_heads(t):
    b, h, n, d = t.shape
    return t.transpose(0, 2, 1, 3).reshape(b, n, h * d)

def layer_norm(x, g, b):
    xf = x.astype(jnp.float32)
    mu = jnp.mean(xf, -1, keepdims=True)
    var = jnp.mean(jnp.square(xf - mu), -1, keepdims=True)
    return ((xf - mu) * lax.rsqrt(var + LN_EPS) * g + b).astype(x.dtype)

def head_norm(y, eps, center):
    yf = y.astype(jnp.float32)
    if center:
        yf = yf - jnp.mean(yf, -1, keepdims=True)
    return yf * lax.rsqrt(jnp.mean(jnp.square(yf), -1, keepdims=True) + eps)

def quad_shift(p, rows, width):
    b, n, ch = p.shape
    g = p.reshape(b, rows, width, ch // 4, 4)
    left = jnp.pad(g[:, :, :-1, :, 0], ((0, 0), (0, 0), (1, 0), (0, 0)))
    right = jnp.pad(g[:, :, 1:, :, 1], ((0, 0), (0, 0), (0, 1), (0, 0)))
    up = jnp.pad(g[:, :-1, :, :, 2], ((0, 0), (1, 0), (0, 0), (0, 0)))
    down = jnp.pad(g[:, 1:, :, :, 3], ((0, 0), (0, 1), (0, 0), (0, 0)))
    return jnp.stack([left, right, up, down], axis=-1).reshape(b, n, ch)

def depthwise_conv_grid(x, w, bias, rows, width):
    b, n, ch = x.shape
    y = lax.conv_general_dilated(x.reshape(b, rows, width, ch), w, window_strides=(1, 1), padding='SAME',
                                 dimension_numbers=('NHWC', 'HWIO', 'NHWC'), feature_group_count=ch)
    return y.reshape(b, n, ch) + bias

def headwise(x, w):
    b, n, ch = x.shape
    nb, blk, _ = w.shape
    return jnp.einsum('bnjc,jcd->bnjd', x.reshape(b, n, nb, blk), w).reshape(b, n, ch)

def _chunks(t):
    b, h, n = t.shape[:3]
    t = t.reshape((b, h, n // CHUNK, CHUNK) + t.shape[3:])
    return jnp.moveaxis(t, 2, 0)

def _unchunks(t):
    t = jnp.moveaxis(t, 0, 2)
    b, h, nc, l = t.shape[:4]
    return t.reshape((b, h, nc * l) + t.shape[4:])

def gla_chunked(q, k, v, log_a, state):
    f32 = jnp.float32
    mask = jnp.tril(jnp.ones((CHUNK, CHUNK), bool))[:, :, None]

    def step(s, inp):
        qc, kc, vc, ac = inp
        bcum = jnp.cumsum(ac, axis=-2)
        inter = jnp.einsum('bhtk,bhkv->bhtv', qc * jnp.exp(bcum), s)
        diff = bcum[:, :, :, None, :] - bcum[:, :, None, :, :]
        decay = jnp.exp(jnp.where(mask, diff, -jnp.inf))
        scores = jnp.einsum('bhtk,bhsk,bhtsk->bhts', qc, kc, decay)
        intra = jnp.einsum('bhts,bhsv->bhtv', scores, vc)
        total = bcum[:, :, -1, :]
        kdec = kc * jnp.exp(total[:, :, None, :] - bcum)
        s_new = s * jnp.exp(total)[..., None] + jnp.einsum('bhsk,bhsv->bhkv', kdec, vc)
        return s_new, inter + intra

    xs = tuple(_chunks(t.astype(f32)) for t in (q, k, v, log_a))
    s_fin, out = lax.scan(step, state, xs)
    return _unchunks(out), s_fin

def rwkv7_scan(r, w, k, v, a, bvec, state):
    xs = tuple(jnp.moveaxis(t.astype(jnp.float32), 2, 0) for t in (r, w, k, v, a, bvec))

    def step(s, inp):
        r_t, w_t, k_t, v_t, a_t, b_t = inp
        sa = jnp.einsum('bhvk,bhk->bhv', s, a_t)
        s = s * w_t[:, :, None, :] + sa[..., None] * b_t[:, :, None, :] + v_t[..., None] * k_t[:, :, None, :]
        return s, jnp.einsum('bhvk,bhk->bhv', s, r_t)

    s_fin, y = lax.scan(step, state, xs)
    return jnp.moveaxis(y, 0, 2), s_fin

def mlstm_chunked(q, k, v, i_pre, log_f, state):
    f32 = jnp.float32
    mask = jnp.tril(jnp.ones((CHUNK, CHUNK), bool))

    def step(carry, inp):
        c0, n0, m0 = carry
        qc, kc, vc, ic, fc = inp
        bcum = jnp.cumsum(fc, axis=-1)
        log_d = jnp.where(mask, bcum[..., :, None] - bcum[..., None, :] + ic[..., None, :], -jnp.inf)
        log_inter = bcum + m0[..., None]
        m_t = jnp.maximum(jnp.max(log_d, axis=-1), log_inter)
        dmat = jnp.exp(log_d - m_t[..., None])
        g_inter = jnp.exp(log_inter - m_t)
        s = jnp.einsum('bhtd,bhsd->bhts', qc, kc) * dmat
        num = jnp.einsum('bhts,bhsv->bhtv', s, vc) + g_inter[..., None] * jnp.einsum('bhvk,bhtk->bhtv', c0, qc)
        den = jnp.sum(s, -1) + g_inter * jnp.einsum('bhk,bhtk->bht', n0, qc)
        h = num / jnp.maximum(jnp.abs(den), jnp.exp(-m_t))[..., None]
        tot = bcum[..., -1]
        log_w = tot[..., None] - bcum + ic
        m_new = jnp.maximum(tot + m0, jnp.max(log_w, axis=-1))
        wts = jnp.exp(log_w - m_new[..., None])
        decay0 = jnp.exp(tot + m0 - m_new)
        c_new = decay0[..., None, None] * c0 + jnp.einsum('bhsv,bhsk->bhvk', wts[..., None] * vc, kc)
        n_new = decay0[..., None] * n0 + jnp.einsum('bhs,bhsk->bhk', wts, kc)
        return (c_new, n_new, m_new), h

    xs = tuple(_chunks(t.astype(f32)) for t in (q, k, v, i_pre, log_f))
    st, out = lax.scan(step, state, xs)
    return _unchunks(out), st

def bidirectional(scan_fn, ctx_f, ctx_b, lat_f, lat_b, init):
    rev = lambda args: tuple(jnp.flip(a, axis=2) for a in args)
    yc_f, st_f = scan_fn(*ctx_f, init)
    yc_b, st_b = scan_fn(*rev(ctx_b), init)
    yl_f, _ = scan_fn(*lat_f, st_f)
    yl_b, _ = scan_fn(*rev(lat_b), st_b)
    return yc_f + jnp.flip(yc_b, axis=2), yl_f + jnp.flip(yl_b, axis=2)

def gla_branch(p_ctx, p_lat, need_ctx, wa2_f, ba_f, wa2_b, ba_b, norm_g):
    def prep(p):
        q, k, v, g, lr_f, lr_b = split_cols(p, GLA_SIZES)
        q = to_heads(q, GLA_HEADS) * (GLA_DK ** -0.5)
        k = to_heads(k, GLA_HEADS)
        v = to_heads(v, GLA_HEADS)
        la_f = to_heads(jax.nn.log_sigmoid((lr_f @ wa2_f + ba_f).astype(jnp.float32)) / GLA_GATE_NORM, GLA_HEADS)
        la_b = to_heads(jax.nn.log_sigmoid((lr_b @ wa2_b + ba_b).astype(jnp.float32)) / GLA_GATE_NORM, GLA_HEADS)
        return (q, k, v, la_f), (q, k, v, la_b), g

    cf, cb, gc = prep(p_ctx)
    lf, lb, gl = prep(p_lat)
    s0 = jnp.zeros((p_lat.shape[0], GLA_HEADS, GLA_DK, GLA_DV), jnp.float32)
    oc, ol = bidirectional(gla_chunked, cf, cb, lf, lb, s0)

    def finish(o, g):
        y = from_heads(head_norm(o, LN_EPS, False) * norm_g)
        return (y * jax.nn.silu(g.astype(jnp.float32))).astype(g.dtype)

    return (finish(oc, gc) if need_ctx else None), finish(ol, gl)

def rwkv_branch(p_ctx, p_lat, ctx_grid, lat_grid, need_ctx, mu, w0_f, ww2_f, w0_b, ww2_b,
                a0_f, wa2_f, a0_b, wa2_b, k_k, k_a, r_k, gn_g, gn_b):
    rk = r_k.reshape(RWKV_HEADS, 1, RWKV_HEAD_DIM)

    def prep(p, grid):
        p = p + (quad_shift(p, grid[0], grid[1]) - p) * mu
        r, k, v, g, wl_f, wl_b, al_f, al_b = split_cols(p, RWKV_SIZES)
        rh, vh = to_heads(r, RWKV_HEADS), to_heads(v, RWKV_HEADS)
        kk = to_heads(k * k_k, RWKV_HEADS).astype(jnp.float32)
        kk = kk * lax.rsqrt(jnp.maximum(jnp.sum(jnp.square(kk), -1, keepdims=True), 1e-24))

        def direction(w_lr, w0, ww2, a_lr, a0, wa2):
            w = jnp.exp(-RWKV_DECAY_SCALE * jax.nn.sigmoid((w0 + jnp.tanh(w_lr) @ ww2).astype(jnp.float32)))
            a = jax.nn.sigmoid(a0 + a_lr @ wa2)
            kh = to_heads(k * (1.0 + (a - 1.0) * k_a), RWKV_HEADS)
            ah = to_heads(a, RWKV_HEADS).astype(jnp.float32)
            bonus = jnp.sum(rh * kh * rk, -1, keepdims=True) * vh
            return (rh, to_heads(w, RWKV_HEADS), kh, vh, -kk, kk * ah), bonus

        fwd, bonus_f = direction(wl_f, w0_f, ww2_f, al_f, a0_f, wa2_f)
        bwd, bonus_b = direction(wl_b, w0_b, ww2_b, al_b, a0_b, wa2_b)
        return fwd, bwd, bonus_f + bonus_b, g

    cf, cb, bon_c, gc = prep(p_ctx, ctx_grid)
    lf, lb, bon_l, gl = prep(p_lat, lat_grid)
    s0 = jnp.zeros((p_lat.shape[0], RWKV_HEADS, RWKV_HEAD_DIM, RWKV_HEAD_DIM), jnp.float32)
    yc, yl = bidirectional(rwkv7_scan, cf, cb, lf, lb, s0)

    def finish(y, bonus, g):
        y = from_heads(head_norm(y, RWKV_GN_EPS, True)) * gn_g + gn_b + from_heads(bonus)
        return (y * jax.nn.silu(g.astype(jnp.float32))).astype(g.dtype)

    return (finish(yc, bon_c, gc) if need_ctx else None), finish(yl, bon_l, gl)

def mlstm_branch(p_ctx, p_lat, ctx_grid, lat_grid, need_ctx, conv_w, conv_b, wq, wk, wv,
                 wi_f, bi_f, wf_f, bf_f, wi_b, bi_b, wf_b, bf_b, norm_g, skip):
    def prep(p, grid):
        xm, z = split_cols(p, (MLSTM_INNER, MLSTM_INNER))
        xc = jax.nn.silu(depthwise_conv_grid(xm, conv_w, conv_b, grid[0], grid[1]))
        q, k, v = headwise(xc, wq), headwise(xc, wk), headwise(xm, wv)
        qkv = jnp.concatenate([q, k, v], axis=-1)
        qh = to_heads(q, MLSTM_HEADS)
        kh = to_heads(k, MLSTM_HEADS) * (MLSTM_DH ** -0.5)
        vh = to_heads(v, MLSTM_HEADS)

        def gates(wi, bi, wf, bf):
            i_pre = jnp.swapaxes((qkv @ wi + bi).astype(jnp.float32), 1, 2)
            log_f = jnp.swapaxes(jax.nn.log_sigmoid((qkv @ wf + bf).astype(jnp.float32)), 1, 2)
            return (qh, kh, vh, i_pre, log_f)

        return gates(wi_f, bi_f, wf_f, bf_f), gates(wi_b, bi_b, wf_b, bf_b), xc, z

    cf, cb, xc_c, z_c = prep(p_ctx, ctx_grid)
    lf, lb, xc_l, z_l = prep(p_lat, lat_grid)
    b = p_lat.shape[0]
    st0 = (jnp.zeros((b, MLSTM_HEADS, MLSTM_DH, MLSTM_DH), jnp.float32),
           jnp.zeros((b, MLSTM_HEADS, MLSTM_DH), jnp.float32),
           jnp.full((b, MLSTM_HEADS), -jnp.inf, jnp.float32))
    hc, hl = bidirectional(mlstm_chunked, cf, cb, lf, lb, st0)

    def finish(h, xc, z):
        y = from_heads(head_norm(h, LN_EPS, True)) * norm_g + skip * xc
        return (y * jax.nn.silu(z.astype(jnp.float32))).astype(z.dtype)

    return (finish(hc, xc_c, z_c) if need_ctx else None), finish(hl, xc_l, z_l)

def setup_inputs(seed: int = 0) -> dict:
    key = jax.random.key(seed)
    ks = iter(jax.random.split(key, 96))
    f32 = jnp.float32
    nrm = lambda shape, scale: jax.random.normal(next(ks), shape, f32) * scale
    uni = lambda shape, lo, hi: jax.random.uniform(next(ks), shape, f32, lo, hi)
    D = D_MODEL
    E = (DEPTH + 1) // 2
    O = DEPTH // 2
    beta = (8.0 * DEPTH) ** -0.25
    return {
        'x': nrm((BATCH, SEQ, D), 1.0),
        'c': nrm((BATCH, D), 1.0),
        'ctx': nrm((BATCH, CTX_LEN, D), 1.0),
        'c_ctx': nrm((D,), 1.0),
        'mod_w': nrm((DEPTH, D, 3 * D), D ** -0.5),
        'mod_b': nrm((DEPTH, 3 * D), 0.02),
        'ln_g': 1.0 + nrm((DEPTH, D), 0.02),
        'ln_b': nrm((DEPTH, D), 0.02),
        'e_w_in': nrm((E, D, EVEN_IN), D ** -0.5),
        'e_w_out': nrm((E, EVEN_OUT, D), beta * EVEN_OUT ** -0.5),
        'gla_wa2_f': nrm((E, GLA_GATE_RANK, GLA_HEADS * GLA_DK), GLA_GATE_RANK ** -0.5),
        'gla_ba_f': nrm((E, GLA_HEADS * GLA_DK), 0.1),
        'gla_wa2_b': nrm((E, GLA_GATE_RANK, GLA_HEADS * GLA_DK), GLA_GATE_RANK ** -0.5),
        'gla_ba_b': nrm((E, GLA_HEADS * GLA_DK), 0.1),
        'gla_norm_g': 1.0 + nrm((E, GLA_DV), 0.02),
        'rwkv_mu': uni((E, RWKV_COLS), 0.0, 1.0),
        'rwkv_w0_f': uni((E, RWKV_WIDTH), -6.0, 0.0),
        'rwkv_ww2_f': nrm((E, RWKV_DECAY_RANK, RWKV_WIDTH), 0.1 * RWKV_DECAY_RANK ** -0.5),
        'rwkv_w0_b': uni((E, RWKV_WIDTH), -6.0, 0.0),
        'rwkv_ww2_b': nrm((E, RWKV_DECAY_RANK, RWKV_WIDTH), 0.1 * RWKV_DECAY_RANK ** -0.5),
        'rwkv_a0_f': nrm((E, RWKV_WIDTH), 0.1),
        'rwkv_wa2_f': nrm((E, RWKV_ICLR_RANK, RWKV_WIDTH), 0.1 * RWKV_ICLR_RANK ** -0.5),
        'rwkv_a0_b': nrm((E, RWKV_WIDTH), 0.1),
        'rwkv_wa2_b': nrm((E, RWKV_ICLR_RANK, RWKV_WIDTH), 0.1 * RWKV_ICLR_RANK ** -0.5),
        'rwkv_k_k': 0.85 + nrm((E, RWKV_WIDTH), 0.02),
        'rwkv_k_a': 1.0 + nrm((E, RWKV_WIDTH), 0.02),
        'rwkv_r_k': nrm((E, RWKV_WIDTH), 0.1),
        'rwkv_gn_g': 1.0 + nrm((E, RWKV_WIDTH), 0.02),
        'rwkv_gn_b': nrm((E, RWKV_WIDTH), 0.02),
        'o_w_in': nrm((O, D, 2 * MLSTM_INNER), D ** -0.5),
        'o_w_out': nrm((O, MLSTM_INNER, D), beta * MLSTM_INNER ** -0.5),
        'ml_conv_w': nrm((O, CONV_K, CONV_K, 1, MLSTM_INNER), 1.0 / CONV_K),
        'ml_conv_b': nrm((O, MLSTM_INNER), 0.02),
        'ml_wq': nrm((O, MLSTM_INNER // QKV_BLOCK, QKV_BLOCK, QKV_BLOCK), QKV_BLOCK ** -0.5),
        'ml_wk': nrm((O, MLSTM_INNER // QKV_BLOCK, QKV_BLOCK, QKV_BLOCK), QKV_BLOCK ** -0.5),
        'ml_wv': nrm((O, MLSTM_INNER // QKV_BLOCK, QKV_BLOCK, QKV_BLOCK), QKV_BLOCK ** -0.5),
        'ml_wi_f': nrm((O, 3 * MLSTM_INNER, MLSTM_HEADS), (3 * MLSTM_INNER) ** -0.5),
        'ml_bi_f': nrm((O, MLSTM_HEADS), 0.1),
        'ml_wf_f': nrm((O, 3 * MLSTM_INNER, MLSTM_HEADS), (3 * MLSTM_INNER) ** -0.5),
        'ml_bf_f': jnp.linspace(3.0, 6.0, MLSTM_HEADS, dtype=f32) + nrm((O, MLSTM_HEADS), 0.1),
        'ml_wi_b': nrm((O, 3 * MLSTM_INNER, MLSTM_HEADS), (3 * MLSTM_INNER) ** -0.5),
        'ml_bi_b': nrm((O, MLSTM_HEADS), 0.1),
        'ml_wf_b': nrm((O, 3 * MLSTM_INNER, MLSTM_HEADS), (3 * MLSTM_INNER) ** -0.5),
        'ml_bf_b': jnp.linspace(3.0, 6.0, MLSTM_HEADS, dtype=f32) + nrm((O, MLSTM_HEADS), 0.1),
        'ml_norm_g': 1.0 + nrm((O, MLSTM_INNER), 0.02),
        'ml_skip': 1.0 + nrm((O, MLSTM_INNER), 0.02),
    }

def reference(x, c, ctx, c_ctx, mod_w, mod_b, ln_g, ln_b, e_w_in, e_w_out,
              gla_wa2_f, gla_ba_f, gla_wa2_b, gla_ba_b, gla_norm_g,
              rwkv_mu, rwkv_w0_f, rwkv_ww2_f, rwkv_w0_b, rwkv_ww2_b, rwkv_a0_f, rwkv_wa2_f,
              rwkv_a0_b, rwkv_wa2_b, rwkv_k_k, rwkv_k_a, rwkv_r_k, rwkv_gn_g, rwkv_gn_b,
              o_w_in, o_w_out, ml_conv_w, ml_conv_b, ml_wq, ml_wk, ml_wv,
              ml_wi_f, ml_bi_f, ml_wf_f, ml_bf_f, ml_wi_b, ml_bi_b, ml_wf_b, ml_bf_b,
              ml_norm_g, ml_skip):
    rows = x.shape[1] // GRID_W
    lat_grid = (rows, GRID_W)
    ctx_grid = (1, ctx.shape[1])
    alpha = (2.0 * DEPTH) ** 0.25
    xl, xc = x, ctx
    sc = jax.nn.silu(c)
    scc = jax.nn.silu(c_ctx)
    for layer in range(DEPTH):
        need_ctx = layer < DEPTH - 1
        mod_l = (sc @ mod_w[layer] + mod_b[layer])[:, None, :]
        mod_c = scc @ mod_w[layer] + mod_b[layer]
        shift_l, scale_l, gate_l = jnp.split(mod_l, 3, axis=-1)
        shift_c, scale_c, gate_c = jnp.split(mod_c, 3, axis=-1)
        hl = xl * (1.0 + scale_l) + shift_l
        hc = xc * (1.0 + scale_c) + shift_c
        j = layer // 2
        if layer % 2 == 0:
            pl = hl @ e_w_in[j]
            pc = hc @ e_w_in[j]
            gc_, gl_ = gla_branch(pc[..., :GLA_COLS], pl[..., :GLA_COLS], need_ctx,
                                  gla_wa2_f[j], gla_ba_f[j], gla_wa2_b[j], gla_ba_b[j], gla_norm_g[j])
            rc_, rl_ = rwkv_branch(pc[..., GLA_COLS:], pl[..., GLA_COLS:], ctx_grid, lat_grid, need_ctx,
                                   rwkv_mu[j], rwkv_w0_f[j], rwkv_ww2_f[j], rwkv_w0_b[j], rwkv_ww2_b[j],
                                   rwkv_a0_f[j], rwkv_wa2_f[j], rwkv_a0_b[j], rwkv_wa2_b[j],
                                   rwkv_k_k[j], rwkv_k_a[j], rwkv_r_k[j], rwkv_gn_g[j], rwkv_gn_b[j])
            out_l = jnp.concatenate([gl_, rl_], axis=-1) @ e_w_out[j]
            out_c = jnp.concatenate([gc_, rc_], axis=-1) @ e_w_out[j] if need_ctx else None
        else:
            pl = hl @ o_w_in[j]
            pc = hc @ o_w_in[j]
            mc_, ml_ = mlstm_branch(pc, pl, ctx_grid, lat_grid, need_ctx, ml_conv_w[j], ml_conv_b[j],
                                    ml_wq[j], ml_wk[j], ml_wv[j],
                                    ml_wi_f[j], ml_bi_f[j], ml_wf_f[j], ml_bf_f[j],
                                    ml_wi_b[j], ml_bi_b[j], ml_wf_b[j], ml_bf_b[j],
                                    ml_norm_g[j], ml_skip[j])
            out_l = ml_ @ o_w_out[j]
            out_c = mc_ @ o_w_out[j] if need_ctx else None
        xl = layer_norm(alpha * xl + gate_l * out_l, ln_g[layer], ln_b[layer])
        if need_ctx:
            xc = layer_norm(alpha * xc + gate_c * out_c, ln_g[layer], ln_b[layer])
    return xl


_drawn_inputs = setup_inputs


def setup_inputs(seed=0):
    import zlib

    import numpy as np

    out = dict(_drawn_inputs(seed))
    spreads = {}
    factors = {'gla_ba_f': 8.0,
     'gla_ba_b': 8.0,
     'gla_norm_g': 8.0,
     'rwkv_ww2_f': 8.0,
     'rwkv_ww2_b': 8.0,
     'rwkv_a0_f': 8.0,
     'rwkv_wa2_f': 8.0,
     'rwkv_a0_b': 8.0,
     'rwkv_wa2_b': 8.0,
     'rwkv_k_k': 5.508,
     'rwkv_k_a': 6.057,
     'rwkv_gn_g': 24.076,
     'rwkv_gn_b': 8.0,
     'ml_conv_b': 4.433,
     'ml_bi_f': 8.0,
     'ml_bi_b': 28.474,
     'ml_norm_g': 34.058,
     'ml_skip': 39.021}
    for name, (base, spread) in spreads.items():
        noise = np.random.default_rng([zlib.crc32(name.encode()), seed]).standard_normal(out[name].shape)
        drawn = base * np.exp(spread * noise) if base else spread * noise
        out[name] = jnp.asarray(drawn.astype(out[name].dtype))
    for name, factor in factors.items():
        out[name] = (out[name] * factor).astype(out[name].dtype)
    return out
```

```python
from contextlib import ExitStack, contextmanager

import numpy as np
import concourse.bass as bass
from concourse import mybir

F32 = mybir.dt.float32
I32 = mybir.dt.int32
ALU = mybir.AluOpType
ACT = mybir.ActivationFunctionType

P = 128
D = 1024
CTX = 256
SEQ = 1024
T = CTX + SEQ
KT = D // P
GRID_W = 64
ROWS = SEQ // GRID_W
CH = 128
NCH = T // CH
CTXCH = CTX // CH
PIECES = [(0, 512), (512, 512), (1024, 256)]
EPS_LN = 1e-5
EPS_GN = 64e-5
DEC = 0.6065306597
HALF = DEC * CH / 2
ALPHA = 4.0 ** 0.25
BIG = 1e30
GQ, GK, GV, GG, GLR = 0, 256, 512, 1024, 1536
RR, RK, RV, RG, RWL, RAL = 1568, 2080, 2592, 3104, 3616, 3744
E_IN = 3872
INNER = 2048
NT1 = INNER // P
HEADS1 = 4
DH = 512
ORDER = [list(range(NCH)), list(range(CTXCH - 1, -1, -1)) + list(range(NCH - 1, CTXCH - 1, -1))]

LEVELS = [1, 2, 4, 8, 16, 32, 64]


def constants():
    p = np.arange(P)[:, None]
    f = np.arange(P)[None, :]
    one = np.float32

    def lr(b):
        return ((p // (2 * b) == f // (2 * b)) & (p % (2 * b) < b) & (f % (2 * b) >= b)).astype(one)

    c = {"ident": np.eye(P, dtype=one)}
    c["ident4"] = np.tile(c["ident"], (1, 4))
    for b in LEVELS:
        m = [lr(b).T, lr(b).T, lr(b), lr(b)]
        c[f"level{b}"] = np.concatenate(m if b > 1 else m[::-1], 1)
    c["score"] = np.concatenate([(f > p), (f >= p), (f < p), (f <= p)], 1).astype(one)
    c["heads"] = ((p // 64) == (f // 64)).astype(one)
    c["ones"] = np.ones((P, P), one)
    c["eye64"] = ((p % 64) == np.arange(64)[None]).astype(one)
    c["side"] = ((p % 4) == np.arange(4)[None]).astype(one)
    c["keep"] = np.broadcast_to((np.arange(T) % CH != 0).astype(one), (P, T))
    c["neg"] = np.concatenate([np.where(f >= p, 0, -BIG), np.where(f <= p, 0, -BIG)], 1).astype(one)
    c["pick"] = np.concatenate([np.broadcast_to(p == 0, (P, P)), np.broadcast_to(p == 1, (P, P))], 1).astype(one)
    c["block4"] = ((p // 4) == (f // 4)).astype(one)
    return c


def const_layout():
    at, n = {}, 0
    for k, v in constants().items():
        at[k] = (n, n + v.shape[1])
        n += v.shape[1]
    return at, n


class Names:
    pass


@contextmanager
def phase(nc, names):
    with ExitStack() as ctx:
        handles = [ctx.enter_context(nc.semaphore(n)) for n in names.split()]
        with nc.Block() as block:
            yield block, dict(zip(names.split(), handles))
        for h in handles:
            nc.sync.sem_clear(h)
        nc.all_engine_barrier(sem_only=True)


class Steps:

    def __init__(self, eng, sem):
        self.eng, self.sem, self.n = eng, sem, 0

    def add(self, ins):
        ins.then_inc(self.sem, 1)
        self.n += 1
        return ins

    def wait(self):
        self.eng.wait_ge(self.sem, self.n)

    def publish(self, ins, sem, value):
        ins.then_inc(sem, 1)
        self.eng.wait_ge(sem, value)

    def link(self, ins):
        self.add(ins)
        self.wait()


def after(names, name):
    return names.index(name) + 1


PAIR_PARAMS = [("rwkv_mu", 0), ("rwkv_mu", 512), ("rwkv_mu", 1024), ("rwkv_mu", 1536), ("rwkv_w0_f", 0),
               ("rwkv_w0_b", 0), ("rwkv_a0_f", 0), ("rwkv_a0_b", 0), ("rwkv_k_k", 0), ("rwkv_k_a", 0),
               ("rwkv_r_k", 0), ("rwkv_gn_g", 0), ("rwkv_gn_b", 0)]
NPAIR = len(PAIR_PARAMS)
(J_MU, J_W0, J_A0, J_KK, J_KA, J_RK, J_GG, J_GB) = (0, 4, 6, 8, 9, 10, 11, 12)
V_MULR = 4 * NPAIR
V_GBA = V_MULR + 2
V_GNG = V_GBA + 4
V_C = V_GNG + 1
V_END = V_C + 16
TILE_PARAMS = 12


def setup_phase(nc, A, G):
    with ExitStack() as ctx:
        def sb(n, s):
            return ctx.enter_context(nc.sbuf_tensor(n, s, F32))
        rows = sb("param_rows", [P, 3, P])
        modw = sb("modw", [P, 4, 3 * D])
        modb = sb("modb", [2, 2, 3 * D])
        modrow = sb("modrow", [2, 2, 3 * D])
        cond = sb("cond", [P, 2, KT])
        gate = sb("gate", [P, 3, D])
        cols1 = sb("cols1", [P, 2, P])
        PS = G.PS
        sems = "consts rows_in modb_in w0 w1 w2 w3 cols cols_sb cond_sb mod_ps mod_row vec_ps vec_sb gate_ps gate_sb step stored"
        with phase(nc, sems) as (block, s):
            ring = [s["w0"], s["w1"], s["w2"], s["w3"]]

            @block.sync
            def _(sp):
                sp.dma_start(G.cst[:], A.consts).then_inc(s["consts"], 16)
                for l in range(2):
                    for k in range(KT):
                        n = l * KT + k
                        if n >= 4:
                            sp.wait_ge(s["mod_ps"], n - 3)
                        sp.dma_start(modw[:, n % 4], A.mod_w[l, k * P:(k + 1) * P, :]).then_inc(ring[n % 4], 16)
                sp.wait_ge(s["gate_sb"], 6)
                sp.dma_start(A.gates_d.rearrange("g p n -> p g n"), gate[:]).then_inc(s["stored"], 16)
                sp.wait_ge(s["cols_sb"], 3)
                for h in range(2):
                    sp.dma_start(A.cols1_d[8 * h:8 * h + 8].rearrange("i p j -> p i j"),
                                 cols1[:, h, 0:8 * TILE_PARAMS].rearrange("p (i j) -> p i j", i=8)).then_inc(s["stored"], 16)
                sp.dma_start(A.cols0_d.rearrange("i p j -> p i j"),
                             G.vc[:, 0:V_MULR].rearrange("p (i j) -> p i j", i=4)).then_inc(s["stored"], 16)
                sp.wait_ge(s["stored"], 4 * 16)

            @block.scalar
            def _(act):
                n = 0
                for j, (name, at) in enumerate(PAIR_PARAMS):
                    act.dma_start(rows[j:j + 3 * NPAIR + 1:NPAIR, 0, :],
                                  A.p[name][0, at:at + 512].rearrange("(i n) -> i n", n=P)).then_inc(s["rows_in"], 16)
                act.dma_start(rows[V_MULR:V_MULR + 2, 0, :],
                              A.p["rwkv_mu"][0, 2048:2304].rearrange("(i n) -> i n", n=P)).then_inc(s["rows_in"], 16)
                for d, name in enumerate(("gla_ba_f", "gla_ba_b")):
                    act.dma_start(rows[V_GBA + 2 * d:V_GBA + 2 * d + 2, 0, :],
                                  A.p[name][0].rearrange("(i n) -> i n", n=P)).then_inc(s["rows_in"], 16)
                act.dma_start(rows[V_GNG:V_GNG + 1, 0, :], A.p["gla_norm_g"]).then_inc(s["rows_in"], 16)
                act.dma_start(rows[V_C:V_C + 8, 0, :], A.p["c"][0].rearrange("(i n) -> i n", n=P)).then_inc(s["rows_in"], 16)
                act.dma_start(rows[V_C + 8:V_END, 0, :], A.p["c_ctx"].rearrange("(i n) -> i n", n=P)).then_inc(s["rows_in"], 16)
                one = [A.p["ml_conv_w"][0, t // 3, t % 3, 0] for t in range(9)] + \
                    [A.p[n][0] for n in ("ml_conv_b", "ml_norm_g", "ml_skip")]
                for j, v in enumerate(one):
                    v = v.rearrange("(h i n) -> h i n", h=2, n=P)
                    for h in range(2):
                        act.dma_start(rows[j:j + 7 * TILE_PARAMS + 1:TILE_PARAMS, 1 + h, :], v[h]).then_inc(s["rows_in"], 16)
                for i in range(2):
                    act.dma_start(modb[i:i + 1], A.p["mod_b"].rearrange("(o l) n -> o l n", o=1)).then_inc(s["modb_in"], 16)
                act.wait_ge(s["cols_sb"], 1)
                act.activation(cond[:], G.vc[:, V_C:V_END].rearrange("p (w k) -> p w k", w=2), ACT.Silu).then_inc(s["cond_sb"], 1)

            n_rows = NPAIR + 1 + 2 + 1 + 2 + 2 * TILE_PARAMS

            @block.tensor
            def _(pe):
                pe.wait_ge(s["consts"], 16)
                pe.wait_ge(s["rows_in"], 16 * n_rows)
                pe.transpose(PS[:, 7, 0:V_END], rows[0:V_END, 0, :], G.c("ident")[0:V_END, 0:V_END])
                m = 8 * TILE_PARAMS
                for h in range(2):
                    last = pe.transpose(PS[:, 7, P * (h + 1):P * (h + 1) + m], rows[0:m, 1 + h, :], G.c("ident")[0:m, 0:m])
                last.then_inc(s["cols"], 1)
                pe.wait_ge(s["cond_sb"], 1)
                for l in range(2):
                    for k in range(KT):
                        n = l * KT + k
                        pe.wait_ge(ring[n % 4], 16 * (n // 4 + 1))
                        if k == 0 and l:
                            pe.wait_ge(s["mod_row"], 1)
                        for j in range(6):
                            last = pe.matmul(PS[0:2, j, :], cond[:, :, k], modw[:, n % 4, 512 * j:512 * j + 512],
                                             start=(k == 0), stop=(k == KT - 1))
                        last.then_inc(s["mod_ps"], 1)
                    pe.wait_ge(s["mod_row"], 2 * l + 2)
                    if l:
                        pe.wait_ge(s["vec_sb"], l)
                    for t in range(16):
                        last = pe.transpose(PS[:, 7, 2 * t:2 * t + 2], modrow[:, l, t * P:(t + 1) * P], G.c("ident")[0:2, 0:2])
                    last.then_inc(s["vec_ps"], 1)
                    for w in range(2 - l):
                        for h in range(2):
                            n = 4 * l + 2 * w + h
                            if n:
                                pe.wait_ge(s["gate_sb"], n)
                            pe.matmul(PS[:, 6, :], G.c("pick")[0:2, w * P:(w + 1) * P],
                                      modrow[:, l, 2 * D + 512 * h:2 * D + 512 * h + 512],
                                      start=True, stop=True).then_inc(s["gate_ps"], 1)

            @block.vector
            def _(dve):
                dve.wait_ge(s["cols"], 1)
                dve.tensor_copy(G.vc[:, 0:V_END], PS[:, 7, 0:V_END]).then_inc(s["cols_sb"], 1)
                m = 8 * TILE_PARAMS
                for h in range(2):
                    dve.tensor_copy(cols1[:, h, 0:m], PS[:, 7, P * (h + 1):P * (h + 1) + m]).then_inc(s["cols_sb"], 1)
                dve.wait_ge(s["modb_in"], 32)
                for l in range(2):
                    dve.wait_ge(s["mod_ps"], KT * (l + 1))
                    dve.tensor_tensor(modrow[:, l, :], PS[0:2, 0:6, :].rearrange("p a b -> p (a b)"), modb[:, l, :],
                                      ALU.add).then_inc(s["mod_row"], 1)
                    dve.wait_ge(s["mod_row"], 2 * l + 1)
                    dve.tensor_scalar(modrow[:, l, D:2 * D], modrow[:, l, D:2 * D], 1.0, None, ALU.add).then_inc(s["mod_row"], 1)
                    dve.wait_ge(s["vec_ps"], l + 1)
                    dve.tensor_copy(G.modc[:, l], PS[:, 7, 0:32].rearrange("p (t w) -> p t w", w=2)).then_inc(s["vec_sb"], 1)
                    for w in range(2 - l):
                        for h in range(2):
                            dve.wait_ge(s["gate_ps"], 4 * l + 2 * w + h + 1)
                            dve.tensor_copy(gate[:, 2 * l + w, 512 * h:512 * h + 512], PS[:, 6, :]).then_inc(s["gate_sb"], 1)


def modulate_phase(nc, A, G, layer, xnat, hT, load):
    PS = G.PS
    jobs = [(k, at, w) for k in range(KT) for at, w in ((0, CTX), (CTX, 512), (CTX + 512, 512))]
    with phase(nc, "x_in turned taken") as (block, s):
        @block.sync
        def _(sp):
            if load:
                sp.dma_start(xnat[:, 0:CTXCH, :], A.ctx[0].rearrange("(c p) d -> p c d", p=P)).then_inc(s["x_in"], 16)
                sp.dma_start(xnat[:, CTXCH:NCH, :], A.x[0].rearrange("(c p) d -> p c d", p=P)).then_inc(s["x_in"], 16)

        @block.tensor
        def _(pe):
            if load:
                pe.wait_ge(s["x_in"], 32)
            for n, (k, at, w) in enumerate(jobs):
                if n >= 4:
                    pe.wait_ge(s["taken"], n - 3)
                for i in range(w // P):
                    last = pe.transpose(PS[:, n % 4, i * P:(i + 1) * P], xnat[:, at // P + i, k * P:(k + 1) * P], G.c("ident"))
                last.then_inc(s["turned"], 1)

        @block.vector
        def _(dve):
            for n, (k, at, w) in enumerate(jobs):
                which = 1 if at < CTX else 0
                dve.wait_ge(s["turned"], n + 1)
                dve.tensor_scalar(hT[:, k, at:at + w], PS[:, n % 4, 0:w], G.modc[:, layer, 8 + k, which:which + 1],
                                  G.modc[:, layer, k, which:which + 1], ALU.mult, ALU.add).then_inc(s["taken"], 1)


def project(pe, PS, bank, w, hT, at=0, rows=P, cols=slice(0, P)):
    for off, n in PIECES if at == 0 else [(0, 512), (512, 512)]:
        for k in range(KT):
            last = pe.matmul(PS[0:rows, bank + off // 512, 0:n], w[:, k, cols], hT[:, k, at + off:at + off + n],
                             start=(k == 0), stop=(k == KT - 1))
    return last


def flat(PS, bank, rows=P, n=T):
    return PS[0:rows, bank:bank + 3, :].rearrange("p a b -> p (a b)")[:, 0:n]


def shift_mix(dve, step, raw, out, keep, mus, done=None, value=0):
    step.link(dve.tensor_scalar(out[:], raw[:], keep, None, ALU.mult))
    lat_o = out[:, CTX:].rearrange("p (r w) -> p r w", w=GRID_W)
    lat_r = raw[:, CTX:].rearrange("p (r w) -> p r w", w=GRID_W)
    W = GRID_W
    moves = [(0, lat_o[:, :, 1:], lat_r[:, :, :W - 1]), (1, lat_o[:, :, :W - 1], lat_r[:, :, 1:]),
             (2, lat_o[:, 1:, :], lat_r[:, :ROWS - 1, :]), (3, lat_o[:, :ROWS - 1, :], lat_r[:, 1:, :]),
             (0, out[:, 1:CTX], raw[:, 0:CTX - 1]), (1, out[:, 0:CTX - 1], raw[:, 1:CTX])]
    for n, (d, o, r) in enumerate(moves):
        ins = dve.scalar_tensor_tensor(o, r, mus[:, d:d + 1], o, ALU.mult, ALU.add)
        if n == len(moves) - 1 and done is not None:
            step.publish(ins, done, value)
        else:
            step.link(ins)


def lowrank_phase(nc, A, G, LW, LA):
    with ExitStack() as ctx:
        def sb(n, s):
            return ctx.enter_context(nc.sbuf_tensor(n, s, F32))
        w = sb("w_lr", [P, KT, 32 + 256])
        lg = sb("lr_gla", [32, T])
        raw = sb("lr_raw", [P, 2, T])
        mixed = sb("lr_mixed", [P, T])
        mus = sb("lr_mus", [P, 2, 4])
        keep = sb("lr_keep", [P, 2])
        PS = G.PS
        with phase(nc, "w_in prod taken mixed_ok step finished stored") as (block, s):
            @block.sync
            def _(sp):
                v = A.p["e_w_in"][0].rearrange("(k p) n -> p k n", p=P)
                sp.dma_start(w[:, :, 0:32], v[:, :, GLR:GLR + 32]).then_inc(s["w_in"], 16)
                sp.dma_start(w[:, :, 32:288], v[:, :, RWL:RWL + 256]).then_inc(s["w_in"], 16)
                sp.wait_ge(s["taken"], 1)
                sp.dma_start(A.lg_d, lg[:]).then_inc(s["stored"], 16)
                sp.wait_ge(s["stored"], 16)

            @block.tensor
            def _(pe):
                pe.wait_ge(s["w_in"], 32)
                project(pe, G.PS, 0, w, G.hT, rows=32, cols=slice(0, 32)).then_inc(s["prod"], 1)
                project(pe, G.PS, 3, w, G.hT, cols=slice(32, 160)).then_inc(s["prod"], 1)
                pe.wait_ge(s["taken"], 1)
                project(pe, G.PS, 0, w, G.hT, cols=slice(160, 288)).then_inc(s["prod"], 1)

            @block.scalar
            def _(act):
                act.wait_ge(s["prod"], 1)
                act.activation(lg[:], flat(PS, 0, 32), ACT.Copy).then_inc(s["taken"], 1)
                for i in range(2):
                    act.wait_ge(s["prod"], 2 + i)
                    act.activation(raw[:, i], flat(PS, 3 * (1 - i)), ACT.Copy).then_inc(s["taken"], 1)
                act.wait_ge(s["mixed_ok"], 1)
                act.activation(LW[:], mixed[:], ACT.Tanh).then_inc(s["finished"], 1)

            @block.vector
            def _(dve):
                step = Steps(dve, s["step"])
                for i in range(2):
                    mu = G.vc[:, V_MULR + i:V_MULR + i + 1]
                    step.add(dve.tensor_scalar(mus[:, i], G.c("side"), mu, None, ALU.mult))
                    step.link(dve.tensor_scalar(keep[:, i:i + 1], mu, -1.0, 1.0, ALU.mult, ALU.add))
                for i in range(2):
                    dve.wait_ge(s["taken"], 2 + i)
                    shift_mix(dve, step, raw[:, i], (mixed, LA)[i], keep[:, i:i + 1], mus[:, i], s["mixed_ok"], i + 1)


PREP_JOBS = ["w0", "a0", "w1", "a1", "k", "r", "ksum", "v", "g", "bonus"]
ACT_PREP = ["w0", "a0", "w1", "a1", "k", "r", "e0", "e1", "sqrt", "v", "g", "silu"]
DVE_PREP = ["c0", "c1", "K", "sq", "R", "ksum", "rk", "V", "G", "bonus", "ready"]


def rwkv_prep(nc, A, G, B, p):
    with ExitStack() as ctx:
        def sb(n, s):
            return ctx.enter_context(nc.sbuf_tensor(n, s, F32))
        w = sb("w_pair", [P, 2, KT, P])
        wlr = sb("w_pair_lr", [P, 2, P])
        raw = sb("raw", [P, 2, T])
        R, K, kk, tmp = sb("R", [P, T]), sb("K", [P, T]), sb("kk", [P, T]), sb("tmp", [P, T])
        sg, aa = sb("sg", [P, 2, T]), sb("aa", [P, 2, T])
        mus, keep = sb("mus", [P, 4, 4]), sb("keep_mu", [P, 4])
        ka1 = sb("ka1", [P, 1])
        half = sb("half", [P, 2])
        khs = B.bonus
        PS = G.PS

        def col(j):
            return B.cols[:, j:j + 1]

        sems = "cols_in lr_in w_in0 w_in1 prod act_out dve_out step act_step consts_ok"
        with phase(nc, sems) as (block, s):
            w_in = [s["w_in0"], s["w_in1"]]

            @block.sync
            def _(sp):
                sp.dma_start(B.cols[:], A.cols0_d[bass.ds(p, 1)].rearrange("o p j -> p (o j)")).then_inc(s["cols_in"], 16)
                for d in range(2):
                    for i, n in enumerate(("rwkv_ww2_", "rwkv_wa2_")):
                        sp.dma_start(wlr[64 * d:64 * d + 64, i], A.p[n + "fb"[d]][0][:, bass.ds(p * P, P)]).then_inc(s["lr_in"], 16)
                win = A.p["e_w_in"][0].rearrange("(k p) n -> p k n", p=P)
                for n, at in enumerate((RK, RR, RV, RG)):
                    if n >= 2:
                        sp.wait_ge(s["prod"], after(PREP_JOBS, ("k", "r")[n - 2]))
                    sp.dma_start(w[:, n % 2], win[:, :, bass.ds(p * P + at, P)]).then_inc(w_in[n % 2], 16)

            @block.tensor
            def _(pe):
                def lowrank(n, src, i, d):
                    for off, m in PIECES:
                        last = pe.matmul(PS[:, 3 * (n % 2) + off // 512, 0:m], wlr[64 * d:64 * d + 64, i],
                                         src[64 * d:64 * d + 64, off:off + m], start=True, stop=True)
                    return last

                def head_sum(n, src):
                    for off, m in PIECES:
                        last = pe.matmul(PS[:, 3 * (n % 2) + off // 512, 0:m], G.c("heads"), src[:, off:off + m],
                                         start=True, stop=True)
                    return last

                pe.wait_ge(s["lr_in"], 64)
                for n, job in enumerate(PREP_JOBS):
                    if n >= 2:
                        before = PREP_JOBS[n - 2]
                        if before == "ksum":
                            pe.wait_ge(s["dve_out"], after(DVE_PREP, "ksum"))
                        else:
                            pe.wait_ge(s["act_out"], after(ACT_PREP, before))
                    if job in ("w0", "w1"):
                        last = lowrank(n, B.LW, 0, int(job[1]))
                    elif job in ("a0", "a1"):
                        last = lowrank(n, B.LA, 1, int(job[1]))
                    elif job == "ksum":
                        pe.wait_ge(s["dve_out"], after(DVE_PREP, "sq"))
                        last = head_sum(n, tmp)
                    elif job == "bonus":
                        pe.wait_ge(s["dve_out"], after(DVE_PREP, "rk"))
                        last = head_sum(n, tmp)
                    else:
                        i = "krvg".index(job)
                        pe.wait_ge(w_in[i % 2], 16 * (i // 2 + 1))
                        last = project(pe, PS, 3 * (n % 2), w[:, i % 2], G.hT)
                    last.then_inc(s["prod"], 1)

            @block.scalar
            def _(act):
                def job(name):
                    act.wait_ge(s["prod"], after(PREP_JOBS, name))
                    return flat(PS, 3 * (PREP_JOBS.index(name) % 2))

                act.wait_ge(s["cols_in"], 16)
                for d in range(2):
                    act.activation(sg[:, d], job(f"w{d}"), ACT.Sigmoid, bias=col(J_W0 + d)).then_inc(s["act_out"], 1)
                    act.activation(aa[:, d], job(f"a{d}"), ACT.Sigmoid, bias=col(J_A0 + d)).then_inc(s["act_out"], 1)
                act.activation(raw[:, 0], job("k"), ACT.Copy).then_inc(s["act_out"], 1)
                act.activation(raw[:, 1], job("r"), ACT.Copy).then_inc(s["act_out"], 1)
                act.wait_ge(s["consts_ok"], 2)
                for d in range(2):
                    act.wait_ge(s["dve_out"], after(DVE_PREP, f"c{d}"))
                    act.activation(B.kt[:, d], B.rt[:, d], ACT.Exp, scale=DEC, bias=half[:, 1:2])
                    ends = B.rt[:, d].rearrange("p (c t) -> p c t", t=CH)[:, :, (CH - 1) * (1 - d)]
                    act.activation(B.PL[:, d], ends, ACT.Exp, scale=-DEC).then_inc(s["act_step"], 1)
                    act.activation(B.at[:, d], B.at[:, d], ACT.Exp, scale=-DEC, bias=half[:, 0:1])
                    act.wait_ge(s["act_step"], d + 1)
                    act.activation(B.rt[:, d], B.rt[:, d], ACT.Exp, scale=-DEC, bias=half[:, 0:1]).then_inc(s["act_out"], 1)
                act.wait_ge(s["dve_out"], after(DVE_PREP, "ksum"))
                act.activation(tmp[:], tmp[:], ACT.Sqrt).then_inc(s["act_out"], 1)
                act.wait_ge(s["dve_out"], after(DVE_PREP, "K"))
                act.activation(raw[:, 0], job("v"), ACT.Copy).then_inc(s["act_out"], 1)
                act.activation(raw[:, 1], job("g"), ACT.Copy).then_inc(s["act_out"], 1)
                act.wait_ge(s["dve_out"], after(DVE_PREP, "G"))
                act.activation(B.sG[:], B.sG[:], ACT.Silu).then_inc(s["act_out"], 1)

            @block.vector
            def _(dve):
                step = Steps(dve, s["step"])
                out = Steps(dve, s["dve_out"])

                def from_act(name):
                    dve.wait_ge(s["act_out"], after(ACT_PREP, name))

                dve.memset(half[:, 0:1], HALF).then_inc(s["consts_ok"], 1)
                dve.memset(half[:, 1:2], -HALF).then_inc(s["consts_ok"], 1)
                dve.wait_ge(s["cols_in"], 16)
                step.add(dve.tensor_scalar(keep[:], B.cols[:, 0:4], -1.0, 1.0, ALU.mult, ALU.add))
                step.add(dve.tensor_scalar(ka1[:], col(J_KA), -1.0, 1.0, ALU.mult, ALU.add))
                for j in range(4):
                    step.add(dve.tensor_scalar(mus[:, j], G.c("side"), col(j), None, ALU.mult))
                step.wait()

                def mix(j, src, dst):
                    shift_mix(dve, step, src, dst, keep[:, j:j + 1], mus[:, j], s["dve_out"], out.n + 1)
                    out.n += 1

                for d in range(2):
                    from_act(f"a{d}")
                    c, x = (B.rt[:, d], sg[:, d]) if d == 0 else (B.rt[:, d][:, ::-1], sg[:, d][:, ::-1])
                    step.link(dve.tensor_tensor_scan(c, G.c("keep"), x, 0.0, ALU.mult, ALU.add))
                    out.add(dve.tensor_tensor(B.at[:, d], B.rt[:, d], sg[:, d], ALU.subtract))
                from_act("k")
                mix(1, raw[:, 0], K)
                step.link(dve.tensor_scalar(kk[:], K[:], col(J_KK), None, ALU.mult))
                out.add(dve.tensor_tensor(tmp[:], kk[:], kk[:], ALU.mult))
                from_act("r")
                mix(0, raw[:, 1], R)
                dve.wait_ge(s["prod"], after(PREP_JOBS, "ksum"))
                out.add(dve.tensor_scalar(tmp[:], flat(PS, 3 * (PREP_JOBS.index("ksum") % 2)), 1e-24, None, ALU.max))
                from_act("sqrt")
                step.link(dve.reciprocal(tmp[:], tmp[:]))
                step.link(dve.tensor_tensor(kk[:], kk[:], tmp[:], ALU.mult))
                for d in range(2):
                    step.link(dve.tensor_scalar(tmp[:], aa[:, d], col(J_KA), ka1[:], ALU.mult, ALU.add))
                    kh = khs if d == 0 else tmp
                    step.add(dve.tensor_tensor(kh[:], K[:], tmp[:], ALU.mult))
                    step.link(dve.tensor_tensor(aa[:, d], kk[:], aa[:, d], ALU.mult))
                    from_act(f"e{d}")
                    step.add(dve.tensor_tensor(B.bt[:, d], aa[:, d], B.kt[:, d], ALU.mult))
                    step.add(dve.tensor_tensor(B.rt[:, d], R[:], B.rt[:, d], ALU.mult))
                    step.add(dve.scalar_tensor_tensor(B.at[:, d], kk[:], -1.0, B.at[:, d], ALU.mult, ALU.mult))
                    step.link(dve.tensor_tensor(B.kt[:, d], kh[:], B.kt[:, d], ALU.mult))
                step.link(dve.tensor_tensor(khs[:], khs[:], tmp[:], ALU.add))
                out.add(dve.scalar_tensor_tensor(tmp[:], R[:], col(J_RK), khs[:], ALU.mult, ALU.mult))
                from_act("v")
                mix(2, raw[:, 0], B.V)
                from_act("g")
                mix(3, raw[:, 1], B.sG)
                dve.wait_ge(s["prod"], after(PREP_JOBS, "bonus"))
                out.add(dve.tensor_tensor(B.bonus[:], flat(PS, 3), B.V[:], ALU.mult))


PE_CHUNK = ["nat", "bx", "kx", "X1"] + [f"{x}{b}" for b in LEVELS[1:] for x in "YDT"] + ["Z", "WU", "out"]
ACT_CHUNK = ["nat", "I", "X1"] + [f"{x}{b}" for b in LEVELS[1:] for x in "YT"] + ["WU", "out"]
DVE_CHUNK = ["bx", "kx", "XT1"] + [f"X{b}" for b in LEVELS[1:]] + ["Z", "out"]
SLOTS = 2


def rwkv_chunks(nc, A, G, B):
    with ExitStack() as ctx:
        def sb(n, s):
            return ctx.enter_context(nc.sbuf_tensor(n, s, F32))
        AZ = [sb(f"AZ{i}", [P, 2, 2, 2, 64]) for i in range(SLOTS)]
        NAT = [sb(f"NAT{i}", [P, 2, 2, P]) for i in range(SLOTS)]
        VN = [sb(f"VN{i}", [P, P]) for i in range(SLOTS)]
        NR = [sb(f"NR{i}", [P, 2, 2, 2, P]) for i in range(SLOTS)]
        AR = [sb(f"AR{i}", [P, 2, 2, 2, P]) for i in range(SLOTS)]
        RK_ = [sb(f"RKS{i}", [P, 2, P]) for i in range(SLOTS)]
        X = [sb(f"X{i}", [P, 4, P]) for i in range(SLOTS)]
        XT = [sb(f"XT{i}", [P, 4, P]) for i in range(SLOTS)]
        Y = [sb(f"Y{i}", [P, 4, P]) for i in range(SLOTS)]
        WU = [sb(f"WU{i}", [P, 4, P]) for i in range(SLOTS)]
        PS = G.PS
        with phase(nc, "pe0 pe1 act0 act1 dve0 dve1") as (block, s):
            done = {"pe": [s["pe0"], s["pe1"]], "act": [s["act0"], s["act1"]], "dve": [s["dve0"], s["dve1"]]}
            names = {"pe": PE_CHUNK, "act": ACT_CHUNK, "dve": DVE_CHUNK}

            def need(eng, c, engine, name, back=0):
                n = c // SLOTS - back
                if n >= 0:
                    eng.wait_ge(done[engine][c % SLOTS], n * len(names[engine]) + after(names[engine], name))

            def bank(c, i):
                return PS[:, 4 * (c % SLOTS) + i, :]

            def tokens(c):
                return slice(CH * c, CH * c + CH)

            @block.tensor
            def _(pe):
                def stage(c, name):
                    i, t = c % SLOTS, tokens(c)
                    b0, b1, b2, b3 = (bank(c, j) for j in range(4))
                    if name == "nat":
                        need(pe, c, "dve", "Z", 1)
                        need(pe, c, "act", "WU", 1)
                        for d, b in enumerate((b0, b1)):
                            for j, x in enumerate((B.bt, B.kt, B.at)):
                                last = pe.transpose(b[:, j * P:(j + 1) * P], x[:, d, t], G.c("ident"))
                        last = pe.transpose(b0[:, 3 * P:4 * P], B.V[:, t], G.c("ident"))
                    elif name in ("bx", "kx"):
                        if name == "bx":
                            need(pe, c, "dve", "out", 1)
                            need(pe, c, "act", "out", 1)
                        else:
                            need(pe, c, "act", "nat")
                        for h in range(2):
                            q = slice(64 * h, 64 * h + 64)
                            b = ((b2, b3) if name == "bx" else (b0, b1))[h]
                            for d in range(2):
                                for j, x in enumerate((B.at, B.rt)):
                                    last = pe.matmul(b[:, (2 * d + j) * P:(2 * d + j + 1) * P],
                                                     (B.bt if name == "bx" else B.kt)[q, d, t], x[q, d, t],
                                                     start=True, stop=True)
                    elif name[0] in "XT":
                        if name == "X1":
                            need(pe, c, "dve", "XT1")
                        else:
                            need(pe, c, "dve", "X" + name[1:])
                        for u in range(4):
                            last = pe.transpose(b2[:, u * P:(u + 1) * P], (XT if name == "X1" else X)[i][:, u], G.c("ident"))
                    elif name[0] == "Y":
                        l = LEVELS.index(int(name[1:]))
                        if l == 1:
                            need(pe, c, "act", "X1")
                        else:
                            need(pe, c, "dve", f"X{LEVELS[l - 1]}")
                        for u in range(4):
                            last = pe.matmul(b0[:, u * P:(u + 1) * P], NR[i][:, u % 2, u // 2, 0], X[i][:, u], start=True, stop=True)
                    elif name[0] == "D":
                        need(pe, c, "act", "Y" + name[1:])
                        for u in range(4):
                            last = pe.matmul(b1[:, u * P:(u + 1) * P], XT[i][:, u], Y[i][:, u], start=True, stop=True)
                    elif name == "Z":
                        for u in range(4):
                            last = pe.matmul(b0[:, u * P:(u + 1) * P], AR[i][:, u % 2, u // 2, 0], VN[i][:], start=True, stop=True)
                    elif name == "WU":
                        need(pe, c, "dve", "Z")
                        need(pe, c, "act", f"T{LEVELS[-1]}")
                        for u in range(4):
                            last = pe.matmul(b1[:, u * P:(u + 1) * P], XT[i][:, u],
                                             AZ[i][:, u // 2, u % 2].rearrange("p a b -> p (a b)"), start=True, stop=True)
                    else:
                        need(pe, c, "act", "WU")
                        for h in range(2):
                            q = slice(64 * h, 64 * h + 64)
                            for d in range(2):
                                W, U = WU[i][:, 2 * d + h, 0:64], WU[i][:, 2 * d + h, 64:128]
                                b_, k_ = NAT[i][:, d, 0, q], NAT[i][:, d, 1, q]
                                pe.matmul(b2[q, d * P:(d + 1) * P], W, NR[i][:, h, d, 1], start=True, stop=True)
                                pe.matmul(b2[q, 256 + 64 * d:320 + 64 * d], W, b_, start=True, stop=True)
                                pe.matmul(b2[q, 384 + 64 * d:448 + 64 * d], b_, U, start=True, stop=False)
                                pe.matmul(b2[q, 384 + 64 * d:448 + 64 * d], k_, VN[i][:, q], start=False, stop=True)
                            for d in range(2):
                                pe.matmul(b3[q, 0:P], WU[i][:, 2 * d + h, 64:128], NR[i][:, h, d, 1], start=(d == 0), stop=False)
                            last = pe.matmul(b3[q, 0:P], VN[i][:, q], RK_[i][:, h], start=False, stop=True)
                    last.then_inc(done["pe"][i], 1)

                for c in range(0, NCH, SLOTS):
                    for name in [n for n in PE_CHUNK]:
                        for i in range(SLOTS):
                            stage(c + i, name)

            @block.scalar
            def _(act):
                def stage(c, name):
                    i = c % SLOTS
                    b0, b1, b2, b3 = (bank(c, j) for j in range(4))
                    if name != "I":
                        need(act, c, "pe", name)
                    if name == "nat":
                        for d, b in enumerate((b0, b1)):
                            act.activation(NAT[i][:, d].rearrange("p a b -> p (a b)"), b[:, 0:2 * P], ACT.Copy)
                            act.activation(AZ[i][:, d, :, 0, :], b[:, 2 * P:3 * P].rearrange("p (h n) -> p h n", h=2), ACT.Copy)
                        last = act.activation(VN[i][:], b0[:, 3 * P:4 * P], ACT.Copy)
                    elif name == "I":
                        last = act.activation(XT[i][:].rearrange("p a b -> p (a b)"), G.c("ident4"), ACT.Copy)
                    elif name == "out":
                        last = act.activation(B.Y[:, tokens(c)], b3[:, 0:P], ACT.Copy)
                    else:
                        dst, b = {"X": (X, b2), "T": (XT, b2), "Y": (Y, b0), "W": (WU, b1)}[name[0]]
                        last = act.activation(dst[i][:].rearrange("p a b -> p (a b)"), b, ACT.Copy)
                    last.then_inc(done["act"][i], 1)

                for c in range(0, NCH, SLOTS):
                    for name in ACT_CHUNK:
                        for i in range(SLOTS):
                            stage(c + i, name)

            @block.vector
            def _(dve):
                def stage(c, name):
                    i = c % SLOTS
                    b0, b1, b2, b3 = (bank(c, j) for j in range(4))
                    if name in ("bx", "kx"):
                        need(dve, c, "pe", name)
                        for h, b in enumerate((b2, b3) if name == "bx" else (b0, b1)):
                            last = dve.tensor_tensor((NR if name == "bx" else AR)[i][:, h].rearrange("p a b c -> p (a b c)"),
                                                     b, G.c("score"), ALU.mult)
                    elif name == "XT1":
                        need(dve, c, "act", "I")
                        need(dve, c, "dve", "kx")
                        dve.tensor_tensor(RK_[i][:], AR[i][:, :, 0, 1], AR[i][:, :, 1, 1], ALU.add)
                        last = dve.copy_predicated(XT[i][:].rearrange("p (d h) n -> p d h n", d=2),
                                                   G.c("level1").bitcast(I32).rearrange("p (d h n) -> p d h n", d=2, h=2),
                                                   NR[i][:, :, :, 0].rearrange("p h d n -> p d h n"))
                    elif name == "Z":
                        need(dve, c, "pe", "Z")
                        for h in range(2):
                            last = dve.tensor_copy(AZ[i][:, :, h, 1, :],
                                                   b0.rearrange("p (d h n) -> p d h n", d=2, h=2)[:, :, h, 64 * h:64 * h + 64])
                    elif name == "out":
                        need(dve, c, "pe", "out")
                        dve.tensor_tensor(B.QT[:, c], b2[:, 0:256].rearrange("p (d t) -> p d t", d=2), B.rt[:, :, tokens(c)], ALU.add)
                        dve.tensor_tensor(B.HS[:, c], b2[:, 384:512].rearrange("p (d t) -> p d t", d=2),
                                          B.PL[:, :, c:c + 1].broadcast_to([P, 2, 64]), ALU.mult)
                        last = dve.tensor_tensor(B.GT[:, c], b2[:, 256:384].rearrange("p (d t) -> p d t", d=2),
                                                 G.c("eye64")[:, None, :].broadcast_to([P, 2, 64]), ALU.add)
                    else:
                        need(dve, c, "pe", "D" + name[1:])
                        last = dve.copy_predicated(X[i][:].rearrange("p a b -> p (a b)"), G.c("level" + name[1:]).bitcast(I32), b1)
                    last.then_inc(done["dve"][i], 1)

                for c in range(0, NCH, SLOTS):
                    for name in DVE_CHUNK:
                        for i in range(SLOTS):
                            stage(c + i, name)


def chunk_chain(d):
    return list(zip(ORDER[d][:-1], ORDER[d][1:]))


def rwkv_finish(nc, A, G, B, p):
    with ExitStack() as ctx:
        def sb(n, s):
            return ctx.enter_context(nc.sbuf_tensor(n, s, F32))
        S = sb("S_rwkv", [P, 2, NCH, 64])
        yc, sq = sb("y_centered", [P, T]), sb("y_square", [P, T])
        eps = sb("eps_gn", [P, 1])
        PS = G.PS

        def col(j):
            return B.cols[:, j:j + 1]

        with phase(nc, "zero chain state0 state1 read_ps read_sb mean_ps centered squared var_ps root step stored eps_ok") as (block, s):
            state = [s["state0"], s["state1"]]

            @block.tensor
            def _(pe):
                pe.wait_ge(s["zero"], 2)
                for n in range(NCH - 1):
                    for d in range(2):
                        c = ORDER[d][n]
                        if n:
                            pe.wait_ge(state[d], n)
                        for h in range(2):
                            q = slice(64 * h, 64 * h + 64)
                            last = pe.matmul(PS[q, d, 0:64], B.GT[q, c, d], S[q, d, c], start=True, stop=True)
                        last.then_inc(s["chain"], 1)
                for d in range(2):
                    pe.wait_ge(state[d], NCH - 1)
                for c in range(NCH):
                    for h in range(2):
                        q = slice(64 * h, 64 * h + 64)
                        for d in range(2):
                            last = pe.matmul(PS[q, 2 + c // 4, (c % 4) * P:(c % 4 + 1) * P], S[q, d, c], B.QT[q, c, d],
                                             start=(d == 0), stop=(d == 1))
                last.then_inc(s["read_ps"], 1)
                pe.wait_ge(s["read_sb"], 1)
                for off, m in PIECES:
                    last = pe.matmul(PS[:, 5 + off // 512, 0:m], G.c("heads"), B.Y[:, off:off + m], start=True, stop=True)
                last.then_inc(s["mean_ps"], 1)
                pe.wait_ge(s["squared"], 1)
                for off, m in PIECES:
                    last = pe.matmul(PS[:, 2 + off // 512, 0:m], G.c("heads"), sq[:, off:off + m], start=True, stop=True)
                last.then_inc(s["var_ps"], 1)

            @block.scalar
            def _(act):
                act.wait_ge(s["centered"], 1)
                act.activation(sq[:], yc[:], ACT.Square).then_inc(s["squared"], 1)
                act.wait_ge(s["var_ps"], 1)
                act.wait_ge(s["eps_ok"], 1)
                act.activation(sq[:], flat(PS, 2), ACT.Sqrt, scale=1.0 / 64, bias=eps[:]).then_inc(s["root"], 1)

            @block.vector
            def _(dve):
                step = Steps(dve, s["step"])
                dve.memset(eps[:], EPS_GN).then_inc(s["eps_ok"], 1)
                for d in range(2):
                    dve.memset(S[:, d, ORDER[d][0]], 0.0).then_inc(s["zero"], 1)
                for n in range(NCH - 1):
                    for d in range(2):
                        c, c1 = ORDER[d][n], ORDER[d][n + 1]
                        dve.wait_ge(s["chain"], 2 * n + d + 1)
                        dve.scalar_tensor_tensor(S[:, d, c1], PS[:, d, 0:64], B.PL[:, d, c:c + 1], B.HS[:, c, d],
                                                 ALU.mult, ALU.add).then_inc(state[d], 1)
                dve.wait_ge(s["read_ps"], 1)
                step.publish(dve.tensor_tensor(B.Y[:], flat(PS, 2), B.Y[:], ALU.add), s["read_sb"], 1)
                dve.wait_ge(s["mean_ps"], 1)
                step.publish(dve.scalar_tensor_tensor(yc[:], flat(PS, 5), -1.0 / 64, B.Y[:], ALU.mult, ALU.add), s["centered"], 1)
                dve.wait_ge(s["root"], 1)
                step.link(dve.reciprocal(sq[:], sq[:]))
                step.link(dve.tensor_tensor(yc[:], yc[:], sq[:], ALU.mult))
                step.link(dve.tensor_scalar(yc[:], yc[:], col(J_GG), col(J_GB), ALU.mult, ALU.add))
                step.link(dve.tensor_tensor(yc[:], yc[:], B.bonus[:], ALU.add))
                step.publish(dve.tensor_tensor(yc[:], yc[:], B.sG[:], ALU.mult), s["read_sb"], 2)

            @block.sync
            def _(sp):
                sp.wait_ge(s["read_sb"], 2)
                sp.dma_start(A.yT_d[bass.ds(p + 4, 1)].rearrange("o p t -> p (o t)"), yc[:]).then_inc(s["stored"], 16)
                sp.wait_ge(s["stored"], 16)


GLA_JOBS = ["x0", "x1", "q", "k", "g0", "g1"]
ACT_GLA = ["x0", "l0", "x1", "l1", "q", "k", "g0", "g1", "eq0", "ek0", "eq1", "ek1"]
DVE_GLA = ["b0", "b1", "kd0", "kd1"]


def gla_prep(nc, A, G, B, g):
    with ExitStack() as ctx:
        def sb(n, s):
            return ctx.enter_context(nc.sbuf_tensor(n, s, F32))
        w = sb("w_gla", [P, 2, KT, P])
        wv = sb("w_gla_v", [P, KT, 2 * P])
        wa2 = sb("wa2", [32, 2, P])
        lg = sb("lg", [32, T])
        ba = sb("gla_ba", [P, 2])
        x, l, kd = sb("gla_x", [P, 2, T]), sb("gla_l", [P, 2, T]), sb("gla_kd", [P, 2, T])
        PS = G.PS
        sems = "zeroed lr_in w_in0 w_in1 wv_in prod v_ps v_sb act_out dve_out step act_step turned kn_sb"
        with phase(nc, sems) as (block, s):
            w_in = [s["w_in0"], s["w_in1"]]

            @block.sync
            def _(sp):
                sp.wait_ge(s["zeroed"], 1)
                for d in range(2):
                    sp.dma_start(wa2[16 * d:16 * d + 16, d], A.p["gla_wa2_" + "fb"[d]][0][:, bass.ds(g * P, P)]).then_inc(s["lr_in"], 16)
                    sp.dma_start(ba[:, d:d + 1], A.p["gla_ba_" + "fb"[d]][0][bass.ds(g * P, P)].rearrange("(p o) -> p o", o=1)).then_inc(s["lr_in"], 16)
                sp.dma_start(lg[:], A.lg_d).then_inc(s["lr_in"], 16)
                win = A.p["e_w_in"][0].rearrange("(k p) n -> p k n", p=P)
                starts = [g * P + GQ, g * P + GK, g * 2 * P + GG, g * 2 * P + (GG + P)]
                for n, at in enumerate(starts):
                    if n >= 2:
                        sp.wait_ge(s["prod"], after(GLA_JOBS, ("q", "k")[n - 2]))
                    sp.dma_start(w[:, n % 2], win[:, :, bass.ds(at, P)]).then_inc(w_in[n % 2], 16)
                    if n == 1:
                        sp.dma_start(wv[:], win[:, :, bass.ds(g * 2 * P + GV, 2 * P)]).then_inc(s["wv_in"], 16)

            @block.tensor
            def _(pe):
                pe.wait_ge(s["lr_in"], 80)
                for n, job in enumerate(GLA_JOBS):
                    if n >= 2:
                        pe.wait_ge(s["act_out"], after(ACT_GLA, GLA_JOBS[n - 2]))
                    if n < 2:
                        for off, m in PIECES:
                            last = pe.matmul(PS[:, 3 * n + off // 512, 0:m], wa2[:, n], lg[:, off:off + m], start=True, stop=True)
                    else:
                        pe.wait_ge(w_in[n % 2], 16 * (n // 2))
                        last = project(pe, PS, 3 * (n % 2), w[:, n % 2], G.hT)
                    last.then_inc(s["prod"], 1)
                pe.wait_ge(s["wv_in"], 16)
                for c in range(NCH):
                    if c >= 2:
                        pe.wait_ge(s["v_sb"], c - 1)
                    for k in range(KT):
                        last = pe.matmul(PS[:, 6 + c % 2, 0:2 * P], G.hT[:, k, c * CH:(c + 1) * CH], wv[:, k],
                                         start=(k == 0), stop=(k == KT - 1))
                    last.then_inc(s["v_ps"], 1)
                for d in range(2):
                    pe.wait_ge(s["dve_out"], after(DVE_GLA, f"kd{d}"))
                    if d == 0:
                        pe.wait_ge(s["act_out"], after(ACT_GLA, "g1"))
                    for j in range(3):
                        for c in range(4 * j, min(4 * j + 4, NCH)):
                            last = pe.transpose(PS[:, 3 * d + j, (c % 4) * P:(c % 4 + 1) * P], kd[:, d, c * CH:(c + 1) * CH], G.c("ident"))
                    last.then_inc(s["turned"], 1)

            @block.scalar
            def _(act):
                step = Steps(act, s["act_step"])
                out = Steps(act, s["act_out"])

                def job(name):
                    act.wait_ge(s["prod"], after(GLA_JOBS, name))
                    return flat(PS, 3 * (GLA_JOBS.index(name) % 2))

                act.wait_ge(s["lr_in"], 80)
                for d in range(2):
                    out.link(act.activation(x[:, d], job(f"x{d}"), ACT.Identity, bias=ba[:, d:d + 1]))
                    step.link(act.activation(l[:, d], x[:, d], ACT.Abs))
                    step.link(act.activation(l[:, d], l[:, d], ACT.Exp, scale=-1.0))
                    out.add(act.activation(l[:, d], l[:, d], ACT.Ln, bias=G.c("ones")[:, 0:1]))
                out.add(act.activation(B.q[:], job("q"), ACT.Copy, scale=0.125))
                out.add(act.activation(B.k[:], job("k"), ACT.Copy))
                for h in range(2):
                    out.add(act.activation(B.sG[:, h], job(f"g{h}"), ACT.Silu))
                for c in range(NCH):
                    act.wait_ge(s["v_ps"], c + 1)
                    act.activation(B.V[:, c], PS[:, 6 + c % 2, 0:2 * P], ACT.Copy).then_inc(s["v_sb"], 1)
                for d in range(2):
                    act.wait_ge(s["dve_out"], after(DVE_GLA, f"b{d}"))
                    out.add(act.activation(B.qd[:, d], B.b[:, d], ACT.Exp, scale=1.0 / 16))
                    act.activation(B.tot[:, d], B.b[:, d].rearrange("p (c t) -> p c t", t=CH)[:, :, (CH - 1) * (1 - d)],
                                   ACT.Exp, scale=1.0 / 16)
                    out.add(act.activation(kd[:, d], kd[:, d], ACT.Exp, scale=1.0 / 16))
                for d in range(2):
                    act.wait_ge(s["turned"], d + 1)
                    act.activation(B.KN[:, d].rearrange("p c n -> p (c n)"), flat(PS, 3 * d), ACT.Copy).then_inc(s["kn_sb"], 1)

            @block.vector
            def _(dve):
                step = Steps(dve, s["step"])
                out = Steps(dve, s["dve_out"])
                dve.memset(wa2[:], 0.0).then_inc(s["zeroed"], 1)
                for d in range(2):
                    dve.wait_ge(s["act_out"], after(ACT_GLA, f"l{d}"))
                    step.link(dve.scalar_tensor_tensor(x[:, d], x[:, d], 0.0, l[:, d], ALU.min, ALU.subtract))
                    c, v = (B.b[:, d], x[:, d]) if d == 0 else (B.b[:, d][:, ::-1], x[:, d][:, ::-1])
                    step.link(dve.tensor_tensor_scan(c, G.c("keep"), v, 0.0, ALU.mult, ALU.add))
                    b3 = B.b[:, d].rearrange("p (c t) -> p c t", t=CH)
                    end = (CH - 1) * (1 - d)
                    out.add(dve.tensor_tensor(kd[:, d].rearrange("p (c t) -> p c t", t=CH), b3[:, :, end:end + 1].broadcast_to([P, NCH, CH]), b3,
                                              ALU.subtract))
                for d in range(2):
                    dve.wait_ge(s["act_out"], after(ACT_GLA, f"ek{d}"))
                    dve.tensor_tensor(B.qd[:, d], B.qd[:, d], B.q[:], ALU.mult)
                    out.add(dve.tensor_tensor(kd[:, d], kd[:, d], B.k[:], ALU.mult))


def gla_scores(nc, A, G, B):
    with ExitStack() as ctx:
        def sb(n, s):
            return ctx.enter_context(nc.sbuf_tensor(n, s, F32))
        E = sb("lev_e", [P, 2, 2, T])
        QL, KL = sb("lev_q", [P, 2, 2, T]), sb("lev_k", [P, 2, 2, T])
        PS = G.PS
        groups = [(0, 4), (4, 4), (8, 2)]
        jobs = [(0, 0, h, j) for h in range(2) for j in range(3)] + \
            [(b, d, h, j) for b in LEVELS for d in range(2) for h in range(2) for j in range(3)]
        with phase(nc, "dist away expd q_ok k_ok scored merged") as (block, s):
            @block.tensor
            def _(pe):
                for n, (b, d, h, j) in enumerate(jobs):
                    lv = LEVELS.index(b) if b else -1
                    if n >= 8:
                        pe.wait_ge(s["merged"], n - 7)
                    if b:
                        pe.wait_ge(s["q_ok"], 2 * lv + d + 1)
                        pe.wait_ge(s["k_ok"], 2 * lv + d + 1)
                    q = slice(64 * h, 64 * h + 64)
                    for i in range(groups[j][1]):
                        c = groups[j][0] + i
                        t = slice(c * CH, c * CH + CH)
                        lhs, rhs = (KL[q, lv % 2, d, t], QL[q, lv % 2, d, t]) if b else (B.k[q, t], B.q[q, t])
                        last = pe.matmul(PS[:, n % 8, i * P:(i + 1) * P], lhs, rhs, start=True, stop=True)
                    last.then_inc(s["scored"], 1)

            def merge_jobs(dve, level):
                for n, (b, d, h, j) in enumerate(jobs):
                    if b != level:
                        continue
                    c0, m = groups[j]
                    dve.wait_ge(s["scored"], n + 1)
                    if n >= 6:
                        dve.wait_ge(s["merged"], n - 5)
                    out = B.A[:, c0:c0 + m, h, :]
                    ps = PS[:, n % 8, 0:m * P].rearrange("p (c t) -> p c t", t=P)
                    if not b:
                        ins = dve.scalar_tensor_tensor(out, ps, 2.0, G.c("ident")[:, None, :].broadcast_to([P, m, P]), ALU.mult, ALU.mult)
                    else:
                        lr = (b > 1) == (d == 0)
                        mask = G.c(f"level{b}")[:, 2 * P:3 * P] if lr else G.c(f"level{b}")[:, 0:P]
                        ins = dve.copy_predicated(out, mask.bitcast(I32)[:, None, :].broadcast_to([P, m, P]), ps)
                    ins.then_inc(s["merged"], 1)

            @block.vector
            def _(dve):
                for lv, b in enumerate(LEVELS):
                    for d in range(2):
                        if lv >= 2:
                            dve.wait_ge(s["scored"], jobs.index((LEVELS[lv - 2], d, 1, 2)) + 1)
                            dve.wait_ge(s["k_ok"], 2 * (lv - 2) + d + 1)
                        blocks = B.b[:, d].rearrange("p (n t) -> p n t", t=2 * b)
                        mid = b - 1 if d == 0 else b
                        dve.tensor_tensor(E[:, lv % 2, d].rearrange("p (n t) -> p n t", t=2 * b), blocks,
                                          blocks[:, :, mid:mid + 1].broadcast_to([P, T // (2 * b), 2 * b]), ALU.subtract).then_inc(s["dist"], 1)
                    if lv:
                        merge_jobs(dve, LEVELS[lv - 1])
                    else:
                        merge_jobs(dve, 0)
                    for d in range(2):
                        dve.wait_ge(s["expd"], 2 * lv + d + 1)
                        dve.tensor_tensor(QL[:, lv % 2, d], E[:, lv % 2, d], B.q[:], ALU.mult).then_inc(s["q_ok"], 1)
                merge_jobs(dve, LEVELS[-1])

            @block.scalar
            def _(act):
                for n in range(2 * len(LEVELS)):
                    lv, d = n // 2, n % 2
                    e = E[:, lv % 2, d]
                    act.wait_ge(s["dist"], n + 1)
                    act.activation(e, e, ACT.Abs).then_inc(s["away"], 1)
                    act.wait_ge(s["away"], n + 1)
                    act.activation(e, e, ACT.Exp, scale=-1.0 / 16).then_inc(s["expd"], 1)

            @block.gpsimd
            def _(pool):
                for n in range(2 * len(LEVELS)):
                    lv, d = n // 2, n % 2
                    pool.wait_ge(s["expd"], n + 1)
                    pool.tensor_tensor(KL[:, lv % 2, d], E[:, lv % 2, d], B.k[:], ALU.mult).then_inc(s["k_ok"], 1)


def gla_out(nc, A, G, B, g):
    with ExitStack() as ctx:
        def sb(n, s):
            return ctx.enter_context(nc.sbuf_tensor(n, s, F32))
        S = sb("S_gla", [P, 2, NCH, P])
        o, sq = sb("gla_o", [P, 2, T]), sb("gla_sq", [P, 2, T])
        eps = sb("eps_gla", [P, 1])
        PS = G.PS
        with phase(nc, "zero outer state0 state1 o_ps o_sb squared var_ps root step y_ok stored eps_ok") as (block, s):
            state = [s["state0"], s["state1"]]

            @block.tensor
            def _(pe):
                for n in range(NCH - 1):
                    for d in range(2):
                        if n:
                            pe.wait_ge(state[d], n)
                        c = ORDER[d][n]
                        for h in range(2):
                            q = slice(64 * h, 64 * h + 64)
                            last = pe.matmul(PS[q, 6 + d, 0:P], B.KN[:, d, c, q], B.V[:, c, h * P:(h + 1) * P], start=True, stop=True)
                        last.then_inc(s["outer"], 1)
                pe.wait_ge(s["zero"], 2)
                for d in range(2):
                    pe.wait_ge(state[d], NCH - 1)
                for h in range(2):
                    q = slice(64 * h, 64 * h + 64)
                    for c in range(NCH):
                        dst = PS[:, 3 * h + c // 4, (c % 4) * P:(c % 4 + 1) * P]
                        t = slice(c * CH, c * CH + CH)
                        pe.matmul(dst, B.V[:, c, h * P:(h + 1) * P], B.A[:, c, h], start=True, stop=False)
                        for d in range(2):
                            last = pe.matmul(dst, S[q, d, c], B.qd[q, d, t], start=False, stop=(d == 1))
                    last.then_inc(s["o_ps"], 1)
                for h in range(2):
                    pe.wait_ge(s["squared"], h + 1)
                    for off, m in PIECES:
                        last = pe.matmul(PS[:, 3 * h + off // 512, 0:m], G.c("ones"), sq[:, h, off:off + m], start=True, stop=True)
                    last.then_inc(s["var_ps"], 1)

            @block.scalar
            def _(act):
                for h in range(2):
                    act.wait_ge(s["o_sb"], h + 1)
                    act.activation(sq[:, h], o[:, h], ACT.Square).then_inc(s["squared"], 1)
                act.wait_ge(s["eps_ok"], 1)
                for h in range(2):
                    act.wait_ge(s["var_ps"], h + 1)
                    act.activation(sq[:, h], flat(PS, 3 * h), ACT.Sqrt, scale=1.0 / P, bias=eps[:]).then_inc(s["root"], 1)

            @block.vector
            def _(dve):
                step = Steps(dve, s["step"])
                dve.memset(eps[:], EPS_LN).then_inc(s["eps_ok"], 1)
                for d in range(2):
                    dve.memset(S[:, d, ORDER[d][0]], 0.0).then_inc(s["zero"], 1)
                dve.wait_ge(s["zero"], 2)
                for n in range(NCH - 1):
                    for d in range(2):
                        c, c1 = ORDER[d][n], ORDER[d][n + 1]
                        dve.wait_ge(s["outer"], 2 * n + d + 1)
                        if n:
                            dve.wait_ge(state[d], n)
                        dve.scalar_tensor_tensor(S[:, d, c1], S[:, d, c], B.tot[:, d, c:c + 1], PS[:, 6 + d, 0:P],
                                                 ALU.mult, ALU.add).then_inc(state[d], 1)
                for h in range(2):
                    dve.wait_ge(s["o_ps"], h + 1)
                    dve.tensor_copy(o[:, h], flat(PS, 3 * h)).then_inc(s["o_sb"], 1)
                for h in range(2):
                    dve.wait_ge(s["root"], h + 1)
                    step.link(dve.reciprocal(sq[:, h], sq[:, h]))
                    step.link(dve.scalar_tensor_tensor(o[:, h], o[:, h], G.vc[:, V_GNG:V_GNG + 1], sq[:, h], ALU.mult, ALU.mult))
                    dve.tensor_tensor(o[:, h], o[:, h], B.sG[:, h], ALU.mult).then_inc(s["y_ok"], 1)

            @block.sync
            def _(sp):
                for h in range(2):
                    sp.wait_ge(s["y_ok"], h + 1)
                    sp.dma_start(A.yT_d[bass.ds(g * 2 + h, 1)].rearrange("o p t -> p (o t)"), o[:, h]).then_inc(s["stored"], 16)
                sp.wait_ge(s["stored"], 32)


def out_phase(nc, A, G, layer, yT_d, w_out, n_k, tiles, x_of, xnew, store):
    with ExitStack() as ctx:
        def sb(n, s):
            return ctx.enter_context(nc.sbuf_tensor(f"{n}{layer}", s, F32))
        w = sb("w_out", [P, n_k, D])
        y = sb("y_in", [P, n_k, P * len(tiles)])
        x = sb("x_res", [P, 3, D])
        gate, ln = sb("gate_row", [P, 2, D]), sb("ln_row", [P, 2, D])
        r = sb("resid", [P, 2, D])
        st = sb("stats", [P, 2, 2, 6])
        mv, rstd = sb("mean_var", [P, 2, 2]), sb("rstd", [P, 2, 2])
        eps = sb("eps_ln", [P, 1])
        PS = G.PS
        n_gate = 2 if layer == 0 else 1
        ktiles = 4
        sems = "row_in k_in0 k_in1 k_in2 k_in3 x_in0 x_in1 x_in2 prod summed mean_ok root normed scaled added stored0 stored1 step eps_ok"
        ring = 2 if layer else len(tiles)
        with phase(nc, sems) as (block, s):
            stored = [s["stored0"], s["stored1"]]
            k_in = [s["k_in0"], s["k_in1"], s["k_in2"], s["k_in3"]]
            x_in = [s["x_in0"], s["x_in1"], s["x_in2"]]

            @block.sync
            def _(sp):
                wv = w_out.rearrange("(k p) n -> p k n", p=P)
                for i in range(n_k // ktiles):
                    q = slice(i * ktiles, (i + 1) * ktiles)
                    sp.dma_start(y[:, q], yT_d[q].rearrange("k p t -> p k t")).then_inc(k_in[i], 16)
                    sp.dma_start(w[:, q], wv[:, q]).then_inc(k_in[i], 16)
                sp.dma_start(gate[:, 0:n_gate], A.gates_d[2 * layer:2 * layer + n_gate].rearrange("g p n -> p g n")).then_inc(s["row_in"], 16)
                for i, v in enumerate(("ln_g", "ln_b")):
                    sp.dma_start(ln[:, i], A.p[v][layer:layer + 1, :].broadcast_to([P, D])).then_inc(s["row_in"], 16)
                for n in range(min(3, len(tiles))):
                    sp.dma_start(x[:, n], x_of(tiles[n])).then_inc(x_in[n], 16)
                for n, t in enumerate(tiles):
                    sp.wait_ge(s["added"], n + 1)
                    sp.dma_start(store(t), xnew[:, n % ring]).then_inc(stored[n % 2], 16)
                    if n + 3 < len(tiles):
                        sp.wait_ge(s["summed"], n + 1)
                        sp.dma_start(x[:, n % 3], x_of(tiles[n + 3])).then_inc(x_in[n % 3], 16)
                for i in range(2):
                    sp.wait_ge(stored[i], 16 * (len(tiles) // 2))

            @block.tensor
            def _(pe):
                for n in range(len(tiles)):
                    if n >= 4:
                        pe.wait_ge(s["summed"], n - 3)
                    for k in range(n_k):
                        if n == 0 and k % ktiles == 0:
                            pe.wait_ge(k_in[k // ktiles], 32)
                        for h in range(2):
                            last = pe.matmul(PS[:, 2 * (n % 4) + h, :], y[:, k, n * P:(n + 1) * P], w[:, k, 512 * h:512 * h + 512],
                                             start=(k == 0), stop=(k == n_k - 1))
                    last.then_inc(s["prod"], 1)

            @block.vector
            def _(dve):
                step = Steps(dve, s["step"])
                dve.memset(eps[:], EPS_LN).then_inc(s["eps_ok"], 1)
                dve.wait_ge(s["row_in"], 48)
                for n, t in enumerate(tiles):
                    i = n % 2
                    gt = gate[:, 1 if (layer == 0 and t < CTXCH) else 0]
                    dve.wait_ge(s["prod"], n + 1)
                    if n >= 2:
                        dve.wait_ge(s["normed"], n - 1)
                    step.link(dve.tensor_tensor(r[:, i], PS[:, 2 * (n % 4):2 * (n % 4) + 2, :].rearrange("p a b -> p (a b)"), gt, ALU.mult))
                    dve.wait_ge(x_in[n % 3], 16 * (n // 3 + 1))
                    step.publish(dve.scalar_tensor_tensor(r[:, i], x[:, n % 3], ALPHA, r[:, i], ALU.mult, ALU.add), s["summed"], n + 1)
                    for h in range(2):
                        step.add(dve.bn_stats(st[:, i, h], r[:, i, 512 * h:512 * h + 512]))
                    step.wait()
                    step.publish(dve.bn_aggr(mv[:, i], st[:, i].rearrange("p a b -> p (a b)")), s["mean_ok"], n + 1)
                    dve.wait_ge(s["root"], n + 1)
                    step.link(dve.reciprocal(rstd[:, i, 0:1], rstd[:, i, 0:1]))
                    step.link(dve.scalar_tensor_tensor(rstd[:, i, 1:2], mv[:, i, 0:1], -1.0, rstd[:, i, 0:1], ALU.mult, ALU.mult))
                    if n >= ring:
                        dve.wait_ge(stored[n % 2], 16 * (n // 2))
                    dve.tensor_scalar(xnew[:, n % ring], r[:, i], rstd[:, i, 0:1], rstd[:, i, 1:2], ALU.mult, ALU.add).then_inc(s["normed"], 1)

            @block.scalar
            def _(act):
                act.wait_ge(s["eps_ok"], 1)
                for n in range(len(tiles)):
                    act.wait_ge(s["mean_ok"], n + 1)
                    if n >= 2:
                        act.wait_ge(s["normed"], n - 1)
                    act.activation(rstd[:, n % 2, 0:1], mv[:, n % 2, 1:2], ACT.Sqrt, bias=eps[:]).then_inc(s["root"], 1)

            @block.gpsimd
            def _(pool):
                pool.wait_ge(s["row_in"], 48)
                for n in range(len(tiles)):
                    pool.wait_ge(s["normed"], n + 1)
                    pool.tensor_tensor(xnew[:, n % ring], xnew[:, n % ring], ln[:, 0], ALU.mult).then_inc(s["scaled"], 1)
                    pool.wait_ge(s["scaled"], n + 1)
                    pool.tensor_tensor(xnew[:, n % ring], xnew[:, n % ring], ln[:, 1], ALU.add).then_inc(s["added"], 1)


PADW = GRID_W + 2


def mlstm_inputs(nc, A, G, B):
    with ExitStack() as ctx:
        def sb(n, s):
            return ctx.enter_context(nc.sbuf_tensor(n, s, F32))
        w = sb("w_in1", [P, 2, KT, P])
        cols = sb("tile_cols", [P, TILE_PARAMS])
        wqkv = sb("wqkv", [P, 3, 4])
        wg = sb("w_gates", [P, 3, 4, 4])
        BD, BDT = sb("BD", [P, 3, P]), sb("BDT", [P, 3, P])
        WG = sb("WG", [P, 2, P])
        xm, xc = sb("xm", [P, T]), sb("xc", [P, T])
        padl, padc = sb("padl", [P, ROWS + 2, PADW]), sb("padc", [P, CTX + 2])
        acc = sb("conv_acc", [P, T])
        q, k = sb("q_out", [P, SEQ]), sb("k_out", [P, T])
        v = sb("v_out", [P, NCH, P])
        sz, sx = sb("sz_out", [P, SEQ]), sb("sx_out", [P, SEQ])
        PS = G.PS
        with phase(nc, "gates_zero") as (block, s):
            @block.vector
            def _(dve):
                dve.memset(B.gates[:], 0.0)
                dve.memset(padl[:].rearrange("p a b -> p (a b)"), 0.0)
                dve.memset(padc[:], 0.0)
                dve.memset(WG[:], 0.0).then_inc(s["gates_zero"], 1)
        with nc.Fori(0, NT1) as i:
            sems = ("cols_in wx_in wz_in small_in bd_ok bdt_ps bdt_sb fold_ps fold_sb xm_ps xm_sb padded "
                    "z_ps z_sb conv_ok xc_ok q_ps q_sb k_ps k_sb v_ps v_sb gate_ps gate_sb skip_sb step stored")
            with phase(nc, sems) as (block, s):
                @block.sync
                def _(sp):
                    win = A.p["o_w_in"][0].rearrange("(k p) n -> p k n", p=P)
                    sp.dma_start(cols[:], A.cols1_d[bass.ds(i, 1)].rearrange("o p j -> p (o j)")).then_inc(s["cols_in"], 16)
                    for j, n in enumerate(("ml_wq", "ml_wk", "ml_wv")):
                        sp.dma_start(wqkv[:, j], A.p[n][0].rearrange("j c d -> (j c) d")[bass.ds(i * P, P)]).then_inc(s["small_in"], 16)
                    for j, n in enumerate(("ml_wi_f", "ml_wf_f", "ml_wi_b", "ml_wf_b")):
                        src = A.p[n][0].rearrange("(a r) h -> r a h", a=3)
                        sp.dma_start(wg[:, :, j], src[bass.ds(i * P, P)]).then_inc(s["small_in"], 16)
                    sp.dma_start(w[:, 0], win[:, :, bass.ds(i * P, P)]).then_inc(s["wx_in"], 16)
                    sp.dma_start(w[:, 1], win[:, :, bass.ds(i * P + INNER, P)]).then_inc(s["wz_in"], 16)
                    sp.wait_ge(s["q_sb"], 1)
                    sp.dma_start(B.q_d[bass.ds(i, 1)].rearrange("o p t -> p (o t)"), q[:]).then_inc(s["stored"], 16)
                    sp.wait_ge(s["k_sb"], 1)
                    sp.dma_start(B.k_d[bass.ds(i, 1)].rearrange("o p t -> p (o t)"), k[:]).then_inc(s["stored"], 16)
                    sp.wait_ge(s["z_sb"], 1)
                    sp.dma_start(B.sz_d[bass.ds(i, 1)].rearrange("o p t -> p (o t)"), sz[:]).then_inc(s["stored"], 16)
                    sp.wait_ge(s["skip_sb"], 1)
                    sp.dma_start(B.sx_d[bass.ds(i, 1)].rearrange("o p t -> p (o t)"), sx[:]).then_inc(s["stored"], 16)
                    sp.wait_ge(s["v_sb"], 3)
                    sp.dma_start(B.v_d[bass.ds(i, 1)].rearrange("o p c n -> p (o c) n"), v[:]).then_inc(s["stored"], 16)
                    sp.wait_ge(s["stored"], 5 * 16)

                @block.tensor
                def _(pe):
                    pe.wait_ge(s["bd_ok"], 1)
                    for j in range(3):
                        last = pe.transpose(PS[:, 6, j * P:(j + 1) * P], BD[:, j], G.c("ident"))
                    last.then_inc(s["bdt_ps"], 1)
                    pe.wait_ge(s["wx_in"], 16)
                    project(pe, PS, 0, w[:, 0], G.hT).then_inc(s["xm_ps"], 1)
                    pe.wait_ge(s["bdt_sb"], 1)
                    g = [wg[:, j].rearrange("p a b -> p (a b)") for j in range(3)]
                    pe.matmul(PS[:, 7, 0:16], BDT[:, 0], g[0], start=True, stop=False)
                    pe.matmul(PS[:, 7, 0:16], BDT[:, 1], g[1], start=False, stop=True)
                    pe.matmul(PS[:, 7, 16:32], BDT[:, 2], g[2], start=True, stop=True).then_inc(s["fold_ps"], 1)
                    pe.wait_ge(s["wz_in"], 16)
                    project(pe, PS, 3, w[:, 1], G.hT, at=CTX).then_inc(s["z_ps"], 1)
                    pe.wait_ge(s["xm_sb"], 1)
                    pe.wait_ge(s["fold_sb"], 1)
                    for c in range(NCH):
                        last = pe.matmul(PS[:, 5 + c // 4, (c % 4) * P:(c % 4 + 1) * P], xm[:, c * CH:(c + 1) * CH], BD[:, 2],
                                         start=True, stop=True)
                        if c in (3, 7, 9):
                            last.then_inc(s["v_ps"], 1)
                    pe.wait_ge(s["xc_ok"], 1)
                    pe.wait_ge(s["padded"], 1)
                    for off, m in PIECES:
                        last = pe.matmul(PS[:, off // 512, 0:m], BD[:, 1], xc[:, off:off + m], start=True, stop=True)
                    last.then_inc(s["k_ps"], 1)
                    pe.wait_ge(s["z_sb"], 1)
                    for off in (0, 512):
                        last = pe.matmul(PS[:, 3 + off // 512, :], BD[:, 0], xc[:, CTX + off:CTX + off + 512], start=True, stop=True)
                    last.then_inc(s["q_ps"], 1)
                    pe.wait_ge(s["v_sb"], 3)
                    for off, m in PIECES:
                        pe.matmul(PS[:, 5 + off // 512, 0:m], WG[:, 0], xc[:, off:off + m], start=True, stop=False)
                        last = pe.matmul(PS[:, 5 + off // 512, 0:m], WG[:, 1], xm[:, off:off + m], start=False, stop=True)
                    last.then_inc(s["gate_ps"], 1)

                @block.scalar
                def _(act):
                    act.wait_ge(s["bdt_ps"], 1)
                    act.activation(BDT[:].rearrange("p a b -> p (a b)"), PS[:, 6, 0:3 * P], ACT.Copy).then_inc(s["bdt_sb"], 1)
                    act.wait_ge(s["xm_ps"], 1)
                    act.activation(padl[:, 1:ROWS + 1, 1:GRID_W + 1], flat(PS, 0)[:, CTX:].rearrange("p (r w) -> p r w", w=GRID_W), ACT.Copy)
                    act.activation(padc[:, 1:CTX + 1], flat(PS, 0)[:, 0:CTX], ACT.Copy).then_inc(s["padded"], 1)
                    act.activation(xm[:], flat(PS, 0), ACT.Copy).then_inc(s["xm_sb"], 1)
                    act.wait_ge(s["z_ps"], 1)
                    act.activation(sz[:], flat(PS, 3)[:, 0:SEQ], ACT.Silu).then_inc(s["z_sb"], 1)
                    for j in range(3):
                        m = 4 if j < 2 else 2
                        act.wait_ge(s["v_ps"], j + 1)
                        act.activation(v[:, 4 * j:4 * j + m].rearrange("p c n -> p (c n)"), PS[:, 5 + j, 0:m * P], ACT.Copy).then_inc(s["v_sb"], 1)
                    act.wait_ge(s["conv_ok"], 1)
                    act.activation(xc[:], acc[:], ACT.Silu).then_inc(s["xc_ok"], 1)
                    act.wait_ge(s["k_ps"], 1)
                    act.activation(k[:], flat(PS, 0), ACT.Copy, scale=float(DH) ** -0.5).then_inc(s["k_sb"], 1)
                    act.wait_ge(s["q_ps"], 1)
                    act.activation(q[:], flat(PS, 3)[:, 0:SEQ], ACT.Copy).then_inc(s["q_sb"], 1)

                @block.vector
                def _(dve):
                    step = Steps(dve, s["step"])
                    dve.wait_ge(s["small_in"], 7 * 16)
                    for j in range(3):
                        last = dve.tensor_tensor(BD[:, j].rearrange("p (a b) -> p a b", b=4), wqkv[:, j:j + 1, :].broadcast_to([P, 32, 4]),
                                                 G.c("block4").rearrange("p (a b) -> p a b", b=4), ALU.mult)
                    last.then_inc(s["bd_ok"], 1)
                    dve.wait_ge(s["fold_ps"], 1)
                    for j in range(2):
                        dst = WG[:, j].rearrange("p (a b) -> p a b", b=32)[:, :, 0:4]
                        last = dve.tensor_copy(dst, PS[:, 7, 16 * j:16 * j + 16].rearrange("p (a b) -> p a b", b=4))
                    last.then_inc(s["fold_sb"], 1)
                    dve.wait_ge(s["cols_in"], 16)
                    dve.wait_ge(s["padded"], 1)
                    lat = acc[:, CTX:].rearrange("p (r w) -> p r w", w=GRID_W)
                    step.add(dve.tensor_scalar(lat, padl[:, 0:ROWS, 0:GRID_W], cols[:, 0:1], cols[:, 9:10], ALU.mult, ALU.add))
                    step.link(dve.tensor_scalar(acc[:, 0:CTX], padc[:, 0:CTX], cols[:, 3:4], cols[:, 9:10], ALU.mult, ALU.add))
                    for t in range(1, 9):
                        a, b = t // 3, t % 3
                        if t in (4, 5):
                            step.add(dve.scalar_tensor_tensor(acc[:, 0:CTX], padc[:, b:b + CTX], cols[:, t:t + 1], acc[:, 0:CTX], ALU.mult, ALU.add))
                        ins = dve.scalar_tensor_tensor(lat, padl[:, a:a + ROWS, b:b + GRID_W], cols[:, t:t + 1], lat, ALU.mult, ALU.add)
                        if t == 8:
                            ins.then_inc(s["conv_ok"], 1)
                        else:
                            step.link(ins)
                    dve.wait_ge(s["xc_ok"], 1)
                    dve.tensor_scalar(sx[:], xc[:, CTX:], cols[:, 11:12], None, ALU.mult).then_inc(s["skip_sb"], 1)
                    dve.wait_ge(s["gate_ps"], 1)
                    dve.tensor_tensor(B.gates[:], flat(PS, 5), B.gates[:], ALU.add).then_inc(s["gate_sb"], 1)


def mlstm_gates(nc, A, G, B):
    with ExitStack() as ctx:
        def sb(n, s):
            return ctx.enter_context(nc.sbuf_tensor(n, s, F32))
        bias = sb("gate_bias", [P, 1])
        x, l = sb("gate_x", [P, T]), sb("gate_l", [P, T])
        F_, a, M, m = [sb(n, [P, T]) for n in ("gate_F", "gate_a", "gate_M", "gate_m")]
        unit = sb("unit", [P, T])
        colsb = sb("gate_cols", [P, 2, NCH, HEADS1, 2])
        PS = G.PS
        with phase(nc, "zero bias_in x_ok l_ok step rows_ok turned0 turned1 cols_ok stored act_step") as (block, s):
            @block.sync
            def _(sp):
                sp.wait_ge(s["zero"], 1)
                for j, n in enumerate(("ml_bi_f", "ml_bf_f", "ml_bi_b", "ml_bf_b")):
                    sp.dma_start(bias[32 * j:32 * j + 4], A.p[n][0].rearrange("(p o) -> p o", o=1)).then_inc(s["bias_in"], 16)
                sp.wait_ge(s["rows_ok"], 1)
                for d in range(2):
                    sp.dma_start(B.M_d[:, d], M[64 * d:64 * d + 4, CTX:]).then_inc(s["stored"], 16)
                sp.wait_ge(s["cols_ok"], 2)
                for h in range(HEADS1):
                    sp.dma_start(B.cols_d[h], colsb[:, :, :, h]).then_inc(s["stored"], 16)
                sp.wait_ge(s["stored"], 6 * 16)

            @block.scalar
            def _(act):
                step = Steps(act, s["act_step"])
                act.wait_ge(s["x_ok"], 1)
                step.link(act.activation(l[:], x[:], ACT.Abs))
                step.link(act.activation(l[:], l[:], ACT.Exp, scale=-1.0))
                act.activation(l[:], l[:], ACT.Ln, bias=G.c("ones")[:, 0:1]).then_inc(s["l_ok"], 1)

            @block.vector
            def _(dve):
                step = Steps(dve, s["step"])
                dve.memset(bias[:], 0.0).then_inc(s["zero"], 1)
                step.add(dve.memset(unit[:], 1.0))
                step.add(dve.memset(a[:], 0.0))
                step.add(dve.memset(M[:], 0.0))
                step.add(dve.memset(m[:], 0.0))
                step.link(dve.memset(F_[:], 0.0))
                dve.wait_ge(s["bias_in"], 64)
                step.publish(dve.tensor_scalar(x[:], B.gates[:], bias[:], None, ALU.add), s["x_ok"], 1)
                dve.wait_ge(s["l_ok"], 1)
                step.link(dve.scalar_tensor_tensor(l[:], x[:], 0.0, l[:], ALU.min, ALU.subtract))
                for d in range(2):
                    r, f = slice(64 * d, 64 * d + 4), slice(64 * d + 32, 64 * d + 36)

                    def scan(out, in0, in1, first, op0, op1):
                        for lo, hi, prev in ((0, CTX, None), (CTX, T, CTX - 1 if d == 0 else 0)):
                            ini = first if prev is None else out[:, prev:prev + 1]
                            v = [z[:, lo:hi] if d == 0 else z[:, lo:hi][:, ::-1] for z in (out, in0, in1)]
                            step.link(dve.tensor_tensor_scan(v[0], v[1], v[2], ini, op0, op1))

                    step.link(dve.tensor_copy(m[r], l[f]))
                    scan(F_[r], unit[r], m[r], 0.0, ALU.mult, ALU.add)
                    step.link(dve.tensor_tensor(a[r], x[r], F_[r], ALU.subtract))
                    scan(M[r], a[r], a[r], -3e38, ALU.max, ALU.max)
                    step.link(dve.scalar_tensor_tensor(m[r], F_[r], -1.0, M[r], ALU.mult, ALU.subtract))
                step.publish(dve.tensor_scalar(M[:], M[:], -1.0, None, ALU.mult), s["rows_ok"], 1)
                for j, t in enumerate((s["turned0"], s["turned1"])):
                    for n in range(3):
                        cnt = min(4, NCH - 4 * n)
                        dve.wait_ge(t, n + 1)
                        for d in range(2):
                            src = PS[:, 4 * j + n, 0:cnt * P].rearrange("p (c r) -> p c r", r=P)[:, :, 64 * d:64 * d + 4]
                            last = dve.tensor_copy(colsb[:, d, 4 * n:4 * n + cnt, :, j], src)
                    last.then_inc(s["cols_ok"], 1)

            @block.tensor
            def _(pe):
                pe.wait_ge(s["rows_ok"], 1)
                for j, (src, t) in enumerate(((a, s["turned0"]), (m, s["turned1"]))):
                    for n in range(3):
                        for c in range(4 * n, min(4 * n + 4, NCH)):
                            last = pe.transpose(PS[:, 4 * j + n, (c % 4) * P:(c % 4 + 1) * P], src[:, c * CH:(c + 1) * CH], G.c("ident"))
                        last.then_inc(t, 1)


TQ = SEQ // P
VCOL = [0, P, 2 * P + 1, 3 * P + 1]


def mlstm_heads(nc, A, G, B):
    def uses(d, c):
        return [j for j in range(NCH) if j < CTXCH or (j <= c if d == 0 else j >= c)]

    groups = [(0, 4), (4, 4), (8, 2)]
    with ExitStack() as ctx:
        def sb(n, s):
            return ctx.enter_context(nc.sbuf_tensor(n, s, F32))
        Q, K = sb("Q", [P, 4, SEQ]), sb("K1", [P, 4, T])
        V = sb("V1", [P, NCH, 4 * P + 1])
        cols, pcol = sb("head_cols", [P, 2, NCH, 2]), sb("head_params", [P, 4, TILE_PARAMS])
        Mrow = sb("M_row", [P, 2, SEQ])
        sx, sz = sb("sx_in", [P, 4, SEQ]), sb("sz_in", [P, 4, SEQ])
        W = sb("weights", [P, 2, 2, NCH, P])
        dg = sb("diag_arg", [P, 2, 2, P])
        H = sb("H", [P, TQ, DH])
        floor = sb("floor", [P, 2, NCH])
        den = sb("den", [P, 2, 2])
        st, mv, rs = sb("h_stats", [P, 2, 6]), sb("h_mv", [P, TQ, 2]), sb("h_rstd", [P, 2, TQ])
        eps = sb("eps_h", [P, 1])
        PS = G.PS
        with phase(nc, "ones_ok") as (block, s):
            @block.vector
            def _(dve):
                dve.memset(V[:, :, 2 * P:2 * P + 1], 1.0)
                dve.memset(eps[:], EPS_LN).then_inc(s["ones_ok"], 1)
        with nc.Fori(0, HEADS1) as h:
            sems = ("qk_in v_in row_in skip_in scored weighted d_ok diag_ok floor_ok av_ps av_sb mean_ok root normed "
                    "turned y_half y_ok step stored taken")
            with phase(nc, sems) as (block, s):
                @block.sync
                def _(sp):
                    sp.dma_start(Mrow[:].rearrange("p d t -> p (d t)"),
                                   B.M_d[bass.ds(h, 1)].rearrange("o d t -> o (d t)").broadcast_to([P, 2 * SEQ])).then_inc(s["row_in"], 16)
                    sp.dma_start(cols[:], B.cols_d[bass.ds(h, 1)].rearrange("o p d c j -> p (o d) c j")).then_inc(s["row_in"], 16)
                    for kt in range(4):
                        sp.dma_start(K[:, kt], B.k_d[bass.ds(h * 4 + kt, 1)].rearrange("o p t -> p (o t)")).then_inc(s["qk_in"], 16)
                        sp.dma_start(Q[:, kt], B.q_d[bass.ds(h * 4 + kt, 1)].rearrange("o p t -> p (o t)")).then_inc(s["qk_in"], 16)
                    for kt in range(4):
                        sp.dma_start(V[:, :, VCOL[kt]:VCOL[kt] + P], B.v_d[bass.ds(h * 4 + kt, 1)].rearrange("o p c n -> p (o c) n")).then_inc(s["v_in"], 16)
                    sp.dma_start(sx[:], B.sx_d[bass.ds(h * 4, 4)].rearrange("k p t -> p k t")).then_inc(s["skip_in"], 16)
                    sp.dma_start(sz[:], B.sz_d[bass.ds(h * 4, 4)].rearrange("k p t -> p k t")).then_inc(s["skip_in"], 16)
                    sp.dma_start(pcol[:], A.cols1_d[bass.ds(h * 4, 4)].rearrange("k p j -> p k j")).then_inc(s["skip_in"], 16)
                    for kt in range(4):
                        sp.wait_ge(s["y_ok"], kt + 1)
                        sp.dma_start(B.y_d[bass.ds(h * 4 + kt, 1)].rearrange("o p t -> p (o t)"), sx[:, kt]).then_inc(s["stored"], 16)
                    sp.wait_ge(s["stored"], 64)

                @block.tensor
                def _(pe):
                    def scores(i):
                        for g, (j0, m) in enumerate(groups):
                            n = 3 * i + g
                            if n >= 4:
                                pe.wait_ge(s["weighted"], n - 3)
                            for j in range(j0, j0 + m):
                                for kt in range(4):
                                    last = pe.matmul(PS[:, 4 + n % 4, (j - j0) * P:(j - j0 + 1) * P], K[:, kt, j * P:(j + 1) * P],
                                                     Q[:, kt, i * P:(i + 1) * P], start=(kt == 0), stop=(kt == 3))
                            last.then_inc(s["scored"], 1)

                    pe.wait_ge(s["qk_in"], 128)
                    scores(0)
                    pe.wait_ge(s["v_in"], 64)
                    for i in range(TQ):
                        if i + 1 < TQ:
                            scores(i + 1)
                        pe.wait_ge(s["weighted"], 3 * i + 3)
                        if i:
                            pe.wait_ge(s["av_sb"], i)
                        for d in range(2):
                            seen = uses(d, i + CTXCH)
                            for j in seen:
                                for half in range(2):
                                    v = V[:, j, 0:2 * P + 1] if half == 0 else V[:, j, 2 * P + 1:4 * P + 1]
                                    last = pe.matmul(PS[:, 2 * d + half, 0:v.shape[1]], W[:, i % 2, d, j], v,
                                                     start=(j == seen[0]), stop=(j == seen[-1]))
                        last.then_inc(s["av_ps"], 1)
                    for kt in range(4):
                        pe.wait_ge(s["normed"], TQ)
                        if kt >= 2:
                            pe.wait_ge(s["y_half"], kt - 1)
                        for i in range(TQ):
                            last = pe.transpose(PS[:, 4 + 2 * (kt % 2) + i // 4, (i % 4) * P:(i % 4 + 1) * P], H[:, i, kt * P:(kt + 1) * P], G.c("ident"))
                        last.then_inc(s["turned"], 1)

                @block.scalar
                def _(act):
                    act.wait_ge(s["row_in"], 32)
                    act.activation(floor[:], cols[:, :, :, 1], ACT.Exp).then_inc(s["floor_ok"], 1)
                    for i in range(TQ):
                        c = i + CTXCH
                        if i >= 2:
                            act.wait_ge(s["av_ps"], i - 1)
                        act.wait_ge(s["diag_ok"], 2 * i + 2)
                        for d in range(2):
                            for j in uses(d, c):
                                arg = dg[:, i % 2, d] if j == c else Mrow[:, d, i * P:(i + 1) * P]
                                last = act.activation(W[:, i % 2, d, j], arg, ACT.Exp, bias=cols[:, d, j, 0:1])
                        last.then_inc(s["d_ok"], 1)
                    act.wait_ge(s["mean_ok"], TQ)
                    act.activation(rs[:, 0], mv[:, :, 1], ACT.Sqrt, bias=eps[:]).then_inc(s["root"], 1)

                @block.vector
                def _(dve):
                    step = Steps(dve, s["step"])

                    def diag(i):
                        if i >= 2:
                            dve.wait_ge(s["d_ok"], i - 1)
                        for d in range(2):
                            dve.tensor_tensor(dg[:, i % 2, d], G.c("neg")[:, d * P:(d + 1) * P], Mrow[:, d, i * P:(i + 1) * P],
                                              ALU.add).then_inc(s["diag_ok"], 1)

                    dve.wait_ge(s["row_in"], 32)
                    dve.wait_ge(s["floor_ok"], 1)
                    diag(0)
                    for i in range(TQ):
                        c = i + CTXCH
                        if i + 1 < TQ:
                            diag(i + 1)
                        dve.wait_ge(s["d_ok"], i + 1)
                        for g, (j0, m) in enumerate(groups):
                            n = 3 * i + g
                            dve.wait_ge(s["scored"], n + 1)
                            for d in range(2):
                                js = [j for j in uses(d, c) if j0 <= j < j0 + m]
                                runs = []
                                for j in js:
                                    if runs and runs[-1][1] == j:
                                        runs[-1][1] = j + 1
                                    else:
                                        runs.append([j, j + 1])
                                for a, b in runs:
                                    w = W[:, i % 2, d, a:b]
                                    last = dve.tensor_tensor(w, PS[:, 4 + n % 4, (a - j0) * P:(b - j0) * P].rearrange("p (j t) -> p j t", t=P), w, ALU.mult)
                            last.then_inc(s["weighted"], 1)
                        dve.wait_ge(s["av_ps"], i + 1)
                        for d in range(2):
                            step.add(dve.scalar_tensor_tensor(den[:, d, 0:1], PS[:, 2 * d, 2 * P:2 * P + 1], -1.0, floor[:, d, c:c + 1],
                                                              ALU.mult, ALU.max))
                        step.wait()
                        for d in range(2):
                            step.add(dve.tensor_tensor(den[:, d, 0:1], PS[:, 2 * d, 2 * P:2 * P + 1], den[:, d, 0:1], ALU.max))
                        step.wait()
                        for d in range(2):
                            step.add(dve.reciprocal(den[:, d, 1:2], den[:, d, 0:1]))
                        step.wait()
                        for half in range(2):
                            step.add(dve.tensor_scalar(H[:, i, 2 * P * half:2 * P * half + 2 * P], PS[:, half, 0:2 * P], den[:, 0, 1:2], None, ALU.mult))
                        step.wait()
                        for half in range(2):
                            hh = H[:, i, 2 * P * half:2 * P * half + 2 * P]
                            ins = dve.scalar_tensor_tensor(hh, PS[:, 2 + half, 0:2 * P], den[:, 1, 1:2], hh, ALU.mult, ALU.add)
                            if half:
                                step.publish(ins, s["av_sb"], i + 1)
                            else:
                                step.add(ins)
                        step.link(dve.bn_stats(st[:, i % 2], H[:, i]))
                        dve.bn_aggr(mv[:, i], st[:, i % 2]).then_inc(s["mean_ok"], 1)
                    dve.wait_ge(s["root"], 1)
                    step.link(dve.reciprocal(rs[:, 0], rs[:, 0]))
                    step.link(dve.scalar_tensor_tensor(rs[:, 1], mv[:, :, 0], -1.0, rs[:, 0], ALU.mult, ALU.mult))
                    for i in range(TQ):
                        dve.tensor_scalar(H[:, i], H[:, i], rs[:, 0, i:i + 1], rs[:, 1, i:i + 1], ALU.mult, ALU.add).then_inc(s["normed"], 1)
                    dve.wait_ge(s["skip_in"], 48)
                    for kt in range(4):
                        dve.wait_ge(s["turned"], kt + 1)
                        b = 4 + 2 * (kt % 2)
                        step.publish(dve.scalar_tensor_tensor(sx[:, kt], PS[:, b:b + 2, :].rearrange("p a b -> p (a b)"), pcol[:, kt, 10:11], sx[:, kt],
                                                              ALU.mult, ALU.add), s["y_half"], kt + 1)
                        dve.tensor_tensor(sx[:, kt], sx[:, kt], sz[:, kt], ALU.mult).then_inc(s["y_ok"], 1)


def build(nc, inputs, out):
    A = Names()
    A.p = inputs
    A.x, A.ctx, A.mod_w, A.consts = inputs["x"], inputs["ctx"], inputs["mod_w"], inputs["consts"]

    def scratch(name, shape):
        return nc.dram_tensor(name, shape, F32, kind="Internal").ap()

    A.gates_d = scratch("gates_d", (3, P, D))
    A.cols0_d = scratch("cols0_d", (4, P, NPAIR))
    A.cols1_d = scratch("cols1_d", (NT1, P, TILE_PARAMS))
    A.lg_d = scratch("lg_d", (32, T))
    A.yT_d = scratch("yT_d", (KT, P, T))
    A.x1_d = scratch("x1_d", (NCH, P, D))
    at, n_const = const_layout()
    with ExitStack() as ctx:
        def sb(n, s):
            return ctx.enter_context(nc.sbuf_tensor(n, s, F32))
        G = Names()
        G.PS = ctx.enter_context(nc.psum_tensor("PS", [P, 8, 512], F32))
        G.cst = sb("cst", [P, n_const])
        G.c = lambda name: G.cst[:, at[name][0]:at[name][1]]
        G.vc = sb("vc", [P, P])
        G.modc = sb("modc", [P, 2, 16, 2])
        setup_phase(nc, A, G)
        B = Names()
        with nc.sbuf_tensor("hT", [P, KT, T], F32) as hT:
            G.hT = hT
            with nc.sbuf_tensor("xnat", [P, NCH, D], F32) as xnat:
                modulate_phase(nc, A, G, 0, xnat, hT, True)
            layer0(nc, A, G)
        with nc.sbuf_tensor("xnew", [P, NCH, D], F32) as xnew:
            def x_of(t):
                return (A.ctx if t < CTXCH else A.x)[0, (t % CTXCH if t < CTXCH else t - CTXCH) * P:][:P]
            out_phase(nc, A, G, 0, A.yT_d, A.p["e_w_out"][0], KT, list(range(NCH)), x_of, xnew, lambda t: A.x1_d[t])
            with nc.sbuf_tensor("hT1", [P, KT, T], F32) as hT:
                G.hT = hT
                modulate_phase(nc, A, G, 1, xnew, hT, False)
                layer1_inputs(nc, A, G, B, scratch)
        mlstm_heads(nc, A, G, B)
        with nc.sbuf_tensor("xlast", [P, 2, D], F32) as xlast:
            out_phase(nc, A, G, 1, B.y_d, A.p["o_w_out"][0], NT1, list(range(CTXCH, NCH)), lambda t: A.x1_d[t], xlast,
                      lambda t: out[0, (t - CTXCH) * P:(t - CTXCH + 1) * P, :])


def layer1_inputs(nc, A, G, B, scratch):
    B.q_d, B.k_d = scratch("q_d", (NT1, P, SEQ)), scratch("k_d", (NT1, P, T))
    B.v_d = scratch("v_d", (NT1, P, NCH, P))
    B.sz_d, B.sx_d = scratch("sz_d", (NT1, P, SEQ)), scratch("sx_d", (NT1, P, SEQ))
    B.y_d = scratch("y1_d", (NT1, P, SEQ))
    B.M_d, B.cols_d = scratch("M_d", (HEADS1, 2, SEQ)), scratch("hcols_d", (HEADS1, P, 2, NCH, 2))
    with nc.sbuf_tensor("gates1", [P, T], F32) as gates:
        B.gates = gates
        mlstm_inputs(nc, A, G, B)
        mlstm_gates(nc, A, G, B)


def layer0(nc, A, G):
    with ExitStack() as c2:
        def sb2(n, s):
            return c2.enter_context(nc.sbuf_tensor(n, s, F32))
        B = Names()
        B.LW, B.LA = sb2("LW", [P, T]), sb2("LA", [P, T])
        lowrank_phase(nc, A, G, B.LW, B.LA)
        with ExitStack() as c3:
            def sb3(n, s):
                return c3.enter_context(nc.sbuf_tensor(n, s, F32))
            B.cols = sb3("pair_cols", [P, NPAIR])
            B.rt, B.at, B.bt, B.kt = (sb3(n, [P, 2, T]) for n in ("rt", "at", "bt", "kt"))
            B.V, B.sG, B.bonus = (sb3(n, [P, T]) for n in ("V", "sG", "bonus"))
            B.PL = sb3("PL", [P, 2, NCH])
            with nc.Fori(0, 4) as p:
                rwkv_prep(nc, A, G, B, p)
                with ExitStack() as c4:
                    def sb4(n, s):
                        return c4.enter_context(nc.sbuf_tensor(n, s, F32))
                    B.QT = sb4("QT", [P, NCH, 2, P])
                    B.GT, B.HS = sb4("GT", [P, NCH, 2, 64]), sb4("HS", [P, NCH, 2, 64])
                    B.Y = sb4("Y_rwkv", [P, T])
                    rwkv_chunks(nc, A, G, B)
                    rwkv_finish(nc, A, G, B, p)
    with ExitStack() as c2:
        def sb2(n, s):
            return c2.enter_context(nc.sbuf_tensor(n, s, F32))
        B = Names()
        B.q, B.k = sb2("gla_q", [P, T]), sb2("gla_k", [P, T])
        B.b, B.qd, B.sG = sb2("gla_b", [P, 2, T]), sb2("gla_qd", [P, 2, T]), sb2("gla_sG", [P, 2, T])
        B.V = sb2("gla_V", [P, NCH, 2 * P])
        B.KN, B.A = sb2("gla_KN", [P, 2, NCH, P]), sb2("gla_A", [P, NCH, 2, P])
        B.tot = sb2("gla_tot", [P, 2, NCH])
        with nc.Fori(0, 2) as g:
            gla_prep(nc, A, G, B, g)
            gla_scores(nc, A, G, B)
            gla_out(nc, A, G, B, g)


_INS = ['x', 'c', 'ctx', 'c_ctx', 'mod_w', 'mod_b', 'ln_g', 'ln_b', 'e_w_in', 'e_w_out', 'gla_wa2_f',
        'gla_ba_f', 'gla_wa2_b', 'gla_ba_b', 'gla_norm_g', 'rwkv_mu', 'rwkv_w0_f', 'rwkv_ww2_f',
        'rwkv_w0_b', 'rwkv_ww2_b', 'rwkv_a0_f', 'rwkv_wa2_f', 'rwkv_a0_b', 'rwkv_wa2_b', 'rwkv_k_k',
        'rwkv_k_a', 'rwkv_r_k', 'rwkv_gn_g', 'rwkv_gn_b', 'o_w_in', 'o_w_out', 'ml_conv_w', 'ml_conv_b',
        'ml_wq', 'ml_wk', 'ml_wv', 'ml_wi_f', 'ml_bi_f', 'ml_wf_f', 'ml_bf_f', 'ml_wi_b', 'ml_bi_b',
        'ml_wf_b', 'ml_bf_b', 'ml_norm_g', 'ml_skip']


def kernel(**inputs):
    import concourse.bacc as bacc
    from concourse.bass_utils import run_bass_kernel_spmd

    nc = bacc.Bacc("TRN2", target_bir_lowering=False, num_devices=1)
    arrays, args = {}, {}
    for name in _INS + ["consts"]:
        a = np.concatenate(list(constants().values()), 1) if name == "consts" else inputs[name]
        a = np.ascontiguousarray(a)
        arrays[f"in_{name}_dram"] = a
        args[name] = nc.dram_tensor(f"in_{name}_dram", a.shape, mybir.dt.from_np(a.dtype), kind="ExternalInput").ap()
    out = nc.dram_tensor("out_0_dram", (1, SEQ, D), F32, kind="ExternalOutput").ap()
    build(nc, args, out)
    r = run_bass_kernel_spmd(nc, [arrays], core_ids=[0])
    return r.results[0]["out_0_dram"]
```

```python
from contextlib import ExitStack, contextmanager

import numpy as np
import concourse.bass as bass
from concourse import mybir

F32 = mybir.dt.float32
F32R = mybir.dt.float32r
I32 = mybir.dt.int32
ALU = mybir.AluOpType
ACT = mybir.ActivationFunctionType

P = 128
D = 1024
CTX = 256
SEQ = 1024
T = CTX + SEQ
KT = D // P
GRID_W = 64
ROWS = SEQ // GRID_W
CH = 128
NCH = T // CH
CTXCH = CTX // CH
PIECES = [(0, 512), (512, 512), (1024, 256)]
EPS_LN = 1e-5
EPS_GN = 64e-5
DEC = 0.6065306597
HALF = DEC * CH / 2
ALPHA = 4.0 ** 0.25
BIG = 1e30
GQ, GK, GV, GG, GLR = 0, 256, 512, 1024, 1536
RR, RK, RV, RG, RWL, RAL = 1568, 2080, 2592, 3104, 3616, 3744
E_IN = 3872
INNER = 2048
NT1 = INNER // P
HEADS1 = 4
DH = 512
ORDER = [list(range(NCH)), list(range(CTXCH - 1, -1, -1)) + list(range(NCH - 1, CTXCH - 1, -1))]

LEVELS = [1, 2, 4, 8, 16, 32, 64]


def constants():
    p = np.arange(P)[:, None]
    f = np.arange(P)[None, :]
    one = np.float32

    def lr(b):
        return ((p // (2 * b) == f // (2 * b)) & (p % (2 * b) < b) & (f % (2 * b) >= b)).astype(one)

    c = {"ident": np.eye(P, dtype=one), "ones": np.ones((P, P), one)}
    c["side"] = ((p % 4) == np.arange(4)[None]).astype(one)
    c["neg"] = np.concatenate([np.where(f >= p, 0, -BIG), np.where(f <= p, 0, -BIG)], 1).astype(one)
    c["pick"] = np.concatenate([np.broadcast_to(p == 0, (P, P)), np.broadcast_to(p == 1, (P, P))], 1).astype(one)
    c["block4"] = ((p // 4) == (f // 4)).astype(one)
    for b in LEVELS:
        c[f"parted{b}"] = lr(b) + lr(b).T
    c["keep"] = np.broadcast_to((np.arange(T) % CH != 0).astype(one), (P, T))
    c["ident4"] = np.tile(c["ident"], (1, 4))
    for b in LEVELS:
        m = [lr(b).T, lr(b).T, lr(b), lr(b)]
        c[f"level{b}"] = np.concatenate(m if b > 1 else m[::-1], 1)
    c["score"] = np.concatenate([(f > p), (f >= p), (f < p), (f <= p)], 1).astype(one)
    c["heads"] = ((p // 64) == (f // 64)).astype(one)
    c["eye64"] = ((p % 64) == np.arange(64)[None]).astype(one)
    return c


def const_layout():
    at, n = {}, 0
    for k, v in constants().items():
        at[k] = (n, n + v.shape[1])
        n += v.shape[1]
    return at, [at["parted1"][0], at["ident4"][0], n]


class Names:
    pass


@contextmanager
def phase(nc, names):
    with ExitStack() as ctx:
        handles = [ctx.enter_context(nc.semaphore(n)) for n in names.split()]
        with nc.Block() as block:
            yield block, dict(zip(names.split(), handles))
        for h in handles:
            nc.sync.sem_clear(h)
        nc.all_engine_barrier(sem_only=True)


class Steps:

    def __init__(self, eng, sem):
        self.eng, self.sem, self.n = eng, sem, 0

    def add(self, ins):
        ins.then_inc(self.sem, 1)
        self.n += 1
        return ins

    def wait(self):
        self.eng.wait_ge(self.sem, self.n)

    def publish(self, ins, sem, value):
        ins.then_inc(sem, 1)
        self.eng.wait_ge(sem, value)

    def link(self, ins):
        self.add(ins)
        self.wait()


def after(names, name):
    return names.index(name) + 1


PAIR_PARAMS = [("rwkv_mu", 0), ("rwkv_mu", 512), ("rwkv_mu", 1024), ("rwkv_mu", 1536), ("rwkv_w0_f", 0),
               ("rwkv_w0_b", 0), ("rwkv_a0_f", 0), ("rwkv_a0_b", 0), ("rwkv_k_k", 0), ("rwkv_k_a", 0),
               ("rwkv_r_k", 0), ("rwkv_gn_g", 0), ("rwkv_gn_b", 0)]
NPAIR = len(PAIR_PARAMS)
(J_MU, J_W0, J_A0, J_KK, J_KA, J_RK, J_GG, J_GB) = (0, 4, 6, 8, 9, 10, 11, 12)
V_MULR = 4 * NPAIR
V_GBA = V_MULR + 2
V_GNG = V_GBA + 4
V_C = V_GNG + 1
V_END = V_C + 16
TILE_PARAMS = 12


def setup_phase(nc, A, G):
    with ExitStack() as ctx:
        def sb(n, s):
            return ctx.enter_context(nc.sbuf_tensor(n, s, F32))
        rows = sb("param_rows", [P, 3, P])
        modw = sb("modw", [P, 4, 3 * D])
        modb = sb("modb", [2, 2, 3 * D])
        modrow = sb("modrow", [2, 2, 3 * D])
        cond = sb("cond", [P, 2, KT])
        gate = sb("gate", [P, 3, D])
        cols1 = sb("cols1", [P, 2, P])
        PS = G.PS
        sems = "consts rows_in modb_in w0 w1 w2 w3 cols cols_sb cond_sb mod_ps mod_row vec_ps vec_sb gate_ps gate_sb step stored"
        with phase(nc, sems) as (block, s):
            ring = [s["w0"], s["w1"], s["w2"], s["w3"]]

            @block.sync
            def _(sp):
                sp.dma_start(G.cst[:], A.consts[:, 0:G.ends[0]]).then_inc(s["consts"], 16)
                for l in range(2):
                    for k in range(KT):
                        n = l * KT + k
                        if n >= 4:
                            sp.wait_ge(s["mod_ps"], n - 3)
                        sp.dma_start(modw[:, n % 4], A.mod_w[l, k * P:(k + 1) * P, :]).then_inc(ring[n % 4], 16)
                sp.wait_ge(s["gate_sb"], 6)
                sp.dma_start(A.gates_d.rearrange("g p n -> p g n"), gate[:]).then_inc(s["stored"], 16)
                sp.wait_ge(s["cols_sb"], 3)
                for h in range(2):
                    sp.dma_start(A.cols1_d[8 * h:8 * h + 8].rearrange("i p j -> p i j"),
                                 cols1[:, h, 0:8 * TILE_PARAMS].rearrange("p (i j) -> p i j", i=8)).then_inc(s["stored"], 16)
                sp.dma_start(A.cols0_d.rearrange("i p j -> p i j"),
                             G.vc[:, 0:V_MULR].rearrange("p (i j) -> p i j", i=4)).then_inc(s["stored"], 16)
                sp.wait_ge(s["stored"], 4 * 16)

            @block.scalar
            def _(act):
                n = 0
                for j, (name, at) in enumerate(PAIR_PARAMS):
                    act.dma_start(rows[j:j + 3 * NPAIR + 1:NPAIR, 0, :],
                                  A.p[name][0, at:at + 512].rearrange("(i n) -> i n", n=P)).then_inc(s["rows_in"], 16)
                act.dma_start(rows[V_MULR:V_MULR + 2, 0, :],
                              A.p["rwkv_mu"][0, 2048:2304].rearrange("(i n) -> i n", n=P)).then_inc(s["rows_in"], 16)
                for d, name in enumerate(("gla_ba_f", "gla_ba_b")):
                    act.dma_start(rows[V_GBA + 2 * d:V_GBA + 2 * d + 2, 0, :],
                                  A.p[name][0].rearrange("(i n) -> i n", n=P)).then_inc(s["rows_in"], 16)
                act.dma_start(rows[V_GNG:V_GNG + 1, 0, :], A.p["gla_norm_g"]).then_inc(s["rows_in"], 16)
                act.dma_start(rows[V_C:V_C + 8, 0, :], A.p["c"][0].rearrange("(i n) -> i n", n=P)).then_inc(s["rows_in"], 16)
                act.dma_start(rows[V_C + 8:V_END, 0, :], A.p["c_ctx"].rearrange("(i n) -> i n", n=P)).then_inc(s["rows_in"], 16)
                one = [A.p["ml_conv_w"][0, t // 3, t % 3, 0] for t in range(9)] + \
                    [A.p[n][0] for n in ("ml_conv_b", "ml_norm_g", "ml_skip")]
                for j, v in enumerate(one):
                    v = v.rearrange("(h i n) -> h i n", h=2, n=P)
                    for h in range(2):
                        act.dma_start(rows[j:j + 7 * TILE_PARAMS + 1:TILE_PARAMS, 1 + h, :], v[h]).then_inc(s["rows_in"], 16)
                for i in range(2):
                    act.dma_start(modb[i:i + 1], A.p["mod_b"].rearrange("(o l) n -> o l n", o=1)).then_inc(s["modb_in"], 16)
                act.wait_ge(s["cols_sb"], 1)
                act.activation(cond[:], G.vc[:, V_C:V_END].rearrange("p (w k) -> p w k", w=2), ACT.Silu).then_inc(s["cond_sb"], 1)

            n_rows = NPAIR + 1 + 2 + 1 + 2 + 2 * TILE_PARAMS

            @block.tensor
            def _(pe):
                pe.wait_ge(s["consts"], 16)
                pe.wait_ge(s["rows_in"], 16 * n_rows)
                pe.transpose(PS[:, 7, 0:V_END], rows[0:V_END, 0, :], G.c("ident")[0:V_END, 0:V_END])
                m = 8 * TILE_PARAMS
                for h in range(2):
                    last = pe.transpose(PS[:, 7, P * (h + 1):P * (h + 1) + m], rows[0:m, 1 + h, :], G.c("ident")[0:m, 0:m])
                last.then_inc(s["cols"], 1)
                pe.wait_ge(s["cond_sb"], 1)
                for l in range(2):
                    for k in range(KT):
                        n = l * KT + k
                        pe.wait_ge(ring[n % 4], 16 * (n // 4 + 1))
                        if k == 0 and l:
                            pe.wait_ge(s["mod_row"], 1)
                        for j in range(6):
                            last = pe.matmul(PS[0:2, j, :], cond[:, :, k], modw[:, n % 4, 512 * j:512 * j + 512],
                                             start=(k == 0), stop=(k == KT - 1))
                        last.then_inc(s["mod_ps"], 1)
                    pe.wait_ge(s["mod_row"], 2 * l + 2)
                    if l:
                        pe.wait_ge(s["vec_sb"], l)
                    for t in range(16):
                        last = pe.transpose(PS[:, 7, 2 * t:2 * t + 2], modrow[:, l, t * P:(t + 1) * P], G.c("ident")[0:2, 0:2])
                    last.then_inc(s["vec_ps"], 1)
                    for w in range(2 - l):
                        for h in range(2):
                            n = 4 * l + 2 * w + h
                            if n:
                                pe.wait_ge(s["gate_sb"], n)
                            pe.matmul(PS[:, 6, :], G.c("pick")[0:2, w * P:(w + 1) * P],
                                      modrow[:, l, 2 * D + 512 * h:2 * D + 512 * h + 512],
                                      start=True, stop=True).then_inc(s["gate_ps"], 1)

            @block.vector
            def _(dve):
                dve.wait_ge(s["cols"], 1)
                dve.tensor_copy(G.vc[:, 0:V_END], PS[:, 7, 0:V_END]).then_inc(s["cols_sb"], 1)
                m = 8 * TILE_PARAMS
                for h in range(2):
                    dve.tensor_copy(cols1[:, h, 0:m], PS[:, 7, P * (h + 1):P * (h + 1) + m]).then_inc(s["cols_sb"], 1)
                dve.wait_ge(s["modb_in"], 32)
                for l in range(2):
                    dve.wait_ge(s["mod_ps"], KT * (l + 1))
                    dve.tensor_tensor(modrow[:, l, :], PS[0:2, 0:6, :].rearrange("p a b -> p (a b)"), modb[:, l, :],
                                      ALU.add).then_inc(s["mod_row"], 1)
                    dve.wait_ge(s["mod_row"], 2 * l + 1)
                    dve.tensor_scalar(modrow[:, l, D:2 * D], modrow[:, l, D:2 * D], 1.0, None, ALU.add).then_inc(s["mod_row"], 1)
                    dve.wait_ge(s["vec_ps"], l + 1)
                    dve.tensor_copy(G.modc[:, l], PS[:, 7, 0:32].rearrange("p (t w) -> p t w", w=2)).then_inc(s["vec_sb"], 1)
                    for w in range(2 - l):
                        for h in range(2):
                            dve.wait_ge(s["gate_ps"], 4 * l + 2 * w + h + 1)
                            dve.tensor_copy(gate[:, 2 * l + w, 512 * h:512 * h + 512], PS[:, 6, :]).then_inc(s["gate_sb"], 1)


def modulate_phase(nc, A, G, layer, xnat, hT, load):
    PS = G.PS
    jobs = [(k, at, w) for k in range(KT) for at, w in ((0, CTX), (CTX, 512), (CTX + 512, 512))]
    with phase(nc, "x_in turned taken") as (block, s):
        @block.sync
        def _(sp):
            if load:
                sp.dma_start(xnat[:, 0:CTXCH, :], A.ctx[0].rearrange("(c p) d -> p c d", p=P)).then_inc(s["x_in"], 16)
                sp.dma_start(xnat[:, CTXCH:NCH, :], A.x[0].rearrange("(c p) d -> p c d", p=P)).then_inc(s["x_in"], 16)

        @block.tensor
        def _(pe):
            if load:
                pe.wait_ge(s["x_in"], 32)
            for n, (k, at, w) in enumerate(jobs):
                if n >= 4:
                    pe.wait_ge(s["taken"], n - 3)
                for i in range(w // P):
                    last = pe.transpose(PS[:, n % 4, i * P:(i + 1) * P], xnat[:, at // P + i, k * P:(k + 1) * P], G.c("ident"))
                last.then_inc(s["turned"], 1)

        @block.vector
        def _(dve):
            for n, (k, at, w) in enumerate(jobs):
                which = 1 if at < CTX else 0
                dve.wait_ge(s["turned"], n + 1)
                dve.tensor_scalar(hT[:, k, at:at + w], PS[:, n % 4, 0:w], G.modc[:, layer, 8 + k, which:which + 1],
                                  G.modc[:, layer, k, which:which + 1], ALU.mult, ALU.add).then_inc(s["taken"], 1)


def modulate_split(nc, G, layer, xnat, hi, lo):
    PS = G.PS
    jobs = [(k, at, w) for k in range(KT) for at, w in ((0, CTX), (CTX, 512), (CTX + 512, 512))]
    with nc.sbuf_tensor("h_full", [P, 4, 512], F32) as full, phase(nc, "turned taken hi_ok lo_ok") as (block, s):
        @block.tensor
        def _(pe):
            for n, (k, at, w) in enumerate(jobs):
                if n >= 4:
                    pe.wait_ge(s["taken"], n - 3)
                for i in range(w // P):
                    last = pe.transpose(PS[:, n % 4, i * P:(i + 1) * P], xnat[:, at // P + i, k * P:(k + 1) * P], G.c("ident"))
                last.then_inc(s["turned"], 1)

        @block.vector
        def _(dve):
            for n, (k, at, w) in enumerate(jobs):
                which = 1 if at < CTX else 0
                dve.wait_ge(s["turned"], n + 1)
                if n >= 4:
                    dve.wait_ge(s["lo_ok"], n - 3)
                dve.tensor_scalar(full[:, n % 4, 0:w], PS[:, n % 4, 0:w], G.modc[:, layer, 8 + k, which:which + 1],
                                  G.modc[:, layer, k, which:which + 1], ALU.mult, ALU.add).then_inc(s["taken"], 1)

        @block.scalar
        def _(act):
            for n, (k, at, w) in enumerate(jobs):
                act.wait_ge(s["taken"], n + 1)
                act.activation(hi[:, k, at:at + w], full[:, n % 4, 0:w], ACT.Copy).then_inc(s["hi_ok"], 1)

        @block.gpsimd
        def _(pool):
            for n, (k, at, w) in enumerate(jobs):
                pool.wait_ge(s["hi_ok"], n + 1)
                pool.tensor_tensor(lo[:, k, at:at + w], full[:, n % 4, 0:w], hi[:, k, at:at + w].bitcast(F32),
                                   ALU.subtract).then_inc(s["lo_ok"], 1)


def project_split(pe, PS, bank, wh, wl, hh, hl, pieces, at=0):
    for off, n in pieces:
        t = slice(at + off, at + off + n)
        for k in range(KT):
            pe.matmul(PS[:, bank + off // 512, 0:n], wh[:, k], hh[:, k, t], start=(k == 0), stop=False)
            pe.matmul(PS[:, bank + off // 512, 0:n], wh[:, k], hl[:, k, t], start=False, stop=False)
            last = pe.matmul(PS[:, bank + off // 512, 0:n], wl[:, k], hh[:, k, t], start=False, stop=(k == KT - 1))
    return last


def project(pe, PS, bank, w, hT, at=0, rows=P, cols=slice(0, P)):
    for off, n in PIECES if at == 0 else [(0, 512), (512, 512)]:
        for k in range(KT):
            last = pe.matmul(PS[0:rows, bank + off // 512, 0:n], w[:, k, cols], hT[:, k, at + off:at + off + n],
                             start=(k == 0), stop=(k == KT - 1))
    return last


def flat(PS, bank, rows=P, n=T):
    return PS[0:rows, bank:bank + 3, :].rearrange("p a b -> p (a b)")[:, 0:n]


def shift_mix(dve, step, raw, out, keep, mus, done=None, value=0):
    step.link(dve.tensor_scalar(out[:], raw[:], keep, None, ALU.mult))
    lat_o = out[:, CTX:].rearrange("p (r w) -> p r w", w=GRID_W)
    lat_r = raw[:, CTX:].rearrange("p (r w) -> p r w", w=GRID_W)
    W = GRID_W
    moves = [(0, lat_o[:, :, 1:], lat_r[:, :, :W - 1]), (1, lat_o[:, :, :W - 1], lat_r[:, :, 1:]),
             (2, lat_o[:, 1:, :], lat_r[:, :ROWS - 1, :]), (3, lat_o[:, :ROWS - 1, :], lat_r[:, 1:, :]),
             (0, out[:, 1:CTX], raw[:, 0:CTX - 1]), (1, out[:, 0:CTX - 1], raw[:, 1:CTX])]
    for n, (d, o, r) in enumerate(moves):
        ins = dve.scalar_tensor_tensor(o, r, mus[:, d:d + 1], o, ALU.mult, ALU.add)
        if n == len(moves) - 1 and done is not None:
            step.publish(ins, done, value)
        else:
            step.link(ins)


def lowrank_phase(nc, A, G, LW, LA):
    with ExitStack() as ctx:
        def sb(n, s):
            return ctx.enter_context(nc.sbuf_tensor(n, s, F32))
        w = sb("w_lr", [P, KT, 32 + 256])
        lg = sb("lr_gla", [32, T])
        raw = sb("lr_raw", [P, 2, T])
        mixed = sb("lr_mixed", [P, T])
        mus = sb("lr_mus", [P, 2, 4])
        keep = sb("lr_keep", [P, 2])
        PS = G.PS
        with phase(nc, "w_in prod taken mixed_ok step finished stored") as (block, s):
            @block.sync
            def _(sp):
                v = A.p["e_w_in"][0].rearrange("(k p) n -> p k n", p=P)
                sp.dma_start(w[:, :, 0:32], v[:, :, GLR:GLR + 32]).then_inc(s["w_in"], 16)
                sp.dma_start(w[:, :, 32:288], v[:, :, RWL:RWL + 256]).then_inc(s["w_in"], 16)
                sp.wait_ge(s["taken"], 1)
                sp.dma_start(A.lg_d, lg[:]).then_inc(s["stored"], 16)
                sp.dma_start(G.cst0[:], A.consts[:, G.ends[0]:G.ends[1]]).then_inc(s["stored"], 16)
                sp.dma_start(G.cst_rwkv[:], A.consts[:, G.ends[1]:]).then_inc(s["stored"], 16)
                sp.wait_ge(s["stored"], 48)

            @block.tensor
            def _(pe):
                pe.wait_ge(s["w_in"], 32)
                project(pe, G.PS, 0, w, G.hT, rows=32, cols=slice(0, 32)).then_inc(s["prod"], 1)
                project(pe, G.PS, 3, w, G.hT, cols=slice(32, 160)).then_inc(s["prod"], 1)
                pe.wait_ge(s["taken"], 1)
                project(pe, G.PS, 0, w, G.hT, cols=slice(160, 288)).then_inc(s["prod"], 1)

            @block.scalar
            def _(act):
                act.wait_ge(s["prod"], 1)
                act.activation(lg[:], flat(PS, 0, 32), ACT.Copy).then_inc(s["taken"], 1)
                for i in range(2):
                    act.wait_ge(s["prod"], 2 + i)
                    act.activation(raw[:, i], flat(PS, 3 * (1 - i)), ACT.Copy).then_inc(s["taken"], 1)
                act.wait_ge(s["mixed_ok"], 1)
                act.activation(LW[:], mixed[:], ACT.Tanh).then_inc(s["finished"], 1)

            @block.vector
            def _(dve):
                step = Steps(dve, s["step"])
                for i in range(2):
                    mu = G.vc[:, V_MULR + i:V_MULR + i + 1]
                    step.add(dve.tensor_scalar(mus[:, i], G.c("side"), mu, None, ALU.mult))
                    step.link(dve.tensor_scalar(keep[:, i:i + 1], mu, -1.0, 1.0, ALU.mult, ALU.add))
                for i in range(2):
                    dve.wait_ge(s["taken"], 2 + i)
                    shift_mix(dve, step, raw[:, i], (mixed, LA)[i], keep[:, i:i + 1], mus[:, i], s["mixed_ok"], i + 1)


PREP_JOBS = ["w0", "a0", "w1", "a1", "k", "r", "ksum", "v", "g", "bonus"]
ACT_PREP = ["w0", "a0", "w1", "a1", "k", "r", "e0", "e1", "sqrt", "v", "g", "silu"]
DVE_PREP = ["c0", "c1", "K", "sq", "R", "ksum", "rk", "V", "G", "bonus", "ready"]


def rwkv_prep(nc, A, G, B, p):
    with ExitStack() as ctx:
        def sb(n, s):
            return ctx.enter_context(nc.sbuf_tensor(n, s, F32))
        w = sb("w_pair", [P, 2, KT, P])
        wlr = sb("w_pair_lr", [P, 2, P])
        raw = sb("raw", [P, 2, T])
        R, K, kk, tmp = sb("R", [P, T]), sb("K", [P, T]), sb("kk", [P, T]), sb("tmp", [P, T])
        sg, aa = sb("sg", [P, 2, T]), sb("aa", [P, 2, T])
        mus, keep = sb("mus", [P, 4, 4]), sb("keep_mu", [P, 4])
        ka1 = sb("ka1", [P, 1])
        half = sb("half", [P, 2])
        khs = B.bonus
        PS = G.PS

        def col(j):
            return B.cols[:, j:j + 1]

        sems = "cols_in lr_in w_in0 w_in1 prod act_out dve_out step act_step consts_ok"
        with phase(nc, sems) as (block, s):
            w_in = [s["w_in0"], s["w_in1"]]

            @block.sync
            def _(sp):
                sp.dma_start(B.cols[:], A.cols0_d[bass.ds(p, 1)].rearrange("o p j -> p (o j)")).then_inc(s["cols_in"], 16)
                for d in range(2):
                    for i, n in enumerate(("rwkv_ww2_", "rwkv_wa2_")):
                        sp.dma_start(wlr[64 * d:64 * d + 64, i], A.p[n + "fb"[d]][0][:, bass.ds(p * P, P)]).then_inc(s["lr_in"], 16)
                win = A.p["e_w_in"][0].rearrange("(k p) n -> p k n", p=P)
                for n, at in enumerate((RK, RR, RV, RG)):
                    if n >= 2:
                        sp.wait_ge(s["prod"], after(PREP_JOBS, ("k", "r")[n - 2]))
                    sp.dma_start(w[:, n % 2], win[:, :, bass.ds(p * P + at, P)]).then_inc(w_in[n % 2], 16)

            @block.tensor
            def _(pe):
                def lowrank(n, src, i, d):
                    for off, m in PIECES:
                        last = pe.matmul(PS[:, 3 * (n % 2) + off // 512, 0:m], wlr[64 * d:64 * d + 64, i],
                                         src[64 * d:64 * d + 64, off:off + m], start=True, stop=True)
                    return last

                def head_sum(n, src):
                    for off, m in PIECES:
                        last = pe.matmul(PS[:, 3 * (n % 2) + off // 512, 0:m], G.c("heads"), src[:, off:off + m],
                                         start=True, stop=True)
                    return last

                pe.wait_ge(s["lr_in"], 64)
                for n, job in enumerate(PREP_JOBS):
                    if n >= 2:
                        before = PREP_JOBS[n - 2]
                        if before == "ksum":
                            pe.wait_ge(s["dve_out"], after(DVE_PREP, "ksum"))
                        else:
                            pe.wait_ge(s["act_out"], after(ACT_PREP, before))
                    if job in ("w0", "w1"):
                        last = lowrank(n, B.LW, 0, int(job[1]))
                    elif job in ("a0", "a1"):
                        last = lowrank(n, B.LA, 1, int(job[1]))
                    elif job == "ksum":
                        pe.wait_ge(s["dve_out"], after(DVE_PREP, "sq"))
                        last = head_sum(n, tmp)
                    elif job == "bonus":
                        pe.wait_ge(s["dve_out"], after(DVE_PREP, "rk"))
                        last = head_sum(n, tmp)
                    else:
                        i = "krvg".index(job)
                        pe.wait_ge(w_in[i % 2], 16 * (i // 2 + 1))
                        last = project(pe, PS, 3 * (n % 2), w[:, i % 2], G.hT)
                    last.then_inc(s["prod"], 1)

            @block.scalar
            def _(act):
                def job(name):
                    act.wait_ge(s["prod"], after(PREP_JOBS, name))
                    return flat(PS, 3 * (PREP_JOBS.index(name) % 2))

                act.wait_ge(s["cols_in"], 16)
                for d in range(2):
                    act.activation(sg[:, d], job(f"w{d}"), ACT.Sigmoid, bias=col(J_W0 + d)).then_inc(s["act_out"], 1)
                    act.activation(aa[:, d], job(f"a{d}"), ACT.Sigmoid, bias=col(J_A0 + d)).then_inc(s["act_out"], 1)
                act.activation(raw[:, 0], job("k"), ACT.Copy).then_inc(s["act_out"], 1)
                act.activation(raw[:, 1], job("r"), ACT.Copy).then_inc(s["act_out"], 1)
                act.wait_ge(s["consts_ok"], 2)
                for d in range(2):
                    act.wait_ge(s["dve_out"], after(DVE_PREP, f"c{d}"))
                    act.activation(B.kt[:, d], B.rt[:, d], ACT.Exp, scale=DEC, bias=half[:, 1:2])
                    ends = B.rt[:, d].rearrange("p (c t) -> p c t", t=CH)[:, :, (CH - 1) * (1 - d)]
                    act.activation(B.PL[:, d], ends, ACT.Exp, scale=-DEC).then_inc(s["act_step"], 1)
                    act.activation(B.at[:, d], B.at[:, d], ACT.Exp, scale=-DEC, bias=half[:, 0:1])
                    act.wait_ge(s["act_step"], d + 1)
                    act.activation(B.rt[:, d], B.rt[:, d], ACT.Exp, scale=-DEC, bias=half[:, 0:1]).then_inc(s["act_out"], 1)
                act.wait_ge(s["dve_out"], after(DVE_PREP, "ksum"))
                act.activation(tmp[:], tmp[:], ACT.Sqrt).then_inc(s["act_out"], 1)
                act.wait_ge(s["dve_out"], after(DVE_PREP, "K"))
                act.activation(raw[:, 0], job("v"), ACT.Copy).then_inc(s["act_out"], 1)
                act.activation(raw[:, 1], job("g"), ACT.Copy).then_inc(s["act_out"], 1)
                act.wait_ge(s["dve_out"], after(DVE_PREP, "G"))
                act.activation(B.sG[:], B.sG[:], ACT.Silu).then_inc(s["act_out"], 1)

            @block.vector
            def _(dve):
                step = Steps(dve, s["step"])
                out = Steps(dve, s["dve_out"])

                def from_act(name):
                    dve.wait_ge(s["act_out"], after(ACT_PREP, name))

                dve.memset(half[:, 0:1], HALF).then_inc(s["consts_ok"], 1)
                dve.memset(half[:, 1:2], -HALF).then_inc(s["consts_ok"], 1)
                dve.wait_ge(s["cols_in"], 16)
                step.add(dve.tensor_scalar(keep[:], B.cols[:, 0:4], -1.0, 1.0, ALU.mult, ALU.add))
                step.add(dve.tensor_scalar(ka1[:], col(J_KA), -1.0, 1.0, ALU.mult, ALU.add))
                for j in range(4):
                    step.add(dve.tensor_scalar(mus[:, j], G.c("side"), col(j), None, ALU.mult))
                step.wait()

                def mix(j, src, dst):
                    shift_mix(dve, step, src, dst, keep[:, j:j + 1], mus[:, j], s["dve_out"], out.n + 1)
                    out.n += 1

                for d in range(2):
                    from_act(f"a{d}")
                    c, x = (B.rt[:, d], sg[:, d]) if d == 0 else (B.rt[:, d][:, ::-1], sg[:, d][:, ::-1])
                    step.link(dve.tensor_tensor_scan(c, G.c("keep"), x, 0.0, ALU.mult, ALU.add))
                    out.add(dve.tensor_tensor(B.at[:, d], B.rt[:, d], sg[:, d], ALU.subtract))
                from_act("k")
                mix(1, raw[:, 0], K)
                step.link(dve.tensor_scalar(kk[:], K[:], col(J_KK), None, ALU.mult))
                out.add(dve.tensor_tensor(tmp[:], kk[:], kk[:], ALU.mult))
                from_act("r")
                mix(0, raw[:, 1], R)
                dve.wait_ge(s["prod"], after(PREP_JOBS, "ksum"))
                out.add(dve.tensor_scalar(tmp[:], flat(PS, 3 * (PREP_JOBS.index("ksum") % 2)), 1e-24, None, ALU.max))
                from_act("sqrt")
                step.link(dve.reciprocal(tmp[:], tmp[:]))
                step.link(dve.tensor_tensor(kk[:], kk[:], tmp[:], ALU.mult))
                for d in range(2):
                    step.link(dve.tensor_scalar(tmp[:], aa[:, d], col(J_KA), ka1[:], ALU.mult, ALU.add))
                    kh = khs if d == 0 else tmp
                    step.add(dve.tensor_tensor(kh[:], K[:], tmp[:], ALU.mult))
                    step.link(dve.tensor_tensor(aa[:, d], kk[:], aa[:, d], ALU.mult))
                    from_act(f"e{d}")
                    step.add(dve.tensor_tensor(B.bt[:, d], aa[:, d], B.kt[:, d], ALU.mult))
                    step.add(dve.tensor_tensor(B.rt[:, d], R[:], B.rt[:, d], ALU.mult))
                    step.add(dve.scalar_tensor_tensor(B.at[:, d], kk[:], -1.0, B.at[:, d], ALU.mult, ALU.mult))
                    step.link(dve.tensor_tensor(B.kt[:, d], kh[:], B.kt[:, d], ALU.mult))
                step.link(dve.tensor_tensor(khs[:], khs[:], tmp[:], ALU.add))
                out.add(dve.scalar_tensor_tensor(tmp[:], R[:], col(J_RK), khs[:], ALU.mult, ALU.mult))
                from_act("v")
                mix(2, raw[:, 0], B.V)
                from_act("g")
                mix(3, raw[:, 1], B.sG)
                dve.wait_ge(s["prod"], after(PREP_JOBS, "bonus"))
                out.add(dve.tensor_tensor(B.bonus[:], flat(PS, 3), B.V[:], ALU.mult))


PE_CHUNK = ["nat", "bx", "kx", "X1"] + [f"{x}{b}" for b in LEVELS[1:] for x in "YDT"] + ["Z", "WU", "out"]
ACT_CHUNK = ["nat", "I", "X1"] + [f"{x}{b}" for b in LEVELS[1:] for x in "YT"] + ["WU", "out"]
DVE_CHUNK = ["bx", "kx", "XT1"] + [f"X{b}" for b in LEVELS[1:]] + ["Z", "out"]
SLOTS = 2


def rwkv_chunks(nc, A, G, B):
    with ExitStack() as ctx:
        def sb(n, s):
            return ctx.enter_context(nc.sbuf_tensor(n, s, F32))
        AZ = [sb(f"AZ{i}", [P, 2, 2, 2, 64]) for i in range(SLOTS)]
        NAT = [sb(f"NAT{i}", [P, 2, 2, P]) for i in range(SLOTS)]
        VN = [sb(f"VN{i}", [P, P]) for i in range(SLOTS)]
        NR = [sb(f"NR{i}", [P, 2, 2, 2, P]) for i in range(SLOTS)]
        AR = [sb(f"AR{i}", [P, 2, 2, 2, P]) for i in range(SLOTS)]
        RK_ = [sb(f"RKS{i}", [P, 2, P]) for i in range(SLOTS)]
        X = [sb(f"X{i}", [P, 4, P]) for i in range(SLOTS)]
        XT = [sb(f"XT{i}", [P, 4, P]) for i in range(SLOTS)]
        Y = [sb(f"Y{i}", [P, 4, P]) for i in range(SLOTS)]
        WU = [sb(f"WU{i}", [P, 4, P]) for i in range(SLOTS)]
        PS = G.PS
        with phase(nc, "pe0 pe1 act0 act1 dve0 dve1") as (block, s):
            done = {"pe": [s["pe0"], s["pe1"]], "act": [s["act0"], s["act1"]], "dve": [s["dve0"], s["dve1"]]}
            names = {"pe": PE_CHUNK, "act": ACT_CHUNK, "dve": DVE_CHUNK}

            def need(eng, c, engine, name, back=0):
                n = c // SLOTS - back
                if n >= 0:
                    eng.wait_ge(done[engine][c % SLOTS], n * len(names[engine]) + after(names[engine], name))

            def bank(c, i):
                return PS[:, 4 * (c % SLOTS) + i, :]

            def tokens(c):
                return slice(CH * c, CH * c + CH)

            @block.tensor
            def _(pe):
                def stage(c, name):
                    i, t = c % SLOTS, tokens(c)
                    b0, b1, b2, b3 = (bank(c, j) for j in range(4))
                    if name == "nat":
                        need(pe, c, "dve", "Z", 1)
                        need(pe, c, "act", "WU", 1)
                        for d, b in enumerate((b0, b1)):
                            for j, x in enumerate((B.bt, B.kt, B.at)):
                                last = pe.transpose(b[:, j * P:(j + 1) * P], x[:, d, t], G.c("ident"))
                        last = pe.transpose(b0[:, 3 * P:4 * P], B.V[:, t], G.c("ident"))
                    elif name in ("bx", "kx"):
                        if name == "bx":
                            need(pe, c, "dve", "out", 1)
                            need(pe, c, "act", "out", 1)
                        else:
                            need(pe, c, "act", "nat")
                        for h in range(2):
                            q = slice(64 * h, 64 * h + 64)
                            b = ((b2, b3) if name == "bx" else (b0, b1))[h]
                            for d in range(2):
                                for j, x in enumerate((B.at, B.rt)):
                                    last = pe.matmul(b[:, (2 * d + j) * P:(2 * d + j + 1) * P],
                                                     (B.bt if name == "bx" else B.kt)[q, d, t], x[q, d, t],
                                                     start=True, stop=True)
                    elif name[0] in "XT":
                        if name == "X1":
                            need(pe, c, "dve", "XT1")
                        else:
                            need(pe, c, "dve", "X" + name[1:])
                        for u in range(4):
                            last = pe.transpose(b2[:, u * P:(u + 1) * P], (XT if name == "X1" else X)[i][:, u], G.c("ident"))
                    elif name[0] == "Y":
                        l = LEVELS.index(int(name[1:]))
                        if l == 1:
                            need(pe, c, "act", "X1")
                        else:
                            need(pe, c, "dve", f"X{LEVELS[l - 1]}")
                        for u in range(4):
                            last = pe.matmul(b0[:, u * P:(u + 1) * P], NR[i][:, u % 2, u // 2, 0], X[i][:, u], start=True, stop=True)
                    elif name[0] == "D":
                        need(pe, c, "act", "Y" + name[1:])
                        for u in range(4):
                            last = pe.matmul(b1[:, u * P:(u + 1) * P], XT[i][:, u], Y[i][:, u], start=True, stop=True)
                    elif name == "Z":
                        for u in range(4):
                            last = pe.matmul(b0[:, u * P:(u + 1) * P], AR[i][:, u % 2, u // 2, 0], VN[i][:], start=True, stop=True)
                    elif name == "WU":
                        need(pe, c, "dve", "Z")
                        need(pe, c, "act", f"T{LEVELS[-1]}")
                        for u in range(4):
                            last = pe.matmul(b1[:, u * P:(u + 1) * P], XT[i][:, u],
                                             AZ[i][:, u // 2, u % 2].rearrange("p a b -> p (a b)"), start=True, stop=True)
                    else:
                        need(pe, c, "act", "WU")
                        for h in range(2):
                            q = slice(64 * h, 64 * h + 64)
                            for d in range(2):
                                W, U = WU[i][:, 2 * d + h, 0:64], WU[i][:, 2 * d + h, 64:128]
                                b_, k_ = NAT[i][:, d, 0, q], NAT[i][:, d, 1, q]
                                pe.matmul(b2[q, d * P:(d + 1) * P], W, NR[i][:, h, d, 1], start=True, stop=True)
                                pe.matmul(b2[q, 256 + 64 * d:320 + 64 * d], W, b_, start=True, stop=True)
                                pe.matmul(b2[q, 384 + 64 * d:448 + 64 * d], b_, U, start=True, stop=False)
                                pe.matmul(b2[q, 384 + 64 * d:448 + 64 * d], k_, VN[i][:, q], start=False, stop=True)
                            for d in range(2):
                                pe.matmul(b3[q, 0:P], WU[i][:, 2 * d + h, 64:128], NR[i][:, h, d, 1], start=(d == 0), stop=False)
                            last = pe.matmul(b3[q, 0:P], VN[i][:, q], RK_[i][:, h], start=False, stop=True)
                    last.then_inc(done["pe"][i], 1)

                for c in range(0, NCH, SLOTS):
                    for name in [n for n in PE_CHUNK]:
                        for i in range(SLOTS):
                            stage(c + i, name)

            @block.scalar
            def _(act):
                def stage(c, name):
                    i = c % SLOTS
                    b0, b1, b2, b3 = (bank(c, j) for j in range(4))
                    if name != "I":
                        need(act, c, "pe", name)
                    if name == "nat":
                        for d, b in enumerate((b0, b1)):
                            act.activation(NAT[i][:, d].rearrange("p a b -> p (a b)"), b[:, 0:2 * P], ACT.Copy)
                            act.activation(AZ[i][:, d, :, 0, :], b[:, 2 * P:3 * P].rearrange("p (h n) -> p h n", h=2), ACT.Copy)
                        last = act.activation(VN[i][:], b0[:, 3 * P:4 * P], ACT.Copy)
                    elif name == "I":
                        last = act.activation(XT[i][:].rearrange("p a b -> p (a b)"), G.c("ident4"), ACT.Copy)
                    elif name == "out":
                        last = act.activation(B.Y[:, tokens(c)], b3[:, 0:P], ACT.Copy)
                    else:
                        dst, b = {"X": (X, b2), "T": (XT, b2), "Y": (Y, b0), "W": (WU, b1)}[name[0]]
                        last = act.activation(dst[i][:].rearrange("p a b -> p (a b)"), b, ACT.Copy)
                    last.then_inc(done["act"][i], 1)

                for c in range(0, NCH, SLOTS):
                    for name in ACT_CHUNK:
                        for i in range(SLOTS):
                            stage(c + i, name)

            @block.vector
            def _(dve):
                def stage(c, name):
                    i = c % SLOTS
                    b0, b1, b2, b3 = (bank(c, j) for j in range(4))
                    if name in ("bx", "kx"):
                        need(dve, c, "pe", name)
                        for h, b in enumerate((b2, b3) if name == "bx" else (b0, b1)):
                            last = dve.tensor_tensor((NR if name == "bx" else AR)[i][:, h].rearrange("p a b c -> p (a b c)"),
                                                     b, G.c("score"), ALU.mult)
                    elif name == "XT1":
                        need(dve, c, "act", "I")
                        need(dve, c, "dve", "kx")
                        dve.tensor_tensor(RK_[i][:], AR[i][:, :, 0, 1], AR[i][:, :, 1, 1], ALU.add)
                        last = dve.copy_predicated(XT[i][:].rearrange("p (d h) n -> p d h n", d=2),
                                                   G.c("level1").bitcast(I32).rearrange("p (d h n) -> p d h n", d=2, h=2),
                                                   NR[i][:, :, :, 0].rearrange("p h d n -> p d h n"))
                    elif name == "Z":
                        need(dve, c, "pe", "Z")
                        for h in range(2):
                            last = dve.tensor_copy(AZ[i][:, :, h, 1, :],
                                                   b0.rearrange("p (d h n) -> p d h n", d=2, h=2)[:, :, h, 64 * h:64 * h + 64])
                    elif name == "out":
                        need(dve, c, "pe", "out")
                        dve.tensor_tensor(B.QT[:, c], b2[:, 0:256].rearrange("p (d t) -> p d t", d=2), B.rt[:, :, tokens(c)], ALU.add)
                        dve.tensor_tensor(B.HS[:, c], b2[:, 384:512].rearrange("p (d t) -> p d t", d=2),
                                          B.PL[:, :, c:c + 1].broadcast_to([P, 2, 64]), ALU.mult)
                        last = dve.tensor_tensor(B.GT[:, c], b2[:, 256:384].rearrange("p (d t) -> p d t", d=2),
                                                 G.c("eye64")[:, None, :].broadcast_to([P, 2, 64]), ALU.add)
                    else:
                        need(dve, c, "pe", "D" + name[1:])
                        last = dve.copy_predicated(X[i][:].rearrange("p a b -> p (a b)"), G.c("level" + name[1:]).bitcast(I32), b1)
                    last.then_inc(done["dve"][i], 1)

                for c in range(0, NCH, SLOTS):
                    for name in DVE_CHUNK:
                        for i in range(SLOTS):
                            stage(c + i, name)


def chunk_chain(d):
    return list(zip(ORDER[d][:-1], ORDER[d][1:]))


def rwkv_finish(nc, A, G, B, p):
    with ExitStack() as ctx:
        def sb(n, s):
            return ctx.enter_context(nc.sbuf_tensor(n, s, F32))
        S = sb("S_rwkv", [P, 2, NCH, 64])
        yc, sq = sb("y_centered", [P, T]), sb("y_square", [P, T])
        eps = sb("eps_gn", [P, 1])
        PS = G.PS

        def col(j):
            return B.cols[:, j:j + 1]

        with phase(nc, "zero chain state0 state1 read_ps read_sb mean_ps centered squared var_ps root step stored eps_ok") as (block, s):
            state = [s["state0"], s["state1"]]

            @block.tensor
            def _(pe):
                pe.wait_ge(s["zero"], 2)
                for n in range(NCH - 1):
                    for d in range(2):
                        c = ORDER[d][n]
                        if n:
                            pe.wait_ge(state[d], n)
                        for h in range(2):
                            q = slice(64 * h, 64 * h + 64)
                            last = pe.matmul(PS[q, d, 0:64], B.GT[q, c, d], S[q, d, c], start=True, stop=True)
                        last.then_inc(s["chain"], 1)
                for d in range(2):
                    pe.wait_ge(state[d], NCH - 1)
                for c in range(NCH):
                    for h in range(2):
                        q = slice(64 * h, 64 * h + 64)
                        for d in range(2):
                            last = pe.matmul(PS[q, 2 + c // 4, (c % 4) * P:(c % 4 + 1) * P], S[q, d, c], B.QT[q, c, d],
                                             start=(d == 0), stop=(d == 1))
                last.then_inc(s["read_ps"], 1)
                pe.wait_ge(s["read_sb"], 1)
                for off, m in PIECES:
                    last = pe.matmul(PS[:, 5 + off // 512, 0:m], G.c("heads"), B.Y[:, off:off + m], start=True, stop=True)
                last.then_inc(s["mean_ps"], 1)
                pe.wait_ge(s["squared"], 1)
                for off, m in PIECES:
                    last = pe.matmul(PS[:, 2 + off // 512, 0:m], G.c("heads"), sq[:, off:off + m], start=True, stop=True)
                last.then_inc(s["var_ps"], 1)

            @block.scalar
            def _(act):
                act.wait_ge(s["centered"], 1)
                act.activation(sq[:], yc[:], ACT.Square).then_inc(s["squared"], 1)
                act.wait_ge(s["var_ps"], 1)
                act.wait_ge(s["eps_ok"], 1)
                act.activation(sq[:], flat(PS, 2), ACT.Sqrt, scale=1.0 / 64, bias=eps[:]).then_inc(s["root"], 1)

            @block.vector
            def _(dve):
                step = Steps(dve, s["step"])
                dve.memset(eps[:], EPS_GN).then_inc(s["eps_ok"], 1)
                for d in range(2):
                    dve.memset(S[:, d, ORDER[d][0]], 0.0).then_inc(s["zero"], 1)
                for n in range(NCH - 1):
                    for d in range(2):
                        c, c1 = ORDER[d][n], ORDER[d][n + 1]
                        dve.wait_ge(s["chain"], 2 * n + d + 1)
                        dve.scalar_tensor_tensor(S[:, d, c1], PS[:, d, 0:64], B.PL[:, d, c:c + 1], B.HS[:, c, d],
                                                 ALU.mult, ALU.add).then_inc(state[d], 1)
                dve.wait_ge(s["read_ps"], 1)
                step.publish(dve.tensor_tensor(B.Y[:], flat(PS, 2), B.Y[:], ALU.add), s["read_sb"], 1)
                dve.wait_ge(s["mean_ps"], 1)
                step.publish(dve.scalar_tensor_tensor(yc[:], flat(PS, 5), -1.0 / 64, B.Y[:], ALU.mult, ALU.add), s["centered"], 1)
                dve.wait_ge(s["root"], 1)
                step.link(dve.reciprocal(sq[:], sq[:]))
                step.link(dve.tensor_tensor(yc[:], yc[:], sq[:], ALU.mult))
                step.link(dve.tensor_scalar(yc[:], yc[:], col(J_GG), col(J_GB), ALU.mult, ALU.add))
                step.link(dve.tensor_tensor(yc[:], yc[:], B.bonus[:], ALU.add))
                step.publish(dve.tensor_tensor(yc[:], yc[:], B.sG[:], ALU.mult), s["read_sb"], 2)

            @block.sync
            def _(sp):
                sp.wait_ge(s["read_sb"], 2)
                sp.dma_start(A.yT_d[bass.ds(p + 4, 1)].rearrange("o p t -> p (o t)"), yc[:]).then_inc(s["stored"], 16)
                sp.wait_ge(s["stored"], 16)


GLA_JOBS = ["x0", "x1", "q", "k", "g0", "g1"]
ACT_GLA = ["x0", "l0", "x1", "l1", "q", "k", "g0", "g1", "eq0", "ek0", "eq1", "ek1"]
DVE_GLA = ["b0", "b1", "kd0", "kd1"]


def gla_prep(nc, A, G, B, g):
    with ExitStack() as ctx:
        def sb(n, s):
            return ctx.enter_context(nc.sbuf_tensor(n, s, F32))
        w = sb("w_gla", [P, 2, KT, P])
        wv = sb("w_gla_v", [P, KT, 2 * P])
        wa2 = sb("wa2", [32, 2, P])
        lg = sb("lg", [32, T])
        ba = sb("gla_ba", [P, 2])
        x, l, kd = sb("gla_x", [P, 2, T]), sb("gla_l", [P, 2, T]), sb("gla_kd", [P, 2, T])
        PS = G.PS
        sems = "zeroed lr_in w_in0 w_in1 wv_in prod v_ps v_sb act_out dve_out step act_step turned kn_sb"
        with phase(nc, sems) as (block, s):
            w_in = [s["w_in0"], s["w_in1"]]

            @block.sync
            def _(sp):
                sp.wait_ge(s["zeroed"], 1)
                for d in range(2):
                    q = slice(64 * d, 64 * d + 64)
                    sp.dma_start(wa2[16 * d:16 * d + 16, :, q],
                                 A.p["gla_wa2_" + "fb"[d]][0][:, bass.ds(g * P, P)].rearrange("r (h c) -> r h c", h=2)).then_inc(s["lr_in"], 16)
                    for h in range(2):
                        sp.dma_start(ba[q, h:h + 1], A.p["gla_ba_" + "fb"[d]][0][bass.ds(g * P + 64 * h, 64)].rearrange("(c o) -> c o", o=1)).then_inc(s["lr_in"], 16)
                sp.dma_start(lg[:], A.lg_d).then_inc(s["lr_in"], 16)
                win = A.p["e_w_in"][0].rearrange("(k p) n -> p k n", p=P)
                starts = [g * P + GQ, g * P + GK, g * 2 * P + GG, g * 2 * P + (GG + P)]
                for n, at in enumerate(starts):
                    if n >= 2:
                        sp.wait_ge(s["prod"], after(GLA_JOBS, ("q", "k")[n - 2]))
                    sp.dma_start(w[:, n % 2], win[:, :, bass.ds(at, P)]).then_inc(w_in[n % 2], 16)
                    if n == 1:
                        sp.dma_start(wv[:], win[:, :, bass.ds(g * 2 * P + GV, 2 * P)]).then_inc(s["wv_in"], 16)

            @block.tensor
            def _(pe):
                pe.wait_ge(s["lr_in"], 7 * 16)
                for n, job in enumerate(GLA_JOBS):
                    if n >= 2:
                        pe.wait_ge(s["act_out"], after(ACT_GLA, GLA_JOBS[n - 2]))
                    if n < 2:
                        for off, m in PIECES:
                            last = pe.matmul(PS[:, 3 * n + off // 512, 0:m], wa2[:, n], lg[:, off:off + m], start=True, stop=True)
                    else:
                        pe.wait_ge(w_in[n % 2], 16 * (n // 2))
                        last = project(pe, PS, 3 * (n % 2), w[:, n % 2], G.hT)
                    last.then_inc(s["prod"], 1)
                pe.wait_ge(s["wv_in"], 16)
                for c in range(NCH):
                    if c >= 2:
                        pe.wait_ge(s["v_sb"], c - 1)
                    for k in range(KT):
                        last = pe.matmul(PS[:, 6 + c % 2, 0:2 * P], G.hT[:, k, c * CH:(c + 1) * CH], wv[:, k],
                                         start=(k == 0), stop=(k == KT - 1))
                    last.then_inc(s["v_ps"], 1)
                for h in range(2):
                    pe.wait_ge(s["dve_out"], after(DVE_GLA, f"kd{h}"))
                    if h == 0:
                        pe.wait_ge(s["act_out"], after(ACT_GLA, "g1"))
                    for j in range(3):
                        for c in range(4 * j, min(4 * j + 4, NCH)):
                            last = pe.transpose(PS[:, 3 * h + j, (c % 4) * P:(c % 4 + 1) * P], kd[:, h, c * CH:(c + 1) * CH], G.c("ident"))
                    last.then_inc(s["turned"], 1)

            @block.scalar
            def _(act):
                step = Steps(act, s["act_step"])
                out = Steps(act, s["act_out"])

                def job(name):
                    act.wait_ge(s["prod"], after(GLA_JOBS, name))
                    return flat(PS, 3 * (GLA_JOBS.index(name) % 2))

                act.wait_ge(s["lr_in"], 7 * 16)
                for h in range(2):
                    out.link(act.activation(x[:, h], job(f"x{h}"), ACT.Identity, bias=ba[:, h:h + 1]))
                    step.link(act.activation(l[:, h], x[:, h], ACT.Abs))
                    step.link(act.activation(l[:, h], l[:, h], ACT.Exp, scale=-1.0))
                    out.add(act.activation(l[:, h], l[:, h], ACT.Ln, bias=G.c("ones")[:, 0:1]))
                for name, dst, scale in (("q", B.q, 0.125), ("k", B.k, 1.0)):
                    src = job(name)
                    for h in range(2):
                        for d in range(2):
                            last = act.activation(dst[64 * d:64 * d + 64, h], src[64 * h:64 * h + 64], ACT.Copy, scale=scale)
                    out.add(last)
                for h in range(2):
                    out.add(act.activation(B.sG[:, h], job(f"g{h}"), ACT.Silu))
                for c in range(NCH):
                    act.wait_ge(s["v_ps"], c + 1)
                    act.activation(B.V[:, c], PS[:, 6 + c % 2, 0:2 * P], ACT.Copy).then_inc(s["v_sb"], 1)
                for h in range(2):
                    act.wait_ge(s["dve_out"], after(DVE_GLA, f"b{h}"))
                    out.add(act.activation(B.qd[:, h], B.b[:, h], ACT.Exp, scale=1.0 / 16))
                    for d in range(2):
                        q = slice(64 * d, 64 * d + 64)
                        act.activation(B.tot[q, h], B.b[q, h].rearrange("p (c t) -> p c t", t=CH)[:, :, (CH - 1) * (1 - d)],
                                       ACT.Exp, scale=1.0 / 16)
                    out.add(act.activation(kd[:, h], kd[:, h], ACT.Exp, scale=1.0 / 16))
                for h in range(2):
                    act.wait_ge(s["turned"], h + 1)
                    act.activation(B.KN[:, h].rearrange("p c n -> p (c n)"), flat(PS, 3 * h), ACT.Copy).then_inc(s["kn_sb"], 1)

            @block.vector
            def _(dve):
                step = Steps(dve, s["step"])
                out = Steps(dve, s["dve_out"])
                dve.memset(wa2[:], 0.0).then_inc(s["zeroed"], 1)
                for h in range(2):
                    dve.wait_ge(s["act_out"], after(ACT_GLA, f"l{h}"))
                    step.link(dve.scalar_tensor_tensor(x[:, h], x[:, h], 0.0, l[:, h], ALU.min, ALU.subtract))
                    rows = [slice(64 * d, 64 * d + 64) for d in range(2)]
                    for d, q in enumerate(rows):
                        c, v = (B.b[q, h], x[q, h]) if d == 0 else (B.b[q, h][:, ::-1], x[q, h][:, ::-1])
                        step.add(dve.tensor_tensor_scan(c, G.c("keep")[q], v, 0.0, ALU.mult, ALU.add))
                    step.wait()
                    for d, q in enumerate(rows):
                        b3 = B.b[q, h].rearrange("p (c t) -> p c t", t=CH)
                        end = (CH - 1) * (1 - d)
                        last = dve.tensor_tensor(kd[q, h].rearrange("p (c t) -> p c t", t=CH), b3[:, :, end:end + 1].broadcast_to([64, NCH, CH]), b3,
                                                 ALU.subtract)
                    out.add(last)
                for h in range(2):
                    dve.wait_ge(s["act_out"], after(ACT_GLA, f"ek{h}"))
                    dve.tensor_tensor(B.qd[:, h], B.qd[:, h], B.q[:, h], ALU.mult)
                    out.add(dve.tensor_tensor(kd[:, h], kd[:, h], B.k[:, h], ALU.mult))


def gla_scores(nc, A, G, B):
    with ExitStack() as ctx:
        def sb(n, s):
            return ctx.enter_context(nc.sbuf_tensor(n, s, F32))
        E = sb("lev_e", [P, 2, 2, T])
        QL, KL = sb("lev_q", [P, 2, 2, T]), sb("lev_k", [P, 2, 2, T])
        PS = G.PS
        groups = [(0, 4), (4, 4), (8, 2)]
        jobs = [(b, h, j) for b in [0] + LEVELS for h in range(2) for j in range(3)]

        def half(x, b, d, right):
            v = x[64 * d:64 * d + 64].rearrange("p (n t) -> p n t", t=2 * b)
            return v[:, :, b:] if right else v[:, :, :b]

        with phase(nc, "dist away expd q_zero q_ok k_ok scored merged") as (block, s):
            def buffer_free(eng, lv, h):
                if lv >= 2:
                    eng.wait_ge(s["scored"], jobs.index((LEVELS[lv - 2], h, 2)) + 1)

            @block.tensor
            def _(pe):
                for n, (b, h, j) in enumerate(jobs):
                    lv = LEVELS.index(b) if b else -1
                    if n >= 8:
                        pe.wait_ge(s["merged"], n - 7)
                    if b:
                        pe.wait_ge(s["q_ok"], 2 * lv + h + 1)
                        pe.wait_ge(s["k_ok"], 2 * lv + h + 1)
                    for i in range(groups[j][1]):
                        c = groups[j][0] + i
                        t = slice(c * CH, c * CH + CH)
                        lhs, rhs = (KL[:, lv % 2, h, t], QL[:, lv % 2, h, t]) if b else (B.k[:, h, t], B.q[:, h, t])
                        last = pe.matmul(PS[:, n % 8, i * P:(i + 1) * P], lhs, rhs, start=True, stop=True)
                    last.then_inc(s["scored"], 1)

            def merge_jobs(dve, level):
                for n, (b, h, j) in enumerate(jobs):
                    if b != level:
                        continue
                    c0, m = groups[j]
                    dve.wait_ge(s["scored"], n + 1)
                    if n >= 6:
                        dve.wait_ge(s["merged"], n - 5)
                    out = B.A[:, c0:c0 + m, h, :]
                    ps = PS[:, n % 8, 0:m * P].rearrange("p (c t) -> p c t", t=P)
                    if not b:
                        ins = dve.tensor_tensor(out, ps, G.c("ident")[:, None, :].broadcast_to([P, m, P]), ALU.mult)
                    else:
                        ins = dve.copy_predicated(out, G.c(f"parted{b}").bitcast(I32)[:, None, :].broadcast_to([P, m, P]), ps)
                    ins.then_inc(s["merged"], 1)

            @block.vector
            def _(dve):
                for lv, b in enumerate(LEVELS):
                    for h in range(2):
                        buffer_free(dve, lv, h)
                        if lv >= 2:
                            dve.wait_ge(s["k_ok"], 2 * (lv - 2) + h + 1)
                            dve.wait_ge(s["q_ok"], 2 * (lv - 2) + h + 1)
                        blocks = B.b[:, h].rearrange("p (n t) -> p n t", t=2 * b)
                        dve.tensor_tensor(E[:, lv % 2, h].rearrange("p (n t) -> p n t", t=2 * b), blocks,
                                          blocks[:, :, b:b + 1].broadcast_to([P, T // (2 * b), 2 * b]), ALU.subtract).then_inc(s["dist"], 1)
                    merge_jobs(dve, LEVELS[lv - 1] if lv else 0)
                    for h in range(2):
                        dve.wait_ge(s["expd"], 2 * lv + h + 1)
                        dve.wait_ge(s["q_zero"], 2 * lv + h + 1)
                        for d in range(2):
                            last = dve.tensor_tensor(half(QL[:, lv % 2, h], b, d, d == 0), half(E[:, lv % 2, h], b, d, d == 0),
                                                     half(B.q[:, h], b, d, d == 0), ALU.mult)
                        last.then_inc(s["q_ok"], 1)
                merge_jobs(dve, LEVELS[-1])

            @block.scalar
            def _(act):
                for n in range(2 * len(LEVELS)):
                    e = E[:, n // 2 % 2, n % 2]
                    act.wait_ge(s["dist"], n + 1)
                    act.activation(e, e, ACT.Abs).then_inc(s["away"], 1)
                    act.wait_ge(s["away"], n + 1)
                    act.activation(e, e, ACT.Exp, scale=-1.0 / 16).then_inc(s["expd"], 1)

            @block.gpsimd
            def _(pool):
                def zeros(n):
                    lv, h = n // 2, n % 2
                    buffer_free(pool, lv, h)
                    if lv >= 2:
                        pool.wait_ge(s["q_ok"], 2 * (lv - 2) + h + 1)
                    for d in range(2):
                        last = pool.memset(half(QL[:, lv % 2, h], LEVELS[lv], d, d == 1), 0.0)
                    last.then_inc(s["q_zero"], 1)

                zeros(0)
                for n in range(2 * len(LEVELS)):
                    lv, h = n // 2, n % 2
                    pool.wait_ge(s["expd"], n + 1)
                    pool.wait_ge(s["q_zero"], n + 1)
                    pool.tensor_tensor(KL[:, lv % 2, h], E[:, lv % 2, h], B.k[:, h], ALU.mult).then_inc(s["k_ok"], 1)
                    pool.wait_ge(s["k_ok"], n + 1)
                    if n + 1 < 2 * len(LEVELS):
                        zeros(n + 1)


def gla_out(nc, A, G, B, g):
    with ExitStack() as ctx:
        def sb(n, s):
            return ctx.enter_context(nc.sbuf_tensor(n, s, F32))
        S = sb("S_gla", [P, 2, NCH, P])
        o, sq = sb("gla_o", [P, 2, T]), sb("gla_sq", [P, 2, T])
        eps = sb("eps_gla", [P, 1])
        PS = G.PS
        with phase(nc, "zero outer state00 state01 state10 state11 o_ps o_sb squared var_ps root step y_ok stored eps_ok") as (block, s):
            state = [[s["state00"], s["state01"]], [s["state10"], s["state11"]]]

            def cols(h, c):
                return PS[:, 3 * h + c // 4, (c % 4) * P:(c % 4 + 1) * P]

            @block.tensor
            def _(pe):
                for h in range(2):
                    for c in range(NCH):
                        last = pe.matmul(cols(h, c), B.KN[:, h, c], B.V[:, c, h * P:(h + 1) * P], start=True, stop=True)
                    last.then_inc(s["outer"], 1)
                pe.wait_ge(s["zero"], 4)
                for h in range(2):
                    for d in range(2):
                        pe.wait_ge(state[h][d], NCH - 1)
                    for c in range(NCH):
                        pe.matmul(cols(h, c), B.V[:, c, h * P:(h + 1) * P], B.A[:, c, h], start=True, stop=False)
                        last = pe.matmul(cols(h, c), S[:, h, c], B.qd[:, h, c * CH:c * CH + CH], start=False, stop=True)
                    last.then_inc(s["o_ps"], 1)
                for h in range(2):
                    pe.wait_ge(s["squared"], h + 1)
                    for off, m in PIECES:
                        last = pe.matmul(PS[:, 3 * h + off // 512, 0:m], G.c("ones"), sq[:, h, off:off + m], start=True, stop=True)
                    last.then_inc(s["var_ps"], 1)

            @block.scalar
            def _(act):
                for h in range(2):
                    act.wait_ge(s["o_sb"], h + 1)
                    act.activation(sq[:, h], o[:, h], ACT.Square).then_inc(s["squared"], 1)
                act.wait_ge(s["eps_ok"], 1)
                for h in range(2):
                    act.wait_ge(s["var_ps"], h + 1)
                    act.activation(sq[:, h], flat(PS, 3 * h), ACT.Sqrt, scale=1.0 / P, bias=eps[:]).then_inc(s["root"], 1)

            @block.vector
            def _(dve):
                step = Steps(dve, s["step"])
                dve.memset(eps[:], EPS_LN).then_inc(s["eps_ok"], 1)
                for h in range(2):
                    for d in range(2):
                        dve.memset(S[64 * d:64 * d + 64, h, ORDER[d][0]], 0.0).then_inc(s["zero"], 1)
                dve.wait_ge(s["zero"], 4)
                dve.wait_ge(s["outer"], 2)
                for n in range(NCH - 1):
                    for h in range(2):
                        for d in range(2):
                            q = slice(64 * d, 64 * d + 64)
                            c, c1 = ORDER[d][n], ORDER[d][n + 1]
                            if n:
                                dve.wait_ge(state[h][d], n)
                            dve.scalar_tensor_tensor(S[q, h, c1], S[q, h, c], B.tot[q, h, c:c + 1], cols(h, c)[q],
                                                     ALU.mult, ALU.add).then_inc(state[h][d], 1)
                for h in range(2):
                    dve.wait_ge(s["o_ps"], h + 1)
                    dve.tensor_copy(o[:, h], flat(PS, 3 * h)).then_inc(s["o_sb"], 1)
                for h in range(2):
                    dve.wait_ge(s["root"], h + 1)
                    step.link(dve.reciprocal(sq[:, h], sq[:, h]))
                    step.link(dve.scalar_tensor_tensor(o[:, h], o[:, h], G.vc[:, V_GNG:V_GNG + 1], sq[:, h], ALU.mult, ALU.mult))
                    dve.tensor_tensor(o[:, h], o[:, h], B.sG[:, h], ALU.mult).then_inc(s["y_ok"], 1)

            @block.sync
            def _(sp):
                for h in range(2):
                    sp.wait_ge(s["y_ok"], h + 1)
                    sp.dma_start(A.yT_d[bass.ds(g * 2 + h, 1)].rearrange("o p t -> p (o t)"), o[:, h]).then_inc(s["stored"], 16)
                sp.wait_ge(s["stored"], 32)


def out_phase(nc, A, G, layer, yT_d, w_out, n_k, tiles, x_of, xnew, store):
    with ExitStack() as ctx:
        def sb(n, s):
            return ctx.enter_context(nc.sbuf_tensor(f"{n}{layer}", s, F32))
        w = sb("w_out", [P, n_k, D])
        y = sb("y_in", [P, n_k, P * len(tiles)])
        x = sb("x_res", [P, 3, D])
        gate, ln = sb("gate_row", [P, 2, D]), sb("ln_row", [P, 2, D])
        r = sb("resid", [P, 2, D])
        st = sb("stats", [P, 2, 2, 6])
        mv, rstd = sb("mean_var", [P, 2, 2]), sb("rstd", [P, 2, 2])
        eps = sb("eps_ln", [P, 1])
        PS = G.PS
        n_gate = 2 if layer == 0 else 1
        ktiles = 4
        sems = "row_in k_in0 k_in1 k_in2 k_in3 x_in0 x_in1 x_in2 prod summed mean_ok root normed scaled added stored0 stored1 step eps_ok"
        ring = 2 if layer else len(tiles)
        with phase(nc, sems) as (block, s):
            stored = [s["stored0"], s["stored1"]]
            k_in = [s["k_in0"], s["k_in1"], s["k_in2"], s["k_in3"]]
            x_in = [s["x_in0"], s["x_in1"], s["x_in2"]]

            @block.sync
            def _(sp):
                wv = w_out.rearrange("(k p) n -> p k n", p=P)
                for i in range(n_k // ktiles):
                    q = slice(i * ktiles, (i + 1) * ktiles)
                    sp.dma_start(y[:, q], yT_d[q].rearrange("k p t -> p k t")).then_inc(k_in[i], 16)
                    sp.dma_start(w[:, q], wv[:, q]).then_inc(k_in[i], 16)
                sp.dma_start(gate[:, 0:n_gate], A.gates_d[2 * layer:2 * layer + n_gate].rearrange("g p n -> p g n")).then_inc(s["row_in"], 16)
                for i, v in enumerate(("ln_g", "ln_b")):
                    sp.dma_start(ln[:, i], A.p[v][layer:layer + 1, :].broadcast_to([P, D])).then_inc(s["row_in"], 16)
                for n in range(min(3, len(tiles))):
                    sp.dma_start(x[:, n], x_of(tiles[n])).then_inc(x_in[n], 16)
                for n, t in enumerate(tiles):
                    sp.wait_ge(s["added"], n + 1)
                    sp.dma_start(store(t), xnew[:, n % ring]).then_inc(stored[n % 2], 16)
                    if n + 3 < len(tiles):
                        sp.wait_ge(s["summed"], n + 1)
                        sp.dma_start(x[:, n % 3], x_of(tiles[n + 3])).then_inc(x_in[n % 3], 16)
                for i in range(2):
                    sp.wait_ge(stored[i], 16 * (len(tiles) // 2))

            @block.tensor
            def _(pe):
                for n in range(len(tiles)):
                    if n >= 4:
                        pe.wait_ge(s["summed"], n - 3)
                    for k in range(n_k):
                        if n == 0 and k % ktiles == 0:
                            pe.wait_ge(k_in[k // ktiles], 32)
                        for h in range(2):
                            last = pe.matmul(PS[:, 2 * (n % 4) + h, :], y[:, k, n * P:(n + 1) * P], w[:, k, 512 * h:512 * h + 512],
                                             start=(k == 0), stop=(k == n_k - 1))
                    last.then_inc(s["prod"], 1)

            @block.vector
            def _(dve):
                step = Steps(dve, s["step"])
                dve.memset(eps[:], EPS_LN).then_inc(s["eps_ok"], 1)
                dve.wait_ge(s["row_in"], 48)
                for n, t in enumerate(tiles):
                    i = n % 2
                    gt = gate[:, 1 if (layer == 0 and t < CTXCH) else 0]
                    dve.wait_ge(s["prod"], n + 1)
                    if n >= 2:
                        dve.wait_ge(s["normed"], n - 1)
                    step.link(dve.tensor_tensor(r[:, i], PS[:, 2 * (n % 4):2 * (n % 4) + 2, :].rearrange("p a b -> p (a b)"), gt, ALU.mult))
                    dve.wait_ge(x_in[n % 3], 16 * (n // 3 + 1))
                    step.publish(dve.scalar_tensor_tensor(r[:, i], x[:, n % 3], ALPHA, r[:, i], ALU.mult, ALU.add), s["summed"], n + 1)
                    for h in range(2):
                        step.add(dve.bn_stats(st[:, i, h], r[:, i, 512 * h:512 * h + 512]))
                    step.wait()
                    step.publish(dve.bn_aggr(mv[:, i], st[:, i].rearrange("p a b -> p (a b)")), s["mean_ok"], n + 1)
                    dve.wait_ge(s["root"], n + 1)
                    step.link(dve.reciprocal(rstd[:, i, 0:1], rstd[:, i, 0:1]))
                    step.link(dve.scalar_tensor_tensor(rstd[:, i, 1:2], mv[:, i, 0:1], -1.0, rstd[:, i, 0:1], ALU.mult, ALU.mult))
                    if n >= ring:
                        dve.wait_ge(stored[n % 2], 16 * (n // 2))
                    dve.tensor_scalar(xnew[:, n % ring], r[:, i], rstd[:, i, 0:1], rstd[:, i, 1:2], ALU.mult, ALU.add).then_inc(s["normed"], 1)

            @block.scalar
            def _(act):
                act.wait_ge(s["eps_ok"], 1)
                for n in range(len(tiles)):
                    act.wait_ge(s["mean_ok"], n + 1)
                    if n >= 2:
                        act.wait_ge(s["normed"], n - 1)
                    act.activation(rstd[:, n % 2, 0:1], mv[:, n % 2, 1:2], ACT.Sqrt, bias=eps[:]).then_inc(s["root"], 1)

            @block.gpsimd
            def _(pool):
                pool.wait_ge(s["row_in"], 48)
                for n in range(len(tiles)):
                    pool.wait_ge(s["normed"], n + 1)
                    pool.tensor_tensor(xnew[:, n % ring], xnew[:, n % ring], ln[:, 0], ALU.mult).then_inc(s["scaled"], 1)
                    pool.wait_ge(s["scaled"], n + 1)
                    pool.tensor_tensor(xnew[:, n % ring], xnew[:, n % ring], ln[:, 1], ALU.add).then_inc(s["added"], 1)


PADW = GRID_W + 2


def mlstm_inputs(nc, A, G, B):
    TILES = NT1 // HEADS1
    with ExitStack() as ctx:
        def sb(n, s, t=F32):
            return ctx.enter_context(nc.sbuf_tensor(n, s, t))
        free = B.xnew[:].rearrange("p c d -> p (c d)")
        sizes = np.cumsum([0, 4 * KT * P, 2 * T, 2 * SEQ, T]).tolist()
        w, v, sz, acc = (free[:, a:b] for a, b in zip(sizes, sizes[1:]))
        w = w.rearrange("p (i j k n) -> p i j k n", i=2, j=2, k=KT)
        v = v.rearrange("p (i c n) -> p i c n", i=2, c=NCH)
        sz = sz.rearrange("p (i t) -> p i t", i=2)
        wh = [sb(f"w_in1_hi{i}", [P, 2, KT, P], F32R) for i in range(2)]
        wl = [sb(f"w_in1_lo{i}", [P, 2, KT, P], F32R) for i in range(2)]
        cols = sb("tile_cols", [P, TILES, TILE_PARAMS])
        wqkv = sb("wqkv", [P, TILES, 3, 4])
        wg = sb("w_gates", [P, TILES, 3, 4, 4])
        BD, BDT = sb("BD", [P, 2, 3, P]), sb("BDT", [P, 2, 3, P])
        BQK = sb("BQK", [P, 2, P])
        WG = sb("WG", [P, 2, 2, P])
        xm, xc = sb("xm", [P, 2, T]), sb("xc", [P, 2, T])
        padl, padc = sb("padl", [P, ROWS + 2, PADW]), sb("padc", [P, CTX + 2])
        q = sb("q_out", [P, 2, SEQ])
        PS = G.PS
        with phase(nc, "gates_zero") as (block, s):
            @block.vector
            def _(dve):
                dve.memset(B.gates[:], 0.0)
                dve.memset(padl[:].rearrange("p a b -> p (a b)"), 0.0)
                dve.memset(padc[:], 0.0)
                dve.memset(WG[:], 0.0).then_inc(s["gates_zero"], 1)
        with nc.Fori(0, HEADS1) as r:
            sems = ("cols_in w_in0 w_in1 hi_ok lo_ok small_in bd_ok bdt_ps bdt_sb fold_ps fold_sb bqk_sb xm_ps xm_sb padded "
                    "z_ps z_sb conv_ok xc_ok q_ps q_sb v_ps v_sb gate_ps gate_sb step stored0 stored1")
            with phase(nc, sems) as (block, s):
                w_in, stored = [s["w_in0"], s["w_in1"]], [s["stored0"], s["stored1"]]

                @block.sync
                def _(sp):
                    win = A.p["o_w_in"][0].rearrange("(k p) n -> p k n", p=P)

                    def load(t):
                        for j in range(2):
                            sp.dma_start(w[:, t % 2, j], win[:, :, bass.ds(r * (TILES * P) + (t * P + j * INNER), P)]).then_inc(w_in[t % 2], 16)

                    def dst(x, t):
                        return x[bass.ds(r * TILES + t, 1)].rearrange("o p t -> p (o t)")

                    load(0)
                    sp.dma_start(cols[:], A.cols1_d[bass.ds(r * TILES, TILES)].rearrange("i p j -> p i j")).then_inc(s["cols_in"], 16)
                    load(1)
                    for t in range(TILES):
                        if t + 2 < TILES:
                            sp.wait_ge(s["hi_ok"], t + 1)
                            sp.wait_ge(s["lo_ok"], t + 1)
                            load(t + 2)
                        sp.wait_ge(s["z_sb"], t + 1)
                        sp.dma_start(dst(B.sz_d, t), sz[:, t % 2]).then_inc(stored[t % 2], 16)
                        sp.wait_ge(s["v_sb"], 3 * t + 3)
                        sp.dma_start(B.v_d[bass.ds(r * TILES + t, 1)].rearrange("o p c n -> p (o c) n"), v[:, t % 2]).then_inc(stored[t % 2], 16)
                        sp.wait_ge(s["xc_ok"], t + 1)
                        sp.dma_start(dst(B.k_d, t), xc[:, t % 2]).then_inc(stored[t % 2], 16)
                        sp.wait_ge(s["q_sb"], t + 1)
                        sp.dma_start(dst(B.q_d, t), q[:, t % 2]).then_inc(stored[t % 2], 16)
                    for i in range(2):
                        sp.wait_ge(stored[i], TILES // 2 * 4 * 16)

                @block.tensor
                def _(pe):
                    def x_part(t):
                        i = t % 2
                        pe.wait_ge(s["bd_ok"], t + 1)
                        if t:
                            pe.wait_ge(s["v_sb"], 3 * t)
                            pe.wait_ge(s["xm_sb"], t)
                            pe.wait_ge(s["padded"], t)
                        for j in range(3):
                            last = pe.transpose(PS[:, 7, j * P:(j + 1) * P], BD[:, i, j], G.c("ident"))
                        last.then_inc(s["bdt_ps"], 1)
                        pe.wait_ge(s["hi_ok"], t + 1)
                        pe.wait_ge(s["lo_ok"], t + 1)
                        project_split(pe, PS, 0, wh[i][:, 0], wl[i][:, 0], G.hT_hi, G.hT_lo, PIECES).then_inc(s["xm_ps"], 1)
                        pe.wait_ge(s["bdt_sb"], t + 1)
                        g = [wg[:, t, j].rearrange("p a b -> p (a b)") for j in range(3)]
                        pe.matmul(PS[:, 7, 0:16], BDT[:, i, 0], g[0], start=True, stop=False)
                        pe.matmul(PS[:, 7, 0:16], BDT[:, i, 1], g[1], start=False, stop=True)
                        pe.matmul(PS[:, 7, 16:32], BDT[:, i, 2], g[2], start=True, stop=True)
                        pe.matmul(PS[:, 7, P:2 * P], BDT[:, i, 0], BDT[:, i, 1], start=True, stop=True).then_inc(s["fold_ps"], 1)

                    def z_part(t):
                        i = t % 2
                        if t:
                            pe.wait_ge(s["q_sb"], t)
                        project_split(pe, PS, 3, wh[i][:, 1], wl[i][:, 1], G.hT_hi, G.hT_lo, [(0, 512), (512, 512)], at=CTX).then_inc(s["z_ps"], 1)
                        pe.wait_ge(s["xm_sb"], t + 1)
                        pe.wait_ge(s["fold_sb"], t + 1)
                        pe.wait_ge(s["bqk_sb"], t + 1)
                        if t:
                            pe.wait_ge(s["gate_sb"], t)
                        for c in range(NCH):
                            last = pe.matmul(PS[:, 5 + c // 4, (c % 4) * P:(c % 4 + 1) * P], xm[:, i, c * CH:(c + 1) * CH], BD[:, i, 2],
                                             start=True, stop=True)
                            if c in (3, 7, 9):
                                last.then_inc(s["v_ps"], 1)

                    def q_part(t):
                        i = t % 2
                        pe.wait_ge(s["xc_ok"], t + 1)
                        pe.wait_ge(s["z_sb"], t + 1)
                        for off in (0, 512):
                            last = pe.matmul(PS[:, 3 + off // 512, :], BQK[:, i], xc[:, i, CTX + off:CTX + off + 512], start=True, stop=True)
                        last.then_inc(s["q_ps"], 1)
                        pe.wait_ge(s["v_sb"], 3 * t + 3)
                        if t + 1 < TILES:
                            pe.wait_ge(s["fold_sb"], t + 2)
                            pe.wait_ge(s["bqk_sb"], t + 2)
                        for off, m in PIECES:
                            pe.matmul(PS[:, 5 + off // 512, 0:m], WG[:, i, 0], xc[:, i, off:off + m], start=True, stop=False)
                            last = pe.matmul(PS[:, 5 + off // 512, 0:m], WG[:, i, 1], xm[:, i, off:off + m], start=False, stop=True)
                        last.then_inc(s["gate_ps"], 1)

                    x_part(0)
                    z_part(0)
                    for t in range(TILES):
                        if t + 1 < TILES:
                            x_part(t + 1)
                        q_part(t)
                        if t + 1 < TILES:
                            z_part(t + 1)

                @block.scalar
                def _(act):
                    for t in range(TILES):
                        for j, n in enumerate(("ml_wq", "ml_wk", "ml_wv")):
                            act.dma_start(wqkv[:, t, j], A.p[n][0].rearrange("j c d -> (j c) d")[bass.ds(r * (TILES * P) + t * P, P)]).then_inc(s["small_in"], 16)
                        for j, n in enumerate(("ml_wi_f", "ml_wf_f", "ml_wi_b", "ml_wf_b")):
                            src = A.p[n][0].rearrange("(a r) h -> r a h", a=3)
                            act.dma_start(wg[:, t, :, j], src[bass.ds(r * (TILES * P) + t * P, P)]).then_inc(s["small_in"], 16)

                    def high(t):
                        act.wait_ge(w_in[t % 2], 32 * (t // 2 + 1))
                        if t >= 2:
                            act.wait_ge(s["z_ps"], t - 1)
                        act.activation(wh[t % 2][:], w[:, t % 2], ACT.Copy).then_inc(s["hi_ok"], 1)

                    def x_out(t):
                        i = t % 2
                        act.wait_ge(s["xm_ps"], t + 1)
                        if t:
                            act.wait_ge(s["conv_ok"], t)
                        act.activation(padl[:, 1:ROWS + 1, 1:GRID_W + 1], flat(PS, 0)[:, CTX:].rearrange("p (r w) -> p r w", w=GRID_W), ACT.Copy)
                        act.activation(padc[:, 1:CTX + 1], flat(PS, 0)[:, 0:CTX], ACT.Copy).then_inc(s["padded"], 1)
                        if t >= 2:
                            act.wait_ge(s["gate_ps"], t - 1)
                        act.activation(xm[:, i], flat(PS, 0), ACT.Copy).then_inc(s["xm_sb"], 1)

                    def turn(t):
                        act.wait_ge(s["bdt_ps"], t + 1)
                        act.activation(BDT[:, t % 2].rearrange("p a b -> p (a b)"), PS[:, 7, 0:3 * P], ACT.Copy).then_inc(s["bdt_sb"], 1)

                    high(0)
                    turn(0)
                    x_out(0)
                    for t in range(TILES):
                        i = t % 2
                        if t + 1 < TILES:
                            high(t + 1)
                        act.wait_ge(s["z_ps"], t + 1)
                        if t >= 2:
                            act.wait_ge(stored[i], t // 2 * 4 * 16)
                        act.activation(sz[:, i], flat(PS, 3)[:, 0:SEQ], ACT.Silu).then_inc(s["z_sb"], 1)
                        for j in range(3):
                            m = 4 if j < 2 else 2
                            act.wait_ge(s["v_ps"], 3 * t + j + 1)
                            act.activation(v[:, i, 4 * j:4 * j + m].rearrange("p c n -> p (c n)"), PS[:, 5 + j, 0:m * P], ACT.Copy).then_inc(s["v_sb"], 1)
                        if t + 1 < TILES:
                            turn(t + 1)
                        act.wait_ge(s["conv_ok"], t + 1)
                        act.activation(xc[:, i], acc, ACT.Silu).then_inc(s["xc_ok"], 1)
                        if t + 1 < TILES:
                            x_out(t + 1)
                        act.wait_ge(s["q_ps"], t + 1)
                        act.activation(q[:, i], flat(PS, 3)[:, 0:SEQ], ACT.Copy, scale=float(DH) ** -0.5).then_inc(s["q_sb"], 1)

                @block.gpsimd
                def _(pool):
                    for t in range(TILES):
                        pool.wait_ge(s["hi_ok"], t + 1)
                        if t >= 2:
                            pool.wait_ge(s["z_ps"], t - 1)
                        pool.tensor_tensor(wl[t % 2][:], w[:, t % 2], wh[t % 2][:].bitcast(F32), ALU.subtract).then_inc(s["lo_ok"], 1)

                @block.vector
                def _(dve):
                    step = Steps(dve, s["step"])

                    def maps(t):
                        if t >= 2:
                            dve.wait_ge(s["v_ps"], 3 * (t - 1))
                        for j in range(3):
                            last = dve.tensor_tensor(BD[:, t % 2, j].rearrange("p (a b) -> p a b", b=4), wqkv[:, t, j:j + 1, :].broadcast_to([P, 32, 4]),
                                                     G.c("block4").rearrange("p (a b) -> p a b", b=4), ALU.mult)
                        last.then_inc(s["bd_ok"], 1)

                    dve.wait_ge(s["small_in"], TILES * 7 * 16)
                    dve.wait_ge(s["cols_in"], 16)
                    def folds(t):
                        dve.wait_ge(s["fold_ps"], t + 1)
                        if t >= 2:
                            dve.wait_ge(s["gate_ps"], t - 1)
                        for j in range(2):
                            dst = WG[:, t % 2, j].rearrange("p (a b) -> p a b", b=32)[:, :, 0:4]
                            last = dve.tensor_copy(dst, PS[:, 7, 16 * j:16 * j + 16].rearrange("p (a b) -> p a b", b=4))
                        last.then_inc(s["fold_sb"], 1)
                        dve.tensor_copy(BQK[:, t % 2], PS[:, 7, P:2 * P]).then_inc(s["bqk_sb"], 1)

                    maps(0)
                    folds(0)
                    for t in range(TILES):
                        if t + 1 < TILES:
                            maps(t + 1)
                        dve.wait_ge(s["padded"], t + 1)
                        if t:
                            dve.wait_ge(s["xc_ok"], t)
                        col = [cols[:, t, j:j + 1] for j in range(TILE_PARAMS)]
                        lat = acc[:, CTX:].rearrange("p (r w) -> p r w", w=GRID_W)
                        step.add(dve.tensor_scalar(lat, padl[:, 0:ROWS, 0:GRID_W], col[0], col[9], ALU.mult, ALU.add))
                        step.link(dve.tensor_scalar(acc[:, 0:CTX], padc[:, 0:CTX], col[3], col[9], ALU.mult, ALU.add))
                        for tap in range(1, 9):
                            a, b = tap // 3, tap % 3
                            if tap in (4, 5):
                                step.add(dve.scalar_tensor_tensor(acc[:, 0:CTX], padc[:, b:b + CTX], col[tap], acc[:, 0:CTX], ALU.mult, ALU.add))
                            ins = dve.scalar_tensor_tensor(lat, padl[:, a:a + ROWS, b:b + GRID_W], col[tap], lat, ALU.mult, ALU.add)
                            if tap == 8:
                                ins.then_inc(s["conv_ok"], 1)
                            else:
                                step.link(ins)
                        if t + 1 < TILES:
                            folds(t + 1)
                        dve.wait_ge(s["gate_ps"], t + 1)
                        if t:
                            dve.wait_ge(s["gate_sb"], t)
                        dve.tensor_tensor(B.gates[:], flat(PS, 5), B.gates[:], ALU.add).then_inc(s["gate_sb"], 1)


def mlstm_gates(nc, A, G, B):
    with ExitStack() as ctx:
        def sb(n, s):
            return ctx.enter_context(nc.sbuf_tensor(n, s, F32))
        bias = sb("gate_bias", [P, 1])
        x, l = sb("gate_x", [P, T]), sb("gate_l", [P, T])
        F_, a, M, m = [sb(n, [P, T]) for n in ("gate_F", "gate_a", "gate_M", "gate_m")]
        unit = sb("unit", [P, T])
        colsb = sb("gate_cols", [P, 2, NCH, HEADS1, 2])
        PS = G.PS
        with phase(nc, "zero bias_in x_ok l_ok step rows_ok turned0 turned1 cols_ok stored act_step") as (block, s):
            @block.sync
            def _(sp):
                sp.wait_ge(s["zero"], 1)
                for j, n in enumerate(("ml_bi_f", "ml_bf_f", "ml_bi_b", "ml_bf_b")):
                    sp.dma_start(bias[32 * j:32 * j + 4], A.p[n][0].rearrange("(p o) -> p o", o=1)).then_inc(s["bias_in"], 16)
                sp.wait_ge(s["rows_ok"], 1)
                for d in range(2):
                    sp.dma_start(B.M_d[:, d], M[64 * d:64 * d + 4, CTX:]).then_inc(s["stored"], 16)
                sp.wait_ge(s["cols_ok"], 2)
                for h in range(HEADS1):
                    sp.dma_start(B.cols_d[h], colsb[:, :, :, h]).then_inc(s["stored"], 16)
                sp.wait_ge(s["stored"], 6 * 16)

            @block.scalar
            def _(act):
                step = Steps(act, s["act_step"])
                act.wait_ge(s["x_ok"], 1)
                step.link(act.activation(l[:], x[:], ACT.Abs))
                step.link(act.activation(l[:], l[:], ACT.Exp, scale=-1.0))
                act.activation(l[:], l[:], ACT.Ln, bias=G.c("ones")[:, 0:1]).then_inc(s["l_ok"], 1)

            @block.vector
            def _(dve):
                step = Steps(dve, s["step"])
                dve.memset(bias[:], 0.0).then_inc(s["zero"], 1)
                step.add(dve.memset(unit[:], 1.0))
                step.add(dve.memset(a[:], 0.0))
                step.add(dve.memset(M[:], 0.0))
                step.add(dve.memset(m[:], 0.0))
                step.link(dve.memset(F_[:], 0.0))
                dve.wait_ge(s["bias_in"], 64)
                step.publish(dve.tensor_scalar(x[:], B.gates[:], bias[:], None, ALU.add), s["x_ok"], 1)
                dve.wait_ge(s["l_ok"], 1)
                step.link(dve.scalar_tensor_tensor(l[:], x[:], 0.0, l[:], ALU.min, ALU.subtract))
                for d in range(2):
                    r, f = slice(64 * d, 64 * d + 4), slice(64 * d + 32, 64 * d + 36)

                    def scan(out, in0, in1, first, op0, op1):
                        for lo, hi, prev in ((0, CTX, None), (CTX, T, CTX - 1 if d == 0 else 0)):
                            ini = first if prev is None else out[:, prev:prev + 1]
                            v = [z[:, lo:hi] if d == 0 else z[:, lo:hi][:, ::-1] for z in (out, in0, in1)]
                            step.link(dve.tensor_tensor_scan(v[0], v[1], v[2], ini, op0, op1))

                    step.link(dve.tensor_copy(m[r], l[f]))
                    scan(F_[r], unit[r], m[r], 0.0, ALU.mult, ALU.add)
                    step.link(dve.tensor_tensor(a[r], x[r], F_[r], ALU.subtract))
                    scan(M[r], a[r], a[r], -3e38, ALU.max, ALU.max)
                    step.link(dve.scalar_tensor_tensor(m[r], F_[r], -1.0, M[r], ALU.mult, ALU.subtract))
                step.publish(dve.tensor_scalar(M[:], M[:], -1.0, None, ALU.mult), s["rows_ok"], 1)
                for j, t in enumerate((s["turned0"], s["turned1"])):
                    for n in range(3):
                        cnt = min(4, NCH - 4 * n)
                        dve.wait_ge(t, n + 1)
                        for d in range(2):
                            src = PS[:, 4 * j + n, 0:cnt * P].rearrange("p (c r) -> p c r", r=P)[:, :, 64 * d:64 * d + 4]
                            last = dve.tensor_copy(colsb[:, d, 4 * n:4 * n + cnt, :, j], src)
                    last.then_inc(s["cols_ok"], 1)

            @block.tensor
            def _(pe):
                pe.wait_ge(s["rows_ok"], 1)
                for j, (src, t) in enumerate(((a, s["turned0"]), (m, s["turned1"]))):
                    for n in range(3):
                        for c in range(4 * n, min(4 * n + 4, NCH)):
                            last = pe.transpose(PS[:, 4 * j + n, (c % 4) * P:(c % 4 + 1) * P], src[:, c * CH:(c + 1) * CH], G.c("ident"))
                        last.then_inc(t, 1)


TQ = SEQ // P
VCOL = [0, P, 2 * P + 1, 3 * P + 1]


def mlstm_heads(nc, A, G, B):
    def uses(d, c):
        return [j for j in range(NCH) if j < CTXCH or (j <= c if d == 0 else j >= c)]

    groups = [(0, 4), (4, 4), (8, 2)]
    with ExitStack() as ctx:
        def sb(n, s):
            return ctx.enter_context(nc.sbuf_tensor(n, s, F32))
        Q, K = sb("Q", [P, 4, SEQ]), sb("K1", [P, 4, T])
        V = sb("V1", [P, NCH, 4 * P + 1])
        cols, pcol = sb("head_cols", [P, 2, NCH, 2]), sb("head_params", [P, 4, TILE_PARAMS])
        Mrow = sb("M_row", [P, 2, SEQ])
        sx, sz = sb("sx_in", [P, 4, SEQ]), sb("sz_in", [P, 4, SEQ])
        W = sb("weights", [P, 2, 2, NCH, P])
        dg = sb("diag_arg", [P, 2, 2, P])
        H = sb("H", [P, TQ, DH])
        floor = sb("floor", [P, 2, NCH])
        den = sb("den", [P, 2, 2])
        st, mv, rs = sb("h_stats", [P, 2, 6]), sb("h_mv", [P, TQ, 2]), sb("h_rstd", [P, 2, TQ])
        eps = sb("eps_h", [P, 1])
        PS = G.PS
        with phase(nc, "ones_ok") as (block, s):
            @block.vector
            def _(dve):
                dve.memset(V[:, :, 2 * P:2 * P + 1], 1.0)
                dve.memset(eps[:], EPS_LN).then_inc(s["ones_ok"], 1)
        with nc.Fori(0, HEADS1) as h:
            sems = ("qk_in v_in row_in skip_in scored weighted d_ok diag_ok floor_ok av_ps av_sb mean_ok root normed "
                    "turned y_half y_ok step stored taken")
            with phase(nc, sems) as (block, s):
                @block.sync
                def _(sp):
                    sp.dma_start(Mrow[:].rearrange("p d t -> p (d t)"),
                                   B.M_d[bass.ds(h, 1)].rearrange("o d t -> o (d t)").broadcast_to([P, 2 * SEQ])).then_inc(s["row_in"], 16)
                    sp.dma_start(cols[:], B.cols_d[bass.ds(h, 1)].rearrange("o p d c j -> p (o d) c j")).then_inc(s["row_in"], 16)
                    for kt in range(4):
                        sp.dma_start(K[:, kt], B.k_d[bass.ds(h * 4 + kt, 1)].rearrange("o p t -> p (o t)")).then_inc(s["qk_in"], 16)
                        sp.dma_start(Q[:, kt], B.q_d[bass.ds(h * 4 + kt, 1)].rearrange("o p t -> p (o t)")).then_inc(s["qk_in"], 16)
                    for kt in range(4):
                        sp.dma_start(V[:, :, VCOL[kt]:VCOL[kt] + P], B.v_d[bass.ds(h * 4 + kt, 1)].rearrange("o p c n -> p (o c) n")).then_inc(s["v_in"], 16)
                    sp.dma_start(sz[:], B.sz_d[bass.ds(h * 4, 4)].rearrange("k p t -> p k t")).then_inc(s["skip_in"], 16)
                    sp.dma_start(pcol[:], A.cols1_d[bass.ds(h * 4, 4)].rearrange("k p j -> p k j")).then_inc(s["skip_in"], 16)
                    for kt in range(4):
                        sp.wait_ge(s["y_ok"], kt + 1)
                        sp.dma_start(B.y_d[bass.ds(h * 4 + kt, 1)].rearrange("o p t -> p (o t)"), sx[:, kt]).then_inc(s["stored"], 16)
                    sp.wait_ge(s["stored"], 64)

                @block.tensor
                def _(pe):
                    def scores(i):
                        for g, (j0, m) in enumerate(groups):
                            n = 3 * i + g
                            if n >= 4:
                                pe.wait_ge(s["weighted"], n - 3)
                            for j in range(j0, j0 + m):
                                for kt in range(4):
                                    last = pe.matmul(PS[:, 4 + n % 4, (j - j0) * P:(j - j0 + 1) * P], K[:, kt, j * P:(j + 1) * P],
                                                     Q[:, kt, i * P:(i + 1) * P], start=(kt == 0), stop=(kt == 3))
                            last.then_inc(s["scored"], 1)

                    pe.wait_ge(s["qk_in"], 128)
                    scores(0)
                    pe.wait_ge(s["v_in"], 64)
                    for i in range(TQ):
                        if i + 1 < TQ:
                            scores(i + 1)
                        pe.wait_ge(s["weighted"], 3 * i + 3)
                        if i:
                            pe.wait_ge(s["av_sb"], i)
                        for d in range(2):
                            seen = uses(d, i + CTXCH)
                            for j in seen:
                                for half in range(2):
                                    v = V[:, j, 0:2 * P + 1] if half == 0 else V[:, j, 2 * P + 1:4 * P + 1]
                                    last = pe.matmul(PS[:, 2 * d + half, 0:v.shape[1]], W[:, i % 2, d, j], v,
                                                     start=(j == seen[0]), stop=(j == seen[-1]))
                        last.then_inc(s["av_ps"], 1)
                    for kt in range(4):
                        pe.wait_ge(s["normed"], TQ)
                        if kt >= 2:
                            pe.wait_ge(s["y_half"], kt - 1)
                        for i in range(TQ):
                            last = pe.transpose(PS[:, 4 + 2 * (kt % 2) + i // 4, (i % 4) * P:(i % 4 + 1) * P], H[:, i, kt * P:(kt + 1) * P], G.c("ident"))
                        last.then_inc(s["turned"], 1)

                @block.scalar
                def _(act):
                    act.wait_ge(s["row_in"], 32)
                    act.activation(floor[:], cols[:, :, :, 1], ACT.Exp).then_inc(s["floor_ok"], 1)
                    for i in range(TQ):
                        c = i + CTXCH
                        if i >= 2:
                            act.wait_ge(s["av_ps"], i - 1)
                        act.wait_ge(s["diag_ok"], 2 * i + 2)
                        for d in range(2):
                            for j in uses(d, c):
                                arg = dg[:, i % 2, d] if j == c else Mrow[:, d, i * P:(i + 1) * P]
                                last = act.activation(W[:, i % 2, d, j], arg, ACT.Exp, bias=cols[:, d, j, 0:1])
                        last.then_inc(s["d_ok"], 1)
                    act.wait_ge(s["mean_ok"], TQ)
                    act.activation(rs[:, 0], mv[:, :, 1], ACT.Sqrt, bias=eps[:]).then_inc(s["root"], 1)

                @block.vector
                def _(dve):
                    step = Steps(dve, s["step"])

                    def diag(i):
                        if i >= 2:
                            dve.wait_ge(s["d_ok"], i - 1)
                        for d in range(2):
                            dve.tensor_tensor(dg[:, i % 2, d], G.c("neg")[:, d * P:(d + 1) * P], Mrow[:, d, i * P:(i + 1) * P],
                                              ALU.add).then_inc(s["diag_ok"], 1)

                    dve.wait_ge(s["row_in"], 32)
                    dve.wait_ge(s["floor_ok"], 1)
                    diag(0)
                    for i in range(TQ):
                        c = i + CTXCH
                        if i + 1 < TQ:
                            diag(i + 1)
                        dve.wait_ge(s["d_ok"], i + 1)
                        for g, (j0, m) in enumerate(groups):
                            n = 3 * i + g
                            dve.wait_ge(s["scored"], n + 1)
                            for d in range(2):
                                js = [j for j in uses(d, c) if j0 <= j < j0 + m]
                                runs = []
                                for j in js:
                                    if runs and runs[-1][1] == j:
                                        runs[-1][1] = j + 1
                                    else:
                                        runs.append([j, j + 1])
                                for a, b in runs:
                                    w = W[:, i % 2, d, a:b]
                                    last = dve.tensor_tensor(w, PS[:, 4 + n % 4, (a - j0) * P:(b - j0) * P].rearrange("p (j t) -> p j t", t=P), w, ALU.mult)
                            last.then_inc(s["weighted"], 1)
                        dve.wait_ge(s["av_ps"], i + 1)
                        for d in range(2):
                            step.add(dve.scalar_tensor_tensor(den[:, d, 0:1], PS[:, 2 * d, 2 * P:2 * P + 1], -1.0, floor[:, d, c:c + 1],
                                                              ALU.mult, ALU.max))
                        step.wait()
                        for d in range(2):
                            step.add(dve.tensor_tensor(den[:, d, 0:1], PS[:, 2 * d, 2 * P:2 * P + 1], den[:, d, 0:1], ALU.max))
                        step.wait()
                        for d in range(2):
                            step.add(dve.reciprocal(den[:, d, 1:2], den[:, d, 0:1]))
                        step.wait()
                        for half in range(2):
                            step.add(dve.tensor_scalar(H[:, i, 2 * P * half:2 * P * half + 2 * P], PS[:, half, 0:2 * P], den[:, 0, 1:2], None, ALU.mult))
                        step.wait()
                        for half in range(2):
                            hh = H[:, i, 2 * P * half:2 * P * half + 2 * P]
                            ins = dve.scalar_tensor_tensor(hh, PS[:, 2 + half, 0:2 * P], den[:, 1, 1:2], hh, ALU.mult, ALU.add)
                            if half:
                                step.publish(ins, s["av_sb"], i + 1)
                            else:
                                step.add(ins)
                        step.link(dve.bn_stats(st[:, i % 2], H[:, i]))
                        dve.bn_aggr(mv[:, i], st[:, i % 2]).then_inc(s["mean_ok"], 1)
                    dve.wait_ge(s["root"], 1)
                    step.link(dve.reciprocal(rs[:, 0], rs[:, 0]))
                    step.link(dve.scalar_tensor_tensor(rs[:, 1], mv[:, :, 0], -1.0, rs[:, 0], ALU.mult, ALU.mult))
                    for i in range(TQ):
                        dve.tensor_scalar(H[:, i], H[:, i], rs[:, 0, i:i + 1], rs[:, 1, i:i + 1], ALU.mult, ALU.add).then_inc(s["normed"], 1)
                    dve.wait_ge(s["skip_in"], 32)
                    for kt in range(4):
                        step.add(dve.tensor_scalar(sx[:, kt], K[:, kt, CTX:], pcol[:, kt, 11:12], None, ALU.mult))
                    step.wait()
                    for kt in range(4):
                        dve.wait_ge(s["turned"], kt + 1)
                        b = 4 + 2 * (kt % 2)
                        step.publish(dve.scalar_tensor_tensor(sx[:, kt], PS[:, b:b + 2, :].rearrange("p a b -> p (a b)"), pcol[:, kt, 10:11], sx[:, kt],
                                                              ALU.mult, ALU.add), s["y_half"], kt + 1)
                        dve.tensor_tensor(sx[:, kt], sx[:, kt], sz[:, kt], ALU.mult).then_inc(s["y_ok"], 1)


def build(nc, inputs, out):
    A = Names()
    A.p = inputs
    A.x, A.ctx, A.mod_w, A.consts = inputs["x"], inputs["ctx"], inputs["mod_w"], inputs["consts"]

    def scratch(name, shape):
        return nc.dram_tensor(name, shape, F32, kind="Internal").ap()

    A.gates_d = scratch("gates_d", (3, P, D))
    A.cols0_d = scratch("cols0_d", (4, P, NPAIR))
    A.cols1_d = scratch("cols1_d", (NT1, P, TILE_PARAMS))
    A.lg_d = scratch("lg_d", (32, T))
    A.yT_d = scratch("yT_d", (KT, P, T))
    A.x1_d = scratch("x1_d", (NCH, P, D))
    at, ends = const_layout()
    with ExitStack() as ctx:
        def sb(n, s):
            return ctx.enter_context(nc.sbuf_tensor(n, s, F32))
        G = Names()
        G.PS = ctx.enter_context(nc.psum_tensor("PS", [P, 8, 512], F32))
        G.ends = ends
        G.cst = sb("cst", [P, ends[0]])

        def const(name):
            a, b = at[name]
            if b <= ends[0]:
                return G.cst[:, a:b]
            if b <= ends[1]:
                return G.cst0[:, a - ends[0]:b - ends[0]]
            return G.cst_rwkv[:, a - ends[1]:b - ends[1]]

        G.c = const
        G.vc = sb("vc", [P, P])
        G.modc = sb("modc", [P, 2, 16, 2])
        setup_phase(nc, A, G)
        B = Names()
        with nc.sbuf_tensor("hT", [P, KT, T], F32) as hT:
            G.hT = hT
            with nc.sbuf_tensor("xnat", [P, NCH, D], F32) as xnat:
                modulate_phase(nc, A, G, 0, xnat, hT, True)
            with nc.sbuf_tensor("cst0", [P, ends[1] - ends[0]], F32) as G.cst0:
                layer0(nc, A, G)
        with ExitStack() as c1:
            xnew = c1.enter_context(nc.sbuf_tensor("xnew", [P, NCH, D], F32))

            def x_of(t):
                return (A.ctx if t < CTXCH else A.x)[0, (t % CTXCH if t < CTXCH else t - CTXCH) * P:][:P]
            out_phase(nc, A, G, 0, A.yT_d, A.p["e_w_out"][0], KT, list(range(NCH)), x_of, xnew, lambda t: A.x1_d[t])
            G.hT_hi, G.hT_lo = (c1.enter_context(nc.sbuf_tensor(n, [P, KT, T], F32R)) for n in ("hT_hi", "hT_lo"))
            modulate_split(nc, G, 1, xnew, G.hT_hi, G.hT_lo)
            B.xnew = xnew
            layer1_inputs(nc, A, G, B, scratch)
        mlstm_heads(nc, A, G, B)
        with nc.sbuf_tensor("xlast", [P, 2, D], F32) as xlast:
            out_phase(nc, A, G, 1, B.y_d, A.p["o_w_out"][0], NT1, list(range(CTXCH, NCH)), lambda t: A.x1_d[t], xlast,
                      lambda t: out[0, (t - CTXCH) * P:(t - CTXCH + 1) * P, :])


def layer1_inputs(nc, A, G, B, scratch):
    B.q_d, B.k_d = scratch("q_d", (NT1, P, SEQ)), scratch("k_d", (NT1, P, T))
    B.v_d = scratch("v_d", (NT1, P, NCH, P))
    B.sz_d = scratch("sz_d", (NT1, P, SEQ))
    B.y_d = scratch("y1_d", (NT1, P, SEQ))
    B.M_d, B.cols_d = scratch("M_d", (HEADS1, 2, SEQ)), scratch("hcols_d", (HEADS1, P, 2, NCH, 2))
    with nc.sbuf_tensor("gates1", [P, T], F32) as gates:
        B.gates = gates
        mlstm_inputs(nc, A, G, B)
        mlstm_gates(nc, A, G, B)


def layer0(nc, A, G):
    with ExitStack() as c2:
        def sb2(n, s):
            return c2.enter_context(nc.sbuf_tensor(n, s, F32))
        B = Names()
        G.cst_rwkv = sb2("cst_rwkv", [P, G.ends[2] - G.ends[1]])
        B.LW, B.LA = sb2("LW", [P, T]), sb2("LA", [P, T])
        lowrank_phase(nc, A, G, B.LW, B.LA)
        with ExitStack() as c3:
            def sb3(n, s):
                return c3.enter_context(nc.sbuf_tensor(n, s, F32))
            B.cols = sb3("pair_cols", [P, NPAIR])
            B.rt, B.at, B.bt, B.kt = (sb3(n, [P, 2, T]) for n in ("rt", "at", "bt", "kt"))
            B.V, B.sG, B.bonus = (sb3(n, [P, T]) for n in ("V", "sG", "bonus"))
            B.PL = sb3("PL", [P, 2, NCH])
            with nc.Fori(0, 4) as p:
                rwkv_prep(nc, A, G, B, p)
                with ExitStack() as c4:
                    def sb4(n, s):
                        return c4.enter_context(nc.sbuf_tensor(n, s, F32))
                    B.QT = sb4("QT", [P, NCH, 2, P])
                    B.GT, B.HS = sb4("GT", [P, NCH, 2, 64]), sb4("HS", [P, NCH, 2, 64])
                    B.Y = sb4("Y_rwkv", [P, T])
                    rwkv_chunks(nc, A, G, B)
                    rwkv_finish(nc, A, G, B, p)
    with ExitStack() as c2:
        def sb2(n, s):
            return c2.enter_context(nc.sbuf_tensor(n, s, F32))
        B = Names()
        B.q, B.k = sb2("gla_q", [P, 2, T]), sb2("gla_k", [P, 2, T])
        B.b, B.qd, B.sG = sb2("gla_b", [P, 2, T]), sb2("gla_qd", [P, 2, T]), sb2("gla_sG", [P, 2, T])
        B.V = sb2("gla_V", [P, NCH, 2 * P])
        B.KN, B.A = sb2("gla_KN", [P, 2, NCH, P]), sb2("gla_A", [P, NCH, 2, P])
        B.tot = sb2("gla_tot", [P, 2, NCH])
        with nc.Fori(0, 2) as g:
            gla_prep(nc, A, G, B, g)
            gla_scores(nc, A, G, B)
            gla_out(nc, A, G, B, g)


_INS = ['x', 'c', 'ctx', 'c_ctx', 'mod_w', 'mod_b', 'ln_g', 'ln_b', 'e_w_in', 'e_w_out', 'gla_wa2_f',
        'gla_ba_f', 'gla_wa2_b', 'gla_ba_b', 'gla_norm_g', 'rwkv_mu', 'rwkv_w0_f', 'rwkv_ww2_f',
        'rwkv_w0_b', 'rwkv_ww2_b', 'rwkv_a0_f', 'rwkv_wa2_f', 'rwkv_a0_b', 'rwkv_wa2_b', 'rwkv_k_k',
        'rwkv_k_a', 'rwkv_r_k', 'rwkv_gn_g', 'rwkv_gn_b', 'o_w_in', 'o_w_out', 'ml_conv_w', 'ml_conv_b',
        'ml_wq', 'ml_wk', 'ml_wv', 'ml_wi_f', 'ml_bi_f', 'ml_wf_f', 'ml_bf_f', 'ml_wi_b', 'ml_bi_b',
        'ml_wf_b', 'ml_bf_b', 'ml_norm_g', 'ml_skip']


def kernel(**inputs):
    import concourse.bacc as bacc
    from concourse.bass_utils import run_bass_kernel_spmd

    nc = bacc.Bacc("TRN2", target_bir_lowering=False, num_devices=1)
    arrays, args = {}, {}
    for name in _INS + ["consts"]:
        a = np.concatenate(list(constants().values()), 1) if name == "consts" else inputs[name]
        a = np.ascontiguousarray(a)
        arrays[f"in_{name}_dram"] = a
        args[name] = nc.dram_tensor(f"in_{name}_dram", a.shape, mybir.dt.from_np(a.dtype), kind="ExternalInput").ap()
    out = nc.dram_tensor("out_0_dram", (1, SEQ, D), F32, kind="ExternalOutput").ap()
    build(nc, args, out)
    r = run_bass_kernel_spmd(nc, [arrays], core_ids=[0])
    return r.results[0]["out_0_dram"]
```

```python
from contextlib import ExitStack, contextmanager

import numpy as np
import concourse.bass as bass
from concourse import mybir

F32 = mybir.dt.float32
F32R = mybir.dt.float32r
I32 = mybir.dt.int32
ALU = mybir.AluOpType
ACT = mybir.ActivationFunctionType

P = 128
D = 1024
CTX = 256
SEQ = 1024
T = CTX + SEQ
KT = D // P
GRID_W = 64
ROWS = SEQ // GRID_W
CH = 128
NCH = T // CH
CTXCH = CTX // CH
PIECES = [(0, 512), (512, 512), (1024, 256)]
EPS_LN = 1e-5
EPS_GN = 64e-5
DEC = 0.6065306597
HALF = DEC * CH / 2
ALPHA = 4.0 ** 0.25
BIG = 1e30
GQ, GK, GV, GG, GLR = 0, 256, 512, 1024, 1536
RR, RK, RV, RG, RWL, RAL = 1568, 2080, 2592, 3104, 3616, 3744
E_IN = 3872
INNER = 2048
NT1 = INNER // P
HEADS1 = 4
DH = 512
ORDER = [list(range(NCH)), list(range(CTXCH - 1, -1, -1)) + list(range(NCH - 1, CTXCH - 1, -1))]

LEVELS = [1, 2, 4, 8, 16, 32, 64]


def constants():
    p = np.arange(P)[:, None]
    f = np.arange(P)[None, :]
    one = np.float32

    def lr(b):
        return ((p // (2 * b) == f // (2 * b)) & (p % (2 * b) < b) & (f % (2 * b) >= b)).astype(one)

    c = {"ident": np.eye(P, dtype=one), "ones": np.ones((P, P), one)}
    c["side"] = ((p % 4) == np.arange(4)[None]).astype(one)
    c["neg"] = np.concatenate([np.where(f >= p, 0, -BIG), np.where(f <= p, 0, -BIG)], 1).astype(one)
    c["pick"] = np.concatenate([np.broadcast_to(p == 0, (P, P)), np.broadcast_to(p == 1, (P, P))], 1).astype(one)
    c["block4"] = ((p // 4) == (f // 4)).astype(one)
    for b in LEVELS:
        c[f"parted{b}"] = lr(b) + lr(b).T
    c["keep"] = np.broadcast_to((np.arange(T) % CH != 0).astype(one), (P, T))
    for b in LEVELS:
        m = [lr(b).T, lr(b).T, lr(b), lr(b)]
        c[f"level{b}"] = np.concatenate(m if b > 1 else m[::-1], 1)
    c["score"] = np.concatenate([(f > p), (f >= p), (f < p), (f <= p)], 1).astype(one)
    c["heads"] = ((p // 64) == (f // 64)).astype(one)
    c["eye64"] = ((p % 64) == np.arange(64)[None]).astype(one)
    return c


def const_layout():
    at, n = {}, 0
    for k, v in constants().items():
        at[k] = (n, n + v.shape[1])
        n += v.shape[1]
    return at, [at["parted1"][0], at["level1"][0], n]


class Names:
    pass


def fresh(G, name):
    G.count += 1
    return f"{name}_{G.count}"


@contextmanager
def phase(nc, names):
    with ExitStack() as ctx:
        handles = [ctx.enter_context(nc.semaphore(n)) for n in names.split()]
        with nc.Block() as block:
            yield block, dict(zip(names.split(), handles))
        for h in handles:
            nc.sync.sem_clear(h)
        nc.all_engine_barrier(sem_only=True)


class Steps:

    def __init__(self, eng, sem):
        self.eng, self.sem, self.n = eng, sem, 0

    def add(self, ins):
        ins.then_inc(self.sem, 1)
        self.n += 1
        return ins

    def wait(self):
        self.eng.wait_ge(self.sem, self.n)

    def publish(self, ins, sem, value):
        ins.then_inc(sem, 1)
        self.eng.wait_ge(sem, value)

    def link(self, ins):
        self.add(ins)
        self.wait()


def after(names, name):
    return names.index(name) + 1


PAIR_PARAMS = [("rwkv_mu", 0), ("rwkv_mu", 512), ("rwkv_mu", 1024), ("rwkv_mu", 1536), ("rwkv_w0_f", 0),
               ("rwkv_w0_b", 0), ("rwkv_a0_f", 0), ("rwkv_a0_b", 0), ("rwkv_k_k", 0), ("rwkv_k_a", 0),
               ("rwkv_r_k", 0), ("rwkv_gn_g", 0), ("rwkv_gn_b", 0)]
NPAIR = len(PAIR_PARAMS)
(J_MU, J_W0, J_A0, J_KK, J_KA, J_RK, J_GG, J_GB) = (0, 4, 6, 8, 9, 10, 11, 12)
V_MULR = 4 * NPAIR
V_GBA = V_MULR + 2
V_GNG = V_GBA + 4
V_C = V_GNG + 1
TILE_PARAMS = 12


def setup_phase(nc, A, G, xnat, w_lr):
    with ExitStack() as ctx:
        def sb(n, s):
            return ctx.enter_context(nc.sbuf_tensor(n, s, F32))
        rows = sb("param_rows", [P, 3, P])
        c_rows = sb("cond_rows", [16, P])
        modw = sb("modw", [P, 4, 3 * D])
        modb = sb("modb", [2, 2, 3 * D])
        modrow = sb("modrow", [2, 2, 3 * D])
        cond = sb("cond", [P, 2, KT])
        gate = sb("gate", [P, 3, D])
        cols1 = sb("cols1", [P, 2, P])
        PS = G.PS
        sems = "consts x_in c_in c_ps rows_in modb_in w0 w1 w2 w3 cols cols_sb cond_sb mod_ps mod_row vec_ps vec_sb gate_ps gate_sb step stored"
        with phase(nc, sems) as (block, s):
            ring = [s["w0"], s["w1"], s["w2"], s["w3"]]

            @block.sync
            def _(sp):
                sp.dma_start(G.cst[:], A.consts[:, 0:G.ends[0]]).then_inc(s["consts"], 16)
                for l in range(2):
                    for k in range(KT):
                        n = l * KT + k
                        if n >= 4:
                            sp.wait_ge(s["mod_ps"], n - 3)
                        sp.dma_start(modw[:, n % 4], A.mod_w[l, k * P:(k + 1) * P, :]).then_inc(ring[n % 4], 16)
                        if n == KT + 3:
                            sp.dma_start(xnat[:, 0:CTXCH, :], A.ctx[0].rearrange("(c p) d -> p c d", p=P)).then_inc(s["x_in"], 16)
                            sp.dma_start(xnat[:, CTXCH:NCH, :], A.x[0].rearrange("(c p) d -> p c d", p=P)).then_inc(s["x_in"], 16)
                            v = A.p["e_w_in"][0].rearrange("(k p) n -> p k n", p=P)
                            sp.dma_start(w_lr[:, :, 0:32], v[:, :, GLR:GLR + 32]).then_inc(s["x_in"], 16)
                            sp.dma_start(w_lr[:, :, 32:288], v[:, :, RWL:RWL + 256]).then_inc(s["x_in"], 16)
                sp.wait_ge(s["gate_sb"], 6)
                sp.dma_start(A.gates_d.rearrange("g p n -> p g n"), gate[:]).then_inc(s["stored"], 16)
                sp.wait_ge(s["cols_sb"], 3)
                for h in range(2):
                    sp.dma_start(A.cols1_d[8 * h:8 * h + 8].rearrange("i p j -> p i j"),
                                 cols1[:, h, 0:8 * TILE_PARAMS].rearrange("p (i j) -> p i j", i=8)).then_inc(s["stored"], 16)
                sp.dma_start(A.cols0_d.rearrange("i p j -> p i j"),
                             G.vc[:, 0:V_MULR].rearrange("p (i j) -> p i j", i=4)).then_inc(s["stored"], 16)
                sp.wait_ge(s["stored"], 4 * 16)
                sp.wait_ge(s["x_in"], 4 * 16)

            @block.scalar
            def _(act):
                act.dma_start(c_rows[0:8, :], A.p["c"][0].rearrange("(i n) -> i n", n=P)).then_inc(s["c_in"], 16)
                act.dma_start(c_rows[8:16, :], A.p["c_ctx"].rearrange("(i n) -> i n", n=P)).then_inc(s["c_in"], 16)
                act.wait_ge(s["c_ps"], 1)
                act.activation(cond[:], PS[:, 6, 0:16].rearrange("p (w k) -> p w k", w=2), ACT.Silu).then_inc(s["cond_sb"], 1)
                for j, (name, at) in enumerate(PAIR_PARAMS):
                    act.dma_start(rows[j:j + 3 * NPAIR + 1:NPAIR, 0, :],
                                  A.p[name][0, at:at + 512].rearrange("(i n) -> i n", n=P)).then_inc(s["rows_in"], 16)
                act.dma_start(rows[V_MULR:V_MULR + 2, 0, :],
                              A.p["rwkv_mu"][0, 2048:2304].rearrange("(i n) -> i n", n=P)).then_inc(s["rows_in"], 16)
                for d, name in enumerate(("gla_ba_f", "gla_ba_b")):
                    act.dma_start(rows[V_GBA + 2 * d:V_GBA + 2 * d + 2, 0, :],
                                  A.p[name][0].rearrange("(i n) -> i n", n=P)).then_inc(s["rows_in"], 16)
                act.dma_start(rows[V_GNG:V_GNG + 1, 0, :], A.p["gla_norm_g"]).then_inc(s["rows_in"], 16)
                one = [A.p["ml_conv_w"][0, t // 3, t % 3, 0] for t in range(9)] + \
                    [A.p[n][0] for n in ("ml_conv_b", "ml_norm_g", "ml_skip")]
                for j, v in enumerate(one):
                    v = v.rearrange("(h i n) -> h i n", h=2, n=P)
                    for h in range(2):
                        act.dma_start(rows[j:j + 7 * TILE_PARAMS + 1:TILE_PARAMS, 1 + h, :], v[h]).then_inc(s["rows_in"], 16)
                for i in range(2):
                    act.dma_start(modb[i:i + 1], A.p["mod_b"].rearrange("(o l) n -> o l n", o=1)).then_inc(s["modb_in"], 16)

            n_rows = NPAIR + 1 + 2 + 1 + 2 * TILE_PARAMS

            @block.tensor
            def _(pe):
                pe.wait_ge(s["consts"], 16)
                pe.wait_ge(s["c_in"], 32)
                pe.transpose(PS[:, 6, 0:16], c_rows[:], G.c("ident")[0:16, 0:16]).then_inc(s["c_ps"], 1)
                pe.wait_ge(s["cond_sb"], 1)
                for l in range(2):
                    for k in range(KT):
                        n = l * KT + k
                        pe.wait_ge(ring[n % 4], 16 * (n // 4 + 1))
                        if k == 0 and l:
                            pe.wait_ge(s["mod_row"], 1)
                        for j in range(6):
                            last = pe.matmul(PS[0:2, j, :], cond[:, :, k], modw[:, n % 4, 512 * j:512 * j + 512],
                                             start=(k == 0), stop=(k == KT - 1))
                        last.then_inc(s["mod_ps"], 1)
                    if l == 0:
                        pe.wait_ge(s["rows_in"], 16 * n_rows)
                        pe.transpose(PS[:, 7, 0:V_C], rows[0:V_C, 0, :], G.c("ident")[0:V_C, 0:V_C])
                        m = 8 * TILE_PARAMS
                        for h in range(2):
                            last = pe.transpose(PS[:, 7, P * (h + 1):P * (h + 1) + m], rows[0:m, 1 + h, :], G.c("ident")[0:m, 0:m])
                        last.then_inc(s["cols"], 1)
                        pe.wait_ge(s["cols_sb"], 3)
                    pe.wait_ge(s["mod_row"], 2 * l + 2)
                    if l:
                        pe.wait_ge(s["vec_sb"], l)
                    for t in range(16):
                        last = pe.transpose(PS[:, 7, 2 * t:2 * t + 2], modrow[:, l, t * P:(t + 1) * P], G.c("ident")[0:2, 0:2])
                    last.then_inc(s["vec_ps"], 1)
                    for w in range(2 - l):
                        for h in range(2):
                            n = 4 * l + 2 * w + h
                            if n:
                                pe.wait_ge(s["gate_sb"], n)
                            pe.matmul(PS[:, 6, :], G.c("pick")[0:2, w * P:(w + 1) * P],
                                      modrow[:, l, 2 * D + 512 * h:2 * D + 512 * h + 512],
                                      start=True, stop=True).then_inc(s["gate_ps"], 1)

            @block.vector
            def _(dve):
                dve.wait_ge(s["modb_in"], 32)
                for l in range(2):
                    dve.wait_ge(s["mod_ps"], KT * (l + 1))
                    dve.tensor_tensor(modrow[:, l, :], PS[0:2, 0:6, :].rearrange("p a b -> p (a b)"), modb[:, l, :],
                                      ALU.add).then_inc(s["mod_row"], 1)
                    dve.wait_ge(s["mod_row"], 2 * l + 1)
                    dve.tensor_scalar(modrow[:, l, D:2 * D], modrow[:, l, D:2 * D], 1.0, None, ALU.add).then_inc(s["mod_row"], 1)
                    if l == 0:
                        dve.wait_ge(s["cols"], 1)
                        dve.tensor_copy(G.vc[:, 0:V_C], PS[:, 7, 0:V_C]).then_inc(s["cols_sb"], 1)
                        m = 8 * TILE_PARAMS
                        for h in range(2):
                            dve.tensor_copy(cols1[:, h, 0:m], PS[:, 7, P * (h + 1):P * (h + 1) + m]).then_inc(s["cols_sb"], 1)
                    dve.wait_ge(s["vec_ps"], l + 1)
                    dve.tensor_copy(G.modc[:, l], PS[:, 7, 0:32].rearrange("p (t w) -> p t w", w=2)).then_inc(s["vec_sb"], 1)
                    for w in range(2 - l):
                        for h in range(2):
                            dve.wait_ge(s["gate_ps"], 4 * l + 2 * w + h + 1)
                            dve.tensor_copy(gate[:, 2 * l + w, 512 * h:512 * h + 512], PS[:, 6, :]).then_inc(s["gate_sb"], 1)


def modulate_phase(nc, A, G, layer, xnat, hT):
    PS = G.PS
    jobs = [(k, at, w) for k in range(KT) for at, w in ((0, CTX), (CTX, 512), (CTX + 512, 512))]
    with phase(nc, "turned taken") as (block, s):
        @block.tensor
        def _(pe):
            for n, (k, at, w) in enumerate(jobs):
                if n >= 4:
                    pe.wait_ge(s["taken"], n - 3)
                for i in range(w // P):
                    last = pe.transpose(PS[:, n % 4, i * P:(i + 1) * P], xnat[:, at // P + i, k * P:(k + 1) * P], G.c("ident"))
                last.then_inc(s["turned"], 1)

        @block.vector
        def _(dve):
            for n, (k, at, w) in enumerate(jobs):
                which = 1 if at < CTX else 0
                dve.wait_ge(s["turned"], n + 1)
                dve.tensor_scalar(hT[:, k, at:at + w], PS[:, n % 4, 0:w], G.modc[:, layer, 8 + k, which:which + 1],
                                  G.modc[:, layer, k, which:which + 1], ALU.mult, ALU.add).then_inc(s["taken"], 1)


def modulate_split(nc, G, layer, xnat, hi, lo, full, first_loads, first_high, first_low):
    PS = G.PS
    jobs = [(k, at, w) for k in range(KT) for at, w in ((0, CTX), (CTX, 512), (CTX + 512, 512))]
    with phase(nc, "w_in small_in turned taken hi_ok lo_dve lo_pool w_hi w_lo") as (block, s):
        def low_part(eng, n):
            k, at, w = jobs[n]
            eng.wait_ge(s["hi_ok"], n + 1)
            eng.tensor_tensor(lo[:, k, at:at + w], full[:, n % 4, 0:w], hi[:, k, at:at + w].bitcast(F32),
                              ALU.subtract).then_inc(s["lo_pool" if n % 2 else "lo_dve"], 1)

        @block.sync
        def _(sp):
            n_small = first_loads(sp, s["w_in"], s["small_in"])
            sp.wait_ge(s["small_in"], 16 * n_small)

        @block.tensor
        def _(pe):
            for n, (k, at, w) in enumerate(jobs):
                if n >= 4:
                    pe.wait_ge(s["taken"], n - 3)
                for i in range(w // P):
                    last = pe.transpose(PS[:, n % 4, i * P:(i + 1) * P], xnat[:, at // P + i, k * P:(k + 1) * P], G.c("ident"))
                last.then_inc(s["turned"], 1)

        @block.vector
        def _(dve):
            for n, (k, at, w) in enumerate(jobs):
                which = 1 if at < CTX else 0
                dve.wait_ge(s["turned"], n + 1)
                if n >= 4:
                    dve.wait_ge(s["lo_pool" if n % 2 else "lo_dve"], n // 2 - 1)
                dve.tensor_scalar(full[:, n % 4, 0:w], PS[:, n % 4, 0:w], G.modc[:, layer, 8 + k, which:which + 1],
                                  G.modc[:, layer, k, which:which + 1], ALU.mult, ALU.add).then_inc(s["taken"], 1)
                if n % 2:
                    low_part(dve, n - 1)

        @block.scalar
        def _(act):
            for n, (k, at, w) in enumerate(jobs):
                act.wait_ge(s["taken"], n + 1)
                act.activation(hi[:, k, at:at + w], full[:, n % 4, 0:w], ACT.Copy).then_inc(s["hi_ok"], 1)
            act.wait_ge(s["w_in"], 32)
            first_high(act).then_inc(s["w_hi"], 1)

        @block.gpsimd
        def _(pool):
            for n in range(1, len(jobs), 2):
                low_part(pool, n)
            pool.wait_ge(s["w_hi"], 1)
            first_low(pool).then_inc(s["w_lo"], 1)


def project_split(pe, PS, bank, wh, wl, hh, hl, pieces, at=0):
    for off, n in pieces:
        t = slice(at + off, at + off + n)
        for k in range(KT):
            pe.matmul(PS[:, bank + off // 512, 0:n], wh[:, k], hh[:, k, t], start=(k == 0), stop=False)
            pe.matmul(PS[:, bank + off // 512, 0:n], wh[:, k], hl[:, k, t], start=False, stop=False)
            last = pe.matmul(PS[:, bank + off // 512, 0:n], wl[:, k], hh[:, k, t], start=False, stop=(k == KT - 1))
    return last


def project(pe, PS, bank, w, hT, at=0, rows=P, cols=slice(0, P)):
    for off, n in PIECES if at == 0 else [(0, 512), (512, 512)]:
        for k in range(KT):
            last = pe.matmul(PS[0:rows, bank + off // 512, 0:n], w[:, k, cols], hT[:, k, at + off:at + off + n],
                             start=(k == 0), stop=(k == KT - 1))
    return last


def load_columns(sp, A, w, at, sem):
    sp.dma_start(w[:], A.p["e_w_in"][0].rearrange("(k p) n -> p k n", p=P)[:, :, bass.ds(at, P)]).then_inc(sem, 16)


def flat(PS, bank, rows=P, n=T):
    return PS[0:rows, bank:bank + 3, :].rearrange("p a b -> p (a b)")[:, 0:n]


SHIFT_OPS = 7


def shift_op(dve, n, raw, out, keep, mus):
    if n == 0:
        return dve.tensor_scalar(out[:], raw[:], keep, None, ALU.mult)
    lat_o = out[:, CTX:].rearrange("p (r w) -> p r w", w=GRID_W)
    lat_r = raw[:, CTX:].rearrange("p (r w) -> p r w", w=GRID_W)
    W = GRID_W
    moves = [(0, lat_o[:, :, 1:], lat_r[:, :, :W - 1]), (1, lat_o[:, :, :W - 1], lat_r[:, :, 1:]),
             (2, lat_o[:, 1:, :], lat_r[:, :ROWS - 1, :]), (3, lat_o[:, :ROWS - 1, :], lat_r[:, 1:, :]),
             (0, out[:, 1:CTX], raw[:, 0:CTX - 1]), (1, out[:, 0:CTX - 1], raw[:, 1:CTX])]
    d, o, r = moves[n - 1]
    return dve.scalar_tensor_tensor(o, r, mus[:, d:d + 1], o, ALU.mult, ALU.add)


def shift_mix(dve, step, raw, out, keep, mus, done=None, value=0):
    for n in range(SHIFT_OPS):
        ins = shift_op(dve, n, raw, out, keep, mus)
        if n == SHIFT_OPS - 1 and done is not None:
            step.publish(ins, done, value)
        else:
            step.link(ins)


def lowrank_phase(nc, A, G, w, LW, LA):
    with ExitStack() as ctx:
        def sb(n, s):
            return ctx.enter_context(nc.sbuf_tensor(n, s, F32))
        lg = sb("lr_gla", [32, T])
        raw = sb("lr_raw", [P, 2, T])
        mixed = sb("lr_mixed", [P, T])
        w_next = sb("w_next_lr", [P, KT, P])
        mus = sb("lr_mus", [P, 2, 4])
        keep = sb("lr_keep", [P, 2])
        PS = G.PS
        with phase(nc, "prod taken mixed_ok step finished next_in next_ps stored") as (block, s):
            @block.sync
            def _(sp):
                load_columns(sp, A, w_next, RK, s["next_in"])
                sp.wait_ge(s["taken"], 1)
                sp.dma_start(A.lg_d, lg[:]).then_inc(s["stored"], 16)
                sp.dma_start(G.cst0[:], A.consts[:, G.ends[0]:G.ends[1]]).then_inc(s["stored"], 16)
                sp.dma_start(G.cst_rwkv[:], A.consts[:, G.ends[1]:]).then_inc(s["stored"], 16)
                sp.wait_ge(s["stored"], 48)

            @block.tensor
            def _(pe):
                project(pe, G.PS, 0, w, G.hT, rows=32, cols=slice(0, 32)).then_inc(s["prod"], 1)
                project(pe, G.PS, 3, w, G.hT, cols=slice(32, 160)).then_inc(s["prod"], 1)
                pe.wait_ge(s["taken"], 1)
                project(pe, G.PS, 0, w, G.hT, cols=slice(160, 288)).then_inc(s["prod"], 1)
                pe.wait_ge(s["next_in"], 16)
                pe.wait_ge(s["taken"], 2)
                project(pe, G.PS, 3, w_next, G.hT).then_inc(s["next_ps"], 1)

            @block.scalar
            def _(act):
                act.wait_ge(s["prod"], 1)
                act.activation(lg[:], flat(PS, 0, 32), ACT.Copy).then_inc(s["taken"], 1)
                for i in range(2):
                    act.wait_ge(s["prod"], 2 + i)
                    act.activation(raw[:, i], flat(PS, 3 * (1 - i)), ACT.Copy).then_inc(s["taken"], 1)
                act.wait_ge(s["mixed_ok"], 1)
                act.activation(LW[:], mixed[:], ACT.Tanh).then_inc(s["finished"], 1)
                act.wait_ge(s["next_ps"], 1)
                act.activation(G.ahead, flat(PS, 3), ACT.Copy).then_inc(s["finished"], 1)

            @block.vector
            def _(dve):
                step = Steps(dve, s["step"])
                for i in range(2):
                    mu = G.vc[:, V_MULR + i:V_MULR + i + 1]
                    step.add(dve.tensor_scalar(mus[:, i], G.c("side"), mu, None, ALU.mult))
                    step.link(dve.tensor_scalar(keep[:, i:i + 1], mu, -1.0, 1.0, ALU.mult, ALU.add))
                for i in range(2):
                    dve.wait_ge(s["taken"], 2 + i)
                    shift_mix(dve, step, raw[:, i], (mixed, LA)[i], keep[:, i:i + 1], mus[:, i], s["mixed_ok"], i + 1)


PREP_JOBS = ["w0", "a0", "w1", "a1", "ksum", "r", "v", "g", "bonus"]
ACT_PREP = ["w0", "a0", "w1", "a1", "e0", "e1", "sqrt", "r", "v", "g"]
DVE_PREP = ["K", "sq", "c0", "c1", "ksum", "R", "rk", "V", "bonus"]


def rwkv_prep(nc, A, G, B, p):
    with ExitStack() as ctx:
        def sb(n, s):
            return ctx.enter_context(nc.sbuf_tensor(fresh(G, n), s, F32))
        w = sb("w_pair", [P, 2, KT, P])
        wlr = sb("w_pair_lr", [P, 2, 2, P])
        raw = sb("raw", [P, 2, T])
        R, K, kk, tmp = sb("R", [P, T]), sb("K", [P, T]), sb("kk", [P, T]), sb("tmp", [P, T])
        sg, aa = sb("sg", [P, 2, T]), sb("aa", [P, 2, T])
        mus, keep = B.mus, B.keep
        ka1 = sb("ka1", [P, 1])
        half = sb("half", [P, 2])
        khs = B.bonus
        PS = G.PS

        def col(j):
            return B.cols[:, j:j + 1]

        sems = "zeroed cols_in lr_in w_in0 w_in1 prod act_out dve_out step act_step consts_ok"
        with phase(nc, sems) as (block, s):
            w_in = [s["w_in0"], s["w_in1"]]

            @block.sync
            def _(sp):
                sp.dma_start(B.cols[:], A.cols0_d[bass.ds(p, 1)].rearrange("o p j -> p (o j)")).then_inc(s["cols_in"], 16)
                sp.wait_ge(s["zeroed"], 2)
                for d in range(2):
                    for i, n in enumerate(("rwkv_ww2_", "rwkv_wa2_")):
                        sp.dma_start(wlr[64 * d:64 * d + 64, i, d], A.p[n + "fb"[d]][0][:, bass.ds(p * P, P)]).then_inc(s["lr_in"], 16)
                win = A.p["e_w_in"][0].rearrange("(k p) n -> p k n", p=P)
                for n, at in enumerate((RR, RV, RG)):
                    if n >= 2:
                        sp.wait_ge(s["prod"], after(PREP_JOBS, "r"))
                    sp.dma_start(w[:, n % 2], win[:, :, bass.ds(p * P + at, P)]).then_inc(w_in[n % 2], 16)

            @block.tensor
            def _(pe):
                def lowrank(n, src, i, d):
                    for off, m in PIECES:
                        last = pe.matmul(PS[:, 3 * (n % 2) + off // 512, 0:m], wlr[:, i, d],
                                         src[:, off:off + m], start=True, stop=True)
                    return last

                def head_sum(n, src):
                    for off, m in PIECES:
                        last = pe.matmul(PS[:, 3 * (n % 2) + off // 512, 0:m], G.c("heads"), src[:, off:off + m],
                                         start=True, stop=True)
                    return last

                pe.wait_ge(s["lr_in"], 64)
                for n, job in enumerate(PREP_JOBS):
                    if n >= 2:
                        before = PREP_JOBS[n - 2]
                        if before == "ksum":
                            pe.wait_ge(s["dve_out"], after(DVE_PREP, "ksum"))
                        else:
                            pe.wait_ge(s["act_out"], after(ACT_PREP, before))
                    if job in ("w0", "w1"):
                        last = lowrank(n, B.LW, 0, int(job[1]))
                    elif job in ("a0", "a1"):
                        last = lowrank(n, B.LA, 1, int(job[1]))
                    elif job == "ksum":
                        pe.wait_ge(s["dve_out"], after(DVE_PREP, "sq"))
                        last = head_sum(n, tmp)
                    elif job == "bonus":
                        pe.wait_ge(s["dve_out"], after(DVE_PREP, "rk"))
                        last = head_sum(n, tmp)
                    else:
                        i = "rvg".index(job)
                        pe.wait_ge(w_in[i % 2], 16 * (i // 2 + 1))
                        last = project(pe, PS, 3 * (n % 2), w[:, i % 2], G.hT)
                    last.then_inc(s["prod"], 1)

            @block.scalar
            def _(act):
                def job(name):
                    act.wait_ge(s["prod"], after(PREP_JOBS, name))
                    return flat(PS, 3 * (PREP_JOBS.index(name) % 2))

                act.wait_ge(s["cols_in"], 16)
                for d in range(2):
                    act.activation(sg[:, d], job(f"w{d}"), ACT.Sigmoid, bias=col(J_W0 + d)).then_inc(s["act_out"], 1)
                    act.activation(aa[:, d], job(f"a{d}"), ACT.Sigmoid, bias=col(J_A0 + d)).then_inc(s["act_out"], 1)
                act.wait_ge(s["consts_ok"], 2)
                for d in range(2):
                    act.wait_ge(s["dve_out"], after(DVE_PREP, f"c{d}"))
                    act.activation(B.kt[:, d], B.rt[:, d], ACT.Exp, scale=DEC, bias=half[:, 1:2])
                    ends = B.rt[:, d].rearrange("p (c t) -> p c t", t=CH)[:, :, (CH - 1) * (1 - d)]
                    act.activation(B.PL[:, d], ends, ACT.Exp, scale=-DEC).then_inc(s["act_step"], 1)
                    act.activation(B.at[:, d], B.at[:, d], ACT.Exp, scale=-DEC, bias=half[:, 0:1])
                    act.wait_ge(s["act_step"], d + 1)
                    act.activation(B.rt[:, d], B.rt[:, d], ACT.Exp, scale=-DEC, bias=half[:, 0:1]).then_inc(s["act_out"], 1)
                act.wait_ge(s["dve_out"], after(DVE_PREP, "ksum"))
                act.activation(tmp[:], tmp[:], ACT.Sqrt).then_inc(s["act_out"], 1)
                act.activation(raw[:, 1], job("r"), ACT.Copy).then_inc(s["act_out"], 1)
                act.activation(raw[:, 0], job("v"), ACT.Copy).then_inc(s["act_out"], 1)
                act.activation(B.sG[:], job("g"), ACT.Copy).then_inc(s["act_out"], 1)

            @block.vector
            def _(dve):
                step = Steps(dve, s["step"])
                out = Steps(dve, s["dve_out"])

                def from_act(name):
                    dve.wait_ge(s["act_out"], after(ACT_PREP, name))

                for d in range(2):
                    dve.memset(wlr[64 * (1 - d):64 * (1 - d) + 64, :, d], 0.0).then_inc(s["zeroed"], 1)
                dve.memset(half[:, 0:1], HALF).then_inc(s["consts_ok"], 1)
                dve.memset(half[:, 1:2], -HALF).then_inc(s["consts_ok"], 1)
                dve.wait_ge(s["cols_in"], 16)
                step.add(dve.tensor_scalar(keep[:], B.cols[:, 0:4], -1.0, 1.0, ALU.mult, ALU.add))
                step.add(dve.tensor_scalar(ka1[:], col(J_KA), -1.0, 1.0, ALU.mult, ALU.add))
                for j in range(4):
                    step.add(dve.tensor_scalar(mus[:, j], G.c("side"), col(j), None, ALU.mult))
                step.wait()

                def mix(j, src, dst):
                    shift_mix(dve, step, src, dst, keep[:, j:j + 1], mus[:, j], s["dve_out"], out.n + 1)
                    out.n += 1

                mix(1, G.ahead, K)
                step.link(dve.tensor_scalar(kk[:], K[:], col(J_KK), None, ALU.mult))
                out.add(dve.tensor_tensor(tmp[:], kk[:], kk[:], ALU.mult))
                for d in range(2):
                    from_act(f"a{d}")
                    c, x = (B.rt[:, d], sg[:, d]) if d == 0 else (B.rt[:, d][:, ::-1], sg[:, d][:, ::-1])
                    step.link(dve.tensor_tensor_scan(c, G.c("keep"), x, 0.0, ALU.mult, ALU.add))
                    out.add(dve.tensor_tensor(B.at[:, d], B.rt[:, d], sg[:, d], ALU.subtract))
                dve.wait_ge(s["prod"], after(PREP_JOBS, "ksum"))
                out.add(dve.tensor_scalar(tmp[:], flat(PS, 3 * (PREP_JOBS.index("ksum") % 2)), 1e-24, None, ALU.max))
                from_act("sqrt")
                step.link(dve.reciprocal(tmp[:], tmp[:]))
                step.link(dve.tensor_tensor(kk[:], kk[:], tmp[:], ALU.mult))
                from_act("r")
                mix(0, raw[:, 1], R)
                for d in range(2):
                    step.link(dve.tensor_scalar(tmp[:], aa[:, d], col(J_KA), ka1[:], ALU.mult, ALU.add))
                    kh = khs if d == 0 else tmp
                    step.add(dve.tensor_tensor(kh[:], K[:], tmp[:], ALU.mult))
                    step.link(dve.tensor_tensor(aa[:, d], kk[:], aa[:, d], ALU.mult))
                    from_act(f"e{d}")
                    step.add(dve.tensor_tensor(B.bt[:, d], aa[:, d], B.kt[:, d], ALU.mult))
                    step.add(dve.tensor_tensor(B.rt[:, d], R[:], B.rt[:, d], ALU.mult))
                    step.add(dve.scalar_tensor_tensor(B.at[:, d], kk[:], -1.0, B.at[:, d], ALU.mult, ALU.mult))
                    step.link(dve.tensor_tensor(B.kt[:, d], kh[:], B.kt[:, d], ALU.mult))
                step.link(dve.tensor_tensor(khs[:], khs[:], tmp[:], ALU.add))
                out.add(dve.scalar_tensor_tensor(tmp[:], R[:], col(J_RK), khs[:], ALU.mult, ALU.mult))
                from_act("v")
                mix(2, raw[:, 0], B.V)
                dve.wait_ge(s["prod"], after(PREP_JOBS, "bonus"))
                out.add(dve.tensor_tensor(B.bonus[:], flat(PS, 3 * (PREP_JOBS.index("bonus") % 2)), B.V[:], ALU.mult))


PE_CHUNK = ["nat", "bx", "kx", "X1"] + [f"{x}{b}" for b in LEVELS[1:] for x in "YDT"] + ["Z", "WU", "out"]
ACT_CHUNK = ["nat", "I", "X1"] + [f"{x}{b}" for b in LEVELS[1:] for x in "YT"] + ["WU", "out"]
DVE_CHUNK = ["bx", "XT1", "kx"] + [f"X{b}" for b in LEVELS[1:]] + ["Z", "out"]
SLOTS = 2


def in_turns(names):
    rest, order = list(names), []
    while rest:
        n = 2 if rest[0][0] == "T" and len(rest) > 1 and rest[1] != "WU" else 1
        for i in range(SLOTS):
            order += [(name, i) for name in rest[:n]]
        rest = rest[n:]
    return order


def rwkv_chunks(nc, A, G, B):
    with ExitStack() as ctx:
        def sb(n, s):
            return ctx.enter_context(nc.sbuf_tensor(fresh(G, n), s, F32))
        AZ = [sb(f"AZ{i}", [P, 2, 2, 2, 64]) for i in range(SLOTS)]
        NAT = [sb(f"NAT{i}", [P, 2, 2, P]) for i in range(SLOTS)]
        VN = [sb(f"VN{i}", [P, P]) for i in range(SLOTS)]
        NR = [sb(f"NR{i}", [P, 2, 2, 2, P]) for i in range(SLOTS)]
        AR = [sb(f"AR{i}", [P, 2, 2, 2, P]) for i in range(SLOTS)]
        RK_ = [sb(f"RKS{i}", [P, 2, P]) for i in range(SLOTS)]
        X = [sb(f"X{i}", [P, 4, P]) for i in range(SLOTS)]
        XT = [sb(f"XT{i}", [P, 4, P]) for i in range(SLOTS)]
        Y = [sb(f"Y{i}", [P, 4, P]) for i in range(SLOTS)]
        WU = [sb(f"WU{i}", [P, 4, P]) for i in range(SLOTS)]
        PS = G.PS
        with phase(nc, "pe0 pe1 act0 act1 dve0 dve1 gate_step gate_ok") as (block, s):
            done = {"pe": [s["pe0"], s["pe1"]], "act": [s["act0"], s["act1"]], "dve": [s["dve0"], s["dve1"]]}
            names = {"pe": PE_CHUNK, "act": ACT_CHUNK, "dve": DVE_CHUNK}

            def need(eng, c, engine, name, back=0):
                n = c // SLOTS - back
                if n >= 0:
                    eng.wait_ge(done[engine][c % SLOTS], n * len(names[engine]) + after(names[engine], name))

            def bank(c, i):
                return PS[:, 4 * (c % SLOTS) + i, :]

            def tokens(c):
                return slice(CH * c, CH * c + CH)

            LO, HI = slice(0, 64), slice(64, 128)
            quarter = [(HI, LO), (LO, HI)]

            def quarters(x, d, turned=False):
                r, q = quarter[d][::-1] if turned else quarter[d]
                return x[r, 2 * d:2 * d + 2, q]

            def units(b):
                return b.rearrange("p (u n) -> p u n", n=P)

            @block.tensor
            def _(pe):
                def stage(c, name):
                    i, t = c % SLOTS, tokens(c)
                    b0, b1, b2, b3 = (bank(c, j) for j in range(4))
                    if name == "nat":
                        need(pe, c, "dve", "Z", 1)
                        need(pe, c, "act", "WU", 1)
                        for d, b in enumerate((b0, b1)):
                            for j, x in enumerate((B.bt, B.kt, B.at)):
                                last = pe.transpose(b[:, j * P:(j + 1) * P], x[:, d, t], G.c("ident"))
                        last = pe.transpose(b0[:, 3 * P:4 * P], B.V[:, t], G.c("ident"))
                    elif name in ("bx", "kx"):
                        if name == "bx":
                            need(pe, c, "dve", "out", 1)
                            need(pe, c, "act", "out", 1)
                        else:
                            need(pe, c, "act", "nat")
                        for h in range(2):
                            q = slice(64 * h, 64 * h + 64)
                            b = ((b2, b3) if name == "bx" else (b0, b1))[h]
                            for d in range(2):
                                for j, x in enumerate((B.at, B.rt)):
                                    last = pe.matmul(b[:, (2 * d + j) * P:(2 * d + j + 1) * P],
                                                     (B.bt if name == "bx" else B.kt)[q, d, t], x[q, d, t],
                                                     start=True, stop=True)
                    elif name == "Y64":
                        need(pe, c, "dve", "X32")
                        for u in range(4):
                            r, q = quarter[u // 2]
                            last = pe.matmul(units(b0)[r, u, q], NR[i][:, u % 2, u // 2, 0, r], X[i][:, u, q], start=True, stop=True)
                    elif name == "D64":
                        need(pe, c, "act", "Y64")
                        for u in range(4):
                            r, q = quarter[u // 2]
                            last = pe.matmul(units(b1)[r, u, q], XT[i][r, u, r], Y[i][r, u, q], start=True, stop=True)
                    elif name[0] in "XT":
                        if name == "X1":
                            need(pe, c, "dve", "XT1")
                        else:
                            need(pe, c, "dve", "X" + name[1:])
                        for u in range(4):
                            last = pe.transpose(b2[:, u * P:(u + 1) * P], (XT if name == "X1" else X)[i][:, u], G.c("ident"))
                    elif name[0] == "Y":
                        l = LEVELS.index(int(name[1:]))
                        if l == 1:
                            need(pe, c, "act", "X1")
                            need(pe, c, "dve", "kx")
                        else:
                            need(pe, c, "dve", f"X{LEVELS[l - 1]}")
                        for u in range(4):
                            last = pe.matmul(b0[:, u * P:(u + 1) * P], NR[i][:, u % 2, u // 2, 0], X[i][:, u], start=True, stop=True)
                    elif name[0] == "D":
                        need(pe, c, "act", "Y" + name[1:])
                        for u in range(4):
                            last = pe.matmul(b1[:, u * P:(u + 1) * P], XT[i][:, u], Y[i][:, u], start=True, stop=True)
                    elif name == "Z":
                        for u in range(4):
                            last = pe.matmul(b0[:, u * P:(u + 1) * P], AR[i][:, u % 2, u // 2, 0], VN[i][:], start=True, stop=True)
                    elif name == "WU":
                        need(pe, c, "dve", "Z")
                        need(pe, c, "act", f"T{LEVELS[-1]}")
                        for u in range(4):
                            last = pe.matmul(b1[:, u * P:(u + 1) * P], XT[i][:, u],
                                             AZ[i][:, u // 2, u % 2].rearrange("p a b -> p (a b)"), start=True, stop=True)
                    else:
                        need(pe, c, "act", "WU")
                        for h in range(2):
                            q = slice(64 * h, 64 * h + 64)
                            for d in range(2):
                                W, U = WU[i][:, 2 * d + h, 0:64], WU[i][:, 2 * d + h, 64:128]
                                b_, k_ = NAT[i][:, d, 0, q], NAT[i][:, d, 1, q]
                                pe.matmul(b2[q, d * P:(d + 1) * P], W, NR[i][:, h, d, 1], start=True, stop=True)
                                pe.matmul(b2[q, 256 + 64 * d:320 + 64 * d], W, b_, start=True, stop=True)
                                pe.matmul(b2[q, 384 + 64 * d:448 + 64 * d], b_, U, start=True, stop=False)
                                pe.matmul(b2[q, 384 + 64 * d:448 + 64 * d], k_, VN[i][:, q], start=False, stop=True)
                            for d in range(2):
                                pe.matmul(b3[q, 0:P], WU[i][:, 2 * d + h, 64:128], NR[i][:, h, d, 1], start=(d == 0), stop=False)
                            last = pe.matmul(b3[q, 0:P], VN[i][:, q], RK_[i][:, h], start=False, stop=True)
                    last.then_inc(done["pe"][i], 1)

                for c in range(0, NCH, SLOTS):
                    for name, i in in_turns(PE_CHUNK):
                        stage(c + i, name)

            @block.scalar
            def _(act):
                def stage(c, name):
                    i = c % SLOTS
                    b0, b1, b2, b3 = (bank(c, j) for j in range(4))
                    if name != "I":
                        need(act, c, "pe", name)
                    if name == "nat":
                        for d, b in enumerate((b0, b1)):
                            act.activation(NAT[i][:, d].rearrange("p a b -> p (a b)"), b[:, 0:2 * P], ACT.Copy)
                            act.activation(AZ[i][:, d, :, 0, :], b[:, 2 * P:3 * P].rearrange("p (h n) -> p h n", h=2), ACT.Copy)
                        last = act.activation(VN[i][:], b0[:, 3 * P:4 * P], ACT.Copy)
                    elif name == "I":
                        last = act.activation(XT[i][:], G.c("ident")[:, None, :].broadcast_to([P, 4, P]), ACT.Copy)
                    elif name == "out":
                        last = act.activation(B.Y[:, tokens(c)], b3[:, 0:P], ACT.Copy)
                    elif name in ("Y64", "T64"):
                        dst, b = (Y, b0) if name == "Y64" else (XT, b2)
                        for d in range(2):
                            last = act.activation(quarters(dst[i], d, name == "T64"), quarters(units(b), d, name == "T64"), ACT.Copy)
                    else:
                        dst, b = {"X": (X, b2), "T": (XT, b2), "Y": (Y, b0), "W": (WU, b1)}[name[0]]
                        last = act.activation(dst[i][:].rearrange("p a b -> p (a b)"), b, ACT.Copy)
                    last.then_inc(done["act"][i], 1)

                for c in range(0, NCH, SLOTS):
                    for name, i in in_turns(ACT_CHUNK):
                        stage(c + i, name)
                    if c == SLOTS:
                        act.wait_ge(s["gate_step"], SHIFT_OPS)
                        act.activation(B.sG[:], B.gate[:], ACT.Silu).then_inc(s["gate_ok"], 1)

            @block.vector
            def _(dve):
                def stage(c, name):
                    i = c % SLOTS
                    b0, b1, b2, b3 = (bank(c, j) for j in range(4))
                    if name in ("bx", "kx"):
                        need(dve, c, "pe", name)
                        for h, b in enumerate((b2, b3) if name == "bx" else (b0, b1)):
                            last = dve.tensor_tensor((NR if name == "bx" else AR)[i][:, h].rearrange("p a b c -> p (a b c)"),
                                                     b, G.c("score"), ALU.mult)
                    elif name == "XT1":
                        need(dve, c, "act", "I")
                        need(dve, c, "dve", "bx")
                        last = dve.copy_predicated(XT[i][:].rearrange("p (d h) n -> p d h n", d=2),
                                                   G.c("level1").bitcast(I32).rearrange("p (d h n) -> p d h n", d=2, h=2),
                                                   NR[i][:, :, :, 0].rearrange("p h d n -> p d h n"))
                    elif name == "Z":
                        need(dve, c, "dve", "kx")
                        dve.tensor_tensor(RK_[i][:], AR[i][:, :, 0, 1], AR[i][:, :, 1, 1], ALU.add)
                        need(dve, c, "pe", "Z")
                        for h in range(2):
                            last = dve.tensor_copy(AZ[i][:, :, h, 1, :],
                                                   b0.rearrange("p (d h n) -> p d h n", d=2, h=2)[:, :, h, 64 * h:64 * h + 64])
                    elif name == "out":
                        need(dve, c, "pe", "out")
                        dve.tensor_tensor(B.QT[:, c], b2[:, 0:256].rearrange("p (d t) -> p d t", d=2), B.rt[:, :, tokens(c)], ALU.add)
                        dve.tensor_tensor(B.HS[:, c], b2[:, 384:512].rearrange("p (d t) -> p d t", d=2),
                                          B.PL[:, :, c:c + 1].broadcast_to([P, 2, 64]), ALU.mult)
                        last = dve.tensor_tensor(B.GT[:, c], b2[:, 256:384].rearrange("p (d t) -> p d t", d=2),
                                                 G.c("eye64")[:, None, :].broadcast_to([P, 2, 64]), ALU.add)
                    elif name == "X64":
                        need(dve, c, "pe", "D64")
                        for d in range(2):
                            last = dve.tensor_copy(quarters(X[i], d), quarters(units(b1), d))
                    else:
                        need(dve, c, "pe", "D" + name[1:])
                        last = dve.copy_predicated(X[i][:].rearrange("p a b -> p (a b)"), G.c("level" + name[1:]).bitcast(I32), b1)
                    last.then_inc(done["dve"][i], 1)

                for c in range(0, NCH, SLOTS):
                    for n, name in enumerate(DVE_CHUNK):
                        for i in range(SLOTS):
                            stage(c + i, name)
                        if c == 0 and 3 <= n < 3 + SHIFT_OPS:
                            if n > 3:
                                dve.wait_ge(s["gate_step"], n - 3)
                            shift_op(dve, n - 3, B.sG, B.gate, B.keep[:, 3:4], B.mus[:, 3]).then_inc(s["gate_step"], 1)


def chunk_chain(d):
    return list(zip(ORDER[d][:-1], ORDER[d][1:]))


def rwkv_finish(nc, A, G, B, p, next_at):
    with ExitStack() as ctx:
        def sb(n, s):
            return ctx.enter_context(nc.sbuf_tensor(fresh(G, n), s, F32))
        S = sb("S_rwkv", [P, 2, NCH, 64])
        yc, sq = sb("y_centered", [P, T]), sb("y_square", [P, T])
        eps = sb("eps_gn", [P, 1])
        w_next = sb("w_next", [P, KT, P])
        PS = G.PS

        def col(j):
            return B.cols[:, j:j + 1]

        with phase(nc, "zero chain state0 state1 read_ps read_sb mean_ps centered squared var_ps root step next_in next_ps next_sb stored eps_ok") as (block, s):
            state = [s["state0"], s["state1"]]

            @block.tensor
            def _(pe):
                pe.wait_ge(s["zero"], 2)
                for n in range(NCH - 1):
                    for d in range(2):
                        c = ORDER[d][n]
                        if n:
                            pe.wait_ge(state[d], n)
                        for h in range(2):
                            q = slice(64 * h, 64 * h + 64)
                            last = pe.matmul(PS[q, d, 0:64], B.GT[q, c, d], S[q, d, c], start=True, stop=True)
                        last.then_inc(s["chain"], 1)
                for d in range(2):
                    pe.wait_ge(state[d], NCH - 1)
                for c in range(NCH):
                    for h in range(2):
                        q = slice(64 * h, 64 * h + 64)
                        for d in range(2):
                            last = pe.matmul(PS[q, 2 + c // 4, (c % 4) * P:(c % 4 + 1) * P], S[q, d, c], B.QT[q, c, d],
                                             start=(d == 0), stop=(d == 1))
                last.then_inc(s["read_ps"], 1)
                pe.wait_ge(s["read_sb"], 1)
                for off, m in PIECES:
                    last = pe.matmul(PS[:, 5 + off // 512, 0:m], G.c("heads"), B.Y[:, off:off + m], start=True, stop=True)
                last.then_inc(s["mean_ps"], 1)
                pe.wait_ge(s["squared"], 1)
                for off, m in PIECES:
                    last = pe.matmul(PS[:, 2 + off // 512, 0:m], G.c("heads"), sq[:, off:off + m], start=True, stop=True)
                last.then_inc(s["var_ps"], 1)
                pe.wait_ge(s["next_in"], 16)
                pe.wait_ge(s["centered"], 1)
                project(pe, PS, 5, w_next, G.hT).then_inc(s["next_ps"], 1)

            @block.scalar
            def _(act):
                act.wait_ge(s["centered"], 1)
                act.activation(sq[:], yc[:], ACT.Square).then_inc(s["squared"], 1)
                act.wait_ge(s["var_ps"], 1)
                act.wait_ge(s["eps_ok"], 1)
                act.activation(sq[:], flat(PS, 2), ACT.Sqrt, scale=1.0 / 64, bias=eps[:]).then_inc(s["root"], 1)
                act.wait_ge(s["next_ps"], 1)
                act.activation(G.ahead, flat(PS, 5), ACT.Copy).then_inc(s["next_sb"], 1)

            @block.vector
            def _(dve):
                step = Steps(dve, s["step"])
                dve.memset(eps[:], EPS_GN).then_inc(s["eps_ok"], 1)
                for d in range(2):
                    dve.memset(S[:, d, ORDER[d][0]], 0.0).then_inc(s["zero"], 1)
                for n in range(NCH - 1):
                    for d in range(2):
                        c, c1 = ORDER[d][n], ORDER[d][n + 1]
                        dve.wait_ge(s["chain"], 2 * n + d + 1)
                        dve.scalar_tensor_tensor(S[:, d, c1], PS[:, d, 0:64], B.PL[:, d, c:c + 1], B.HS[:, c, d],
                                                 ALU.mult, ALU.add).then_inc(state[d], 1)
                dve.wait_ge(s["read_ps"], 1)
                step.publish(dve.tensor_tensor(B.Y[:], flat(PS, 2), B.Y[:], ALU.add), s["read_sb"], 1)
                dve.wait_ge(s["mean_ps"], 1)
                step.publish(dve.scalar_tensor_tensor(yc[:], flat(PS, 5), -1.0 / 64, B.Y[:], ALU.mult, ALU.add), s["centered"], 1)
                dve.wait_ge(s["root"], 1)
                step.link(dve.reciprocal(sq[:], sq[:]))
                step.link(dve.tensor_tensor(yc[:], yc[:], sq[:], ALU.mult))
                step.link(dve.tensor_scalar(yc[:], yc[:], col(J_GG), col(J_GB), ALU.mult, ALU.add))
                step.link(dve.tensor_tensor(yc[:], yc[:], B.bonus[:], ALU.add))
                step.publish(dve.tensor_tensor(yc[:], yc[:], B.sG[:], ALU.mult), s["read_sb"], 2)

            @block.sync
            def _(sp):
                load_columns(sp, A, w_next, next_at, s["next_in"])
                sp.wait_ge(s["read_sb"], 2)
                sp.dma_start(A.yT_d[bass.ds(p + 4, 1)].rearrange("o p t -> p (o t)"), yc[:]).then_inc(s["stored"], 16)
                sp.wait_ge(s["stored"], 16)


GLA_JOBS = ["x0", "x1", "k", "g0", "g1"]
ACT_GLA = ["q", "x0", "l0", "x1", "l1", "k", "g0", "g1", "eq0", "ek0", "eq1", "ek1"]
DVE_GLA = ["b0", "b1", "kd0", "kd1"]


def gla_prep(nc, A, G, B, g):
    with ExitStack() as ctx:
        def sb(n, s):
            return ctx.enter_context(nc.sbuf_tensor(fresh(G, n), s, F32))
        w = sb("w_gla", [P, 2, KT, P])
        wv = sb("w_gla_v", [P, KT, 2 * P])
        wa2 = sb("wa2", [32, 2, P])
        lg = sb("lg", [32, T])
        ba = sb("gla_ba", [P, 2])
        x, l, kd = sb("gla_x", [P, 2, T]), sb("gla_l", [P, 2, T]), sb("gla_kd", [P, 2, T])
        PS = G.PS
        sems = "zeroed lr_in w_in0 w_in1 wv_in prod v_ps v_sb act_out dve_out step act_step turned kn_sb"
        with phase(nc, sems) as (block, s):
            w_in = [s["w_in0"], s["w_in1"]]

            @block.sync
            def _(sp):
                sp.wait_ge(s["zeroed"], 1)
                for d in range(2):
                    q = slice(64 * d, 64 * d + 64)
                    sp.dma_start(wa2[16 * d:16 * d + 16, :, q],
                                 A.p["gla_wa2_" + "fb"[d]][0][:, bass.ds(g * P, P)].rearrange("r (h c) -> r h c", h=2)).then_inc(s["lr_in"], 16)
                    for h in range(2):
                        sp.dma_start(ba[q, h:h + 1], A.p["gla_ba_" + "fb"[d]][0][bass.ds(g * P + 64 * h, 64)].rearrange("(c o) -> c o", o=1)).then_inc(s["lr_in"], 16)
                sp.dma_start(lg[:], A.lg_d).then_inc(s["lr_in"], 16)
                win = A.p["e_w_in"][0].rearrange("(k p) n -> p k n", p=P)
                starts = [g * P + GK, g * 2 * P + GG, g * 2 * P + (GG + P)]
                for n, at in enumerate(starts):
                    if n >= 2:
                        sp.wait_ge(s["prod"], after(GLA_JOBS, "k"))
                    sp.dma_start(w[:, n % 2], win[:, :, bass.ds(at, P)]).then_inc(w_in[n % 2], 16)
                    if n == 1:
                        sp.dma_start(wv[:], win[:, :, bass.ds(g * 2 * P + GV, 2 * P)]).then_inc(s["wv_in"], 16)

            @block.tensor
            def _(pe):
                pe.wait_ge(s["lr_in"], 7 * 16)
                for n, job in enumerate(GLA_JOBS):
                    if n >= 2:
                        pe.wait_ge(s["act_out"], after(ACT_GLA, GLA_JOBS[n - 2]))
                    if n < 2:
                        for off, m in PIECES:
                            last = pe.matmul(PS[:, 3 * n + off // 512, 0:m], wa2[:, n], lg[:, off:off + m], start=True, stop=True)
                    else:
                        pe.wait_ge(w_in[n % 2], 16 * (n // 2))
                        last = project(pe, PS, 3 * (n % 2), w[:, n % 2], G.hT)
                    last.then_inc(s["prod"], 1)
                pe.wait_ge(s["wv_in"], 16)
                for c in range(NCH):
                    if c >= 2:
                        pe.wait_ge(s["v_sb"], c - 1)
                    for k in range(KT):
                        last = pe.matmul(PS[:, 6 + c % 2, 0:2 * P], G.hT[:, k, c * CH:(c + 1) * CH], wv[:, k],
                                         start=(k == 0), stop=(k == KT - 1))
                    last.then_inc(s["v_ps"], 1)
                for h in range(2):
                    pe.wait_ge(s["dve_out"], after(DVE_GLA, f"kd{h}"))
                    if h == 0:
                        pe.wait_ge(s["act_out"], after(ACT_GLA, "g1"))
                    for j in range(3):
                        for c in range(4 * j, min(4 * j + 4, NCH)):
                            last = pe.transpose(PS[:, 3 * h + j, (c % 4) * P:(c % 4 + 1) * P], kd[:, h, c * CH:(c + 1) * CH], G.c("ident"))
                    last.then_inc(s["turned"], 1)

            @block.scalar
            def _(act):
                step = Steps(act, s["act_step"])
                out = Steps(act, s["act_out"])

                def job(name):
                    act.wait_ge(s["prod"], after(GLA_JOBS, name))
                    return flat(PS, 3 * (GLA_JOBS.index(name) % 2))

                def two_halves(dst, src, scale):
                    for h in range(2):
                        for d in range(2):
                            last = act.activation(dst[64 * d:64 * d + 64, h], src[64 * h:64 * h + 64], ACT.Copy, scale=scale)
                    out.add(last)

                two_halves(B.q, G.ahead, 0.125)
                act.wait_ge(s["lr_in"], 7 * 16)
                for h in range(2):
                    out.link(act.activation(x[:, h], job(f"x{h}"), ACT.Identity, bias=ba[:, h:h + 1]))
                    step.link(act.activation(l[:, h], x[:, h], ACT.Abs))
                    step.link(act.activation(l[:, h], l[:, h], ACT.Exp, scale=-1.0))
                    out.add(act.activation(l[:, h], l[:, h], ACT.Ln, bias=G.c("ones")[:, 0:1]))
                two_halves(B.k, job("k"), 1.0)
                for h in range(2):
                    out.add(act.activation(B.sG[:, h], job(f"g{h}"), ACT.Silu))
                for c in range(NCH):
                    act.wait_ge(s["v_ps"], c + 1)
                    act.activation(B.V[:, c], PS[:, 6 + c % 2, 0:2 * P], ACT.Copy).then_inc(s["v_sb"], 1)
                for h in range(2):
                    act.wait_ge(s["dve_out"], after(DVE_GLA, f"b{h}"))
                    out.add(act.activation(B.qd[:, h], B.b[:, h], ACT.Exp, scale=1.0 / 16))
                    for d in range(2):
                        q = slice(64 * d, 64 * d + 64)
                        act.activation(B.tot[q, h], B.b[q, h].rearrange("p (c t) -> p c t", t=CH)[:, :, (CH - 1) * (1 - d)],
                                       ACT.Exp, scale=1.0 / 16)
                    out.add(act.activation(kd[:, h], kd[:, h], ACT.Exp, scale=1.0 / 16))
                for h in range(2):
                    act.wait_ge(s["turned"], h + 1)
                    act.activation(B.KN[:, h].rearrange("p c n -> p (c n)"), flat(PS, 3 * h), ACT.Copy).then_inc(s["kn_sb"], 1)

            @block.vector
            def _(dve):
                step = Steps(dve, s["step"])
                out = Steps(dve, s["dve_out"])
                dve.memset(wa2[:], 0.0).then_inc(s["zeroed"], 1)
                for h in range(2):
                    dve.wait_ge(s["act_out"], after(ACT_GLA, f"l{h}"))
                    step.link(dve.scalar_tensor_tensor(x[:, h], x[:, h], 0.0, l[:, h], ALU.min, ALU.subtract))
                    rows = [slice(64 * d, 64 * d + 64) for d in range(2)]
                    for d, q in enumerate(rows):
                        c, v = (B.b[q, h], x[q, h]) if d == 0 else (B.b[q, h][:, ::-1], x[q, h][:, ::-1])
                        step.add(dve.tensor_tensor_scan(c, G.c("keep")[q], v, 0.0, ALU.mult, ALU.add))
                    step.wait()
                    for d, q in enumerate(rows):
                        b3 = B.b[q, h].rearrange("p (c t) -> p c t", t=CH)
                        end = (CH - 1) * (1 - d)
                        last = dve.tensor_tensor(kd[q, h].rearrange("p (c t) -> p c t", t=CH), b3[:, :, end:end + 1].broadcast_to([64, NCH, CH]), b3,
                                                 ALU.subtract)
                    out.add(last)
                for h in range(2):
                    dve.wait_ge(s["act_out"], after(ACT_GLA, f"ek{h}"))
                    dve.tensor_tensor(B.qd[:, h], B.qd[:, h], B.q[:, h], ALU.mult)
                    out.add(dve.tensor_tensor(kd[:, h], kd[:, h], B.k[:, h], ALU.mult))


def gla_scores(nc, A, G, B):
    with ExitStack() as ctx:
        def sb(n, s):
            return ctx.enter_context(nc.sbuf_tensor(fresh(G, n), s, F32))
        E = sb("lev_e", [P, 2, 2, T])
        QL, KL = sb("lev_q", [P, 2, 2, T]), sb("lev_k", [P, 2, 2, T])
        PS = G.PS
        groups = [(0, 4), (4, 4), (8, 2)]
        jobs = [(b, h, j) for b in [0] + LEVELS for h in range(2) for j in range(3)]

        def half(x, b, d, right):
            v = x[64 * d:64 * d + 64].rearrange("p (n t) -> p n t", t=2 * b)
            return v[:, :, b:] if right else v[:, :, :b]

        with phase(nc, "dist away expd q_zero q_ok k_ok scored merged") as (block, s):
            def buffer_free(eng, lv, h):
                if lv >= 2:
                    eng.wait_ge(s["scored"], jobs.index((LEVELS[lv - 2], h, 2)) + 1)

            @block.tensor
            def _(pe):
                for n, (b, h, j) in enumerate(jobs):
                    lv = LEVELS.index(b) if b else -1
                    if n >= 8:
                        pe.wait_ge(s["merged"], n - 7)
                    if b:
                        pe.wait_ge(s["q_ok"], 2 * lv + h + 1)
                        pe.wait_ge(s["k_ok"], 2 * lv + h + 1)
                    for i in range(groups[j][1]):
                        c = groups[j][0] + i
                        t = slice(c * CH, c * CH + CH)
                        lhs, rhs = (KL[:, lv % 2, h, t], QL[:, lv % 2, h, t]) if b else (B.k[:, h, t], B.q[:, h, t])
                        last = pe.matmul(PS[:, n % 8, i * P:(i + 1) * P], lhs, rhs, start=True, stop=True)
                    last.then_inc(s["scored"], 1)

            def merge_jobs(dve, level):
                for n, (b, h, j) in enumerate(jobs):
                    if b != level:
                        continue
                    c0, m = groups[j]
                    dve.wait_ge(s["scored"], n + 1)
                    if n >= 6:
                        dve.wait_ge(s["merged"], n - 5)
                    out = B.A[:, c0:c0 + m, h, :]
                    ps = PS[:, n % 8, 0:m * P].rearrange("p (c t) -> p c t", t=P)
                    if not b:
                        ins = dve.tensor_tensor(out, ps, G.c("ident")[:, None, :].broadcast_to([P, m, P]), ALU.mult)
                    else:
                        ins = dve.copy_predicated(out, G.c(f"parted{b}").bitcast(I32)[:, None, :].broadcast_to([P, m, P]), ps)
                    ins.then_inc(s["merged"], 1)

            @block.vector
            def _(dve):
                for lv, b in enumerate(LEVELS):
                    for h in range(2):
                        buffer_free(dve, lv, h)
                        if lv >= 2:
                            dve.wait_ge(s["k_ok"], 2 * (lv - 2) + h + 1)
                            dve.wait_ge(s["q_ok"], 2 * (lv - 2) + h + 1)
                        blocks = B.b[:, h].rearrange("p (n t) -> p n t", t=2 * b)
                        dve.tensor_tensor(E[:, lv % 2, h].rearrange("p (n t) -> p n t", t=2 * b), blocks,
                                          blocks[:, :, b:b + 1].broadcast_to([P, T // (2 * b), 2 * b]), ALU.subtract).then_inc(s["dist"], 1)
                    merge_jobs(dve, LEVELS[lv - 1] if lv else 0)
                    for h in range(2):
                        dve.wait_ge(s["expd"], 2 * lv + h + 1)
                        dve.wait_ge(s["q_zero"], 2 * lv + h + 1)
                        for d in range(2):
                            last = dve.tensor_tensor(half(QL[:, lv % 2, h], b, d, d == 0), half(E[:, lv % 2, h], b, d, d == 0),
                                                     half(B.q[:, h], b, d, d == 0), ALU.mult)
                        last.then_inc(s["q_ok"], 1)
                merge_jobs(dve, LEVELS[-1])

            @block.scalar
            def _(act):
                for n in range(2 * len(LEVELS)):
                    e = E[:, n // 2 % 2, n % 2]
                    act.wait_ge(s["dist"], n + 1)
                    act.activation(e, e, ACT.Abs).then_inc(s["away"], 1)
                    act.wait_ge(s["away"], n + 1)
                    act.activation(e, e, ACT.Exp, scale=-1.0 / 16).then_inc(s["expd"], 1)

            @block.gpsimd
            def _(pool):
                def zeros(n):
                    lv, h = n // 2, n % 2
                    buffer_free(pool, lv, h)
                    if lv >= 2:
                        pool.wait_ge(s["q_ok"], 2 * (lv - 2) + h + 1)
                    for d in range(2):
                        last = pool.memset(half(QL[:, lv % 2, h], LEVELS[lv], d, d == 1), 0.0)
                    last.then_inc(s["q_zero"], 1)

                zeros(0)
                for n in range(2 * len(LEVELS)):
                    lv, h = n // 2, n % 2
                    pool.wait_ge(s["expd"], n + 1)
                    pool.wait_ge(s["q_zero"], n + 1)
                    pool.tensor_tensor(KL[:, lv % 2, h], E[:, lv % 2, h], B.k[:, h], ALU.mult).then_inc(s["k_ok"], 1)
                    pool.wait_ge(s["k_ok"], n + 1)
                    if n + 1 < 2 * len(LEVELS):
                        zeros(n + 1)


def gla_out(nc, A, G, B, g, next_at):
    with ExitStack() as ctx:
        def sb(n, s):
            return ctx.enter_context(nc.sbuf_tensor(fresh(G, n), s, F32))
        S = sb("S_gla", [P, 2, NCH, P])
        o, sq = sb("gla_o", [P, 2, T]), sb("gla_sq", [P, 2, T])
        eps = sb("eps_gla", [P, 1])
        w_next = sb("w_next_gla", [P, KT, P])
        PS = G.PS
        with phase(nc, "zero outer state00 state01 state10 state11 o_ps o_sb squared var_ps root step y_ok next_in next_ps next_sb stored eps_ok") as (block, s):
            state = [[s["state00"], s["state01"]], [s["state10"], s["state11"]]]

            def cols(h, c):
                return PS[:, 3 * h + c // 4, (c % 4) * P:(c % 4 + 1) * P]

            @block.tensor
            def _(pe):
                for h in range(2):
                    for c in range(NCH):
                        last = pe.matmul(cols(h, c), B.KN[:, h, c], B.V[:, c, h * P:(h + 1) * P], start=True, stop=True)
                    last.then_inc(s["outer"], 1)
                pe.wait_ge(s["zero"], 4)
                for h in range(2):
                    for d in range(2):
                        pe.wait_ge(state[h][d], NCH - 1)
                    for c in range(NCH):
                        pe.matmul(cols(h, c), B.V[:, c, h * P:(h + 1) * P], B.A[:, c, h], start=True, stop=False)
                        last = pe.matmul(cols(h, c), S[:, h, c], B.qd[:, h, c * CH:c * CH + CH], start=False, stop=True)
                    last.then_inc(s["o_ps"], 1)
                for h in range(2):
                    pe.wait_ge(s["squared"], h + 1)
                    for off, m in PIECES:
                        last = pe.matmul(PS[:, 3 * h + off // 512, 0:m], G.c("ones"), sq[:, h, off:off + m], start=True, stop=True)
                    last.then_inc(s["var_ps"], 1)
                if next_at is not None:
                    pe.wait_ge(s["next_in"], 16)
                    pe.wait_ge(s["root"], 1)
                    project(pe, PS, 0, w_next, G.hT).then_inc(s["next_ps"], 1)

            @block.scalar
            def _(act):
                for h in range(2):
                    act.wait_ge(s["o_sb"], h + 1)
                    act.activation(sq[:, h], o[:, h], ACT.Square).then_inc(s["squared"], 1)
                act.wait_ge(s["eps_ok"], 1)
                for h in range(2):
                    act.wait_ge(s["var_ps"], h + 1)
                    act.activation(sq[:, h], flat(PS, 3 * h), ACT.Sqrt, scale=1.0 / P, bias=eps[:]).then_inc(s["root"], 1)
                if next_at is not None:
                    act.wait_ge(s["next_ps"], 1)
                    act.activation(G.ahead, flat(PS, 0), ACT.Copy).then_inc(s["next_sb"], 1)

            @block.vector
            def _(dve):
                step = Steps(dve, s["step"])
                dve.memset(eps[:], EPS_LN).then_inc(s["eps_ok"], 1)
                for h in range(2):
                    for d in range(2):
                        dve.memset(S[64 * d:64 * d + 64, h, ORDER[d][0]], 0.0).then_inc(s["zero"], 1)
                dve.wait_ge(s["zero"], 4)
                dve.wait_ge(s["outer"], 2)
                for n in range(NCH - 1):
                    for h in range(2):
                        for d in range(2):
                            q = slice(64 * d, 64 * d + 64)
                            c, c1 = ORDER[d][n], ORDER[d][n + 1]
                            if n:
                                dve.wait_ge(state[h][d], n)
                            dve.scalar_tensor_tensor(S[q, h, c1], S[q, h, c], B.tot[q, h, c:c + 1], cols(h, c)[q],
                                                     ALU.mult, ALU.add).then_inc(state[h][d], 1)
                for h in range(2):
                    dve.wait_ge(s["o_ps"], h + 1)
                    dve.tensor_copy(o[:, h], flat(PS, 3 * h)).then_inc(s["o_sb"], 1)
                for h in range(2):
                    dve.wait_ge(s["root"], h + 1)
                    step.link(dve.reciprocal(sq[:, h], sq[:, h]))
                    step.link(dve.scalar_tensor_tensor(o[:, h], o[:, h], G.vc[:, V_GNG:V_GNG + 1], sq[:, h], ALU.mult, ALU.mult))
                    dve.tensor_tensor(o[:, h], o[:, h], B.sG[:, h], ALU.mult).then_inc(s["y_ok"], 1)

            @block.sync
            def _(sp):
                if next_at is not None:
                    load_columns(sp, A, w_next, next_at, s["next_in"])
                for h in range(2):
                    sp.wait_ge(s["y_ok"], h + 1)
                    sp.dma_start(A.yT_d[bass.ds(g * 2 + h, 1)].rearrange("o p t -> p (o t)"), o[:, h]).then_inc(s["stored"], 16)
                sp.wait_ge(s["stored"], 32)


def out_phase(nc, A, G, layer, yT_d, w_out, n_k, tiles, x_of, xnew, store):
    with ExitStack() as ctx:
        def sb(n, s):
            return ctx.enter_context(nc.sbuf_tensor(f"{n}{layer}", s, F32))
        w = sb("w_out", [P, n_k, D])
        y = sb("y_in", [P, n_k, P * len(tiles)])
        x = sb("x_res", [P, 3, D])
        gate, ln = sb("gate_row", [P, 2, D]), sb("ln_row", [P, 2, D])
        r = sb("resid", [P, 2, D])
        st = sb("stats", [P, 2, 2, 6])
        mv, rstd = sb("mean_var", [P, 2, 2]), sb("rstd", [P, 2, 2])
        eps = sb("eps_ln", [P, 1])
        PS = G.PS
        n_gate = 2 if layer == 0 else 1
        ktiles = n_k // 4
        sems = "y_in0 y_in1 y_in2 y_in3 y_in4 row_in k_in0 k_in1 k_in2 k_in3 x_in0 x_in1 x_in2 prod summed mean_ok root normed scaled added stored0 stored1 step eps_ok"
        ring = 2 if layer else len(tiles)
        with phase(nc, sems) as (block, s):
            stored = [s["stored0"], s["stored1"]]
            k_in = [s["k_in0"], s["k_in1"], s["k_in2"], s["k_in3"]]
            y_in = [s["y_in0"], s["y_in1"], s["y_in2"], s["y_in3"], s["y_in4"]]
            x_in = [s["x_in0"], s["x_in1"], s["x_in2"]]

            @block.sync
            def _(sp):
                wv = w_out.rearrange("(k p) n -> p k n", p=P)
                yv = yT_d.rearrange("k p t -> p k t")

                def load_y(i):
                    t = slice(2 * P * i, 2 * P * (i + 1))
                    sp.dma_start(y[:, :, t], yv[:, :, t]).then_inc(y_in[i], 16)

                for i in range(n_k // ktiles):
                    q = slice(i * ktiles, (i + 1) * ktiles)
                    sp.dma_start(w[:, q], wv[:, q]).then_inc(k_in[i], 16)
                    if i == 0:
                        load_y(0)
                sp.dma_start(gate[:, 0:n_gate], A.gates_d[2 * layer:2 * layer + n_gate].rearrange("g p n -> p g n")).then_inc(s["row_in"], 16)
                for i, v in enumerate(("ln_g", "ln_b")):
                    sp.dma_start(ln[:, i], A.p[v][layer:layer + 1, :].broadcast_to([P, D])).then_inc(s["row_in"], 16)
                for n in range(3):
                    sp.dma_start(x[:, n], x_of(tiles[n])).then_inc(x_in[n], 16)
                for i in range(1, len(tiles) // 2):
                    load_y(i)
                for n, t in enumerate(tiles):
                    sp.wait_ge(s["added"], n + 1)
                    sp.dma_start(store(t), xnew[:, n % ring]).then_inc(stored[n % 2], 16)
                    if n + 3 < len(tiles):
                        sp.wait_ge(s["summed"], n + 1)
                        sp.dma_start(x[:, n % 3], x_of(tiles[n + 3])).then_inc(x_in[n % 3], 16)
                for i in range(2):
                    sp.wait_ge(stored[i], 16 * (len(tiles) // 2))

            @block.tensor
            def _(pe):
                for n in range(len(tiles)):
                    if n >= 4:
                        pe.wait_ge(s["summed"], n - 3)
                    if n % 2 == 0:
                        pe.wait_ge(y_in[n // 2], 16)
                    for k in range(n_k):
                        if n == 0 and k % ktiles == 0:
                            pe.wait_ge(k_in[k // ktiles], 16)
                        for h in range(2):
                            last = pe.matmul(PS[:, 2 * (n % 4) + h, :], y[:, k, n * P:(n + 1) * P], w[:, k, 512 * h:512 * h + 512],
                                             start=(k == 0), stop=(k == n_k - 1))
                    last.then_inc(s["prod"], 1)

            @block.vector
            def _(dve):
                step = Steps(dve, s["step"])
                dve.memset(eps[:], EPS_LN).then_inc(s["eps_ok"], 1)
                dve.wait_ge(s["row_in"], 48)
                for n, t in enumerate(tiles):
                    i = n % 2
                    gt = gate[:, 1 if (layer == 0 and t < CTXCH) else 0]
                    dve.wait_ge(s["prod"], n + 1)
                    if n >= 2:
                        dve.wait_ge(s["normed"], n - 1)
                    step.link(dve.tensor_tensor(r[:, i], PS[:, 2 * (n % 4):2 * (n % 4) + 2, :].rearrange("p a b -> p (a b)"), gt, ALU.mult))
                    dve.wait_ge(x_in[n % 3], 16 * (n // 3 + 1))
                    step.publish(dve.scalar_tensor_tensor(r[:, i], x[:, n % 3], ALPHA, r[:, i], ALU.mult, ALU.add), s["summed"], n + 1)
                    for h in range(2):
                        step.add(dve.bn_stats(st[:, i, h], r[:, i, 512 * h:512 * h + 512]))
                    step.wait()
                    step.publish(dve.bn_aggr(mv[:, i], st[:, i].rearrange("p a b -> p (a b)")), s["mean_ok"], n + 1)
                    dve.wait_ge(s["root"], n + 1)
                    step.link(dve.reciprocal(rstd[:, i, 0:1], rstd[:, i, 0:1]))
                    step.link(dve.scalar_tensor_tensor(rstd[:, i, 1:2], mv[:, i, 0:1], -1.0, rstd[:, i, 0:1], ALU.mult, ALU.mult))
                    if n >= ring:
                        dve.wait_ge(stored[n % 2], 16 * (n // 2))
                    dve.tensor_scalar(xnew[:, n % ring], r[:, i], rstd[:, i, 0:1], rstd[:, i, 1:2], ALU.mult, ALU.add).then_inc(s["normed"], 1)

            @block.scalar
            def _(act):
                act.wait_ge(s["eps_ok"], 1)
                for n in range(len(tiles)):
                    act.wait_ge(s["mean_ok"], n + 1)
                    if n >= 2:
                        act.wait_ge(s["normed"], n - 1)
                    act.activation(rstd[:, n % 2, 0:1], mv[:, n % 2, 1:2], ACT.Sqrt, bias=eps[:]).then_inc(s["root"], 1)

            @block.gpsimd
            def _(pool):
                pool.wait_ge(s["row_in"], 48)
                for n in range(len(tiles)):
                    pool.wait_ge(s["normed"], n + 1)
                    pool.tensor_tensor(xnew[:, n % ring], xnew[:, n % ring], ln[:, 0], ALU.mult).then_inc(s["scaled"], 1)
                    pool.wait_ge(s["scaled"], n + 1)
                    pool.tensor_tensor(xnew[:, n % ring], xnew[:, n % ring], ln[:, 1], ALU.add).then_inc(s["added"], 1)


PADW = GRID_W + 2


def mlstm_inputs(nc, A, G, B):
    TILES = NT1 // HEADS1
    with ExitStack() as ctx:
        def sb(n, s, t=F32):
            return ctx.enter_context(nc.sbuf_tensor(n, s, t))
        free = B.xnew[:].rearrange("p c d -> p (c d)")
        sizes = np.cumsum([0, 4 * KT * P, 2 * T, 2 * SEQ, T]).tolist()
        w, v, sz, acc = (free[:, a:b] for a, b in zip(sizes, sizes[1:]))
        w = w.rearrange("p (i j k n) -> p i j k n", i=2, j=2, k=KT)
        v = v.rearrange("p (i c n) -> p i c n", i=2, c=NCH)
        sz = sz.rearrange("p (i t) -> p i t", i=2)
        wh = [sb(f"w_in1_hi{i}", [P, 2, KT, P], F32R) for i in range(2)]
        wl = [sb(f"w_in1_lo{i}", [P, 2, KT, P], F32R) for i in range(2)]
        cols = sb("tile_cols", [P, TILES, TILE_PARAMS])
        wqkv = sb("wqkv", [P, TILES, 3, 4])
        wg = sb("w_gates", [P, TILES, 3, 4, 4])
        BD, BDT = sb("BD", [P, 2, 3, P]), sb("BDT", [P, 2, 3, P])
        BQK = sb("BQK", [P, 2, P])
        WG = sb("WG", [P, 2, 2, P])
        xm, xc = sb("xm", [P, 2, T]), sb("xc", [P, 2, T])
        padl, padc = sb("padl", [P, ROWS + 2, PADW]), sb("padc", [P, CTX + 2])
        q = sb("q_out", [P, 2, SEQ])
        PS = G.PS
        win = A.p["o_w_in"][0].rearrange("(k p) n -> p k n", p=P)

        def load_w(sp, r, t, sem):
            for j in range(2):
                sp.dma_start(w[:, t % 2, j], win[:, :, bass.ds(r * (TILES * P) + (t * P + j * INNER), P)]).then_inc(sem, 16)

        def load_maps(eng, r, sem):
            for t in range(TILES):
                at = r * (TILES * P) + t * P
                for j, n in enumerate(("ml_wq", "ml_wk", "ml_wv")):
                    eng.dma_start(wqkv[:, t, j], A.p[n][0].rearrange("j c d -> (j c) d")[bass.ds(at, P)]).then_inc(sem, 16)
                for j, n in enumerate(("ml_wi_f", "ml_wf_f", "ml_wi_b", "ml_wf_b")):
                    src = A.p[n][0].rearrange("(a r) h -> r a h", a=3)
                    eng.dma_start(wg[:, t, :, j], src[bass.ds(at, P)]).then_inc(sem, 16)

        def load_cols(eng, r, sem):
            eng.dma_start(cols[:], A.cols1_d[bass.ds(r * TILES, TILES)].rearrange("i p j -> p i j")).then_inc(sem, 16)

        def high_part(eng, i, src=None):
            return eng.activation(wh[i][:], w[:, i] if src is None else src, ACT.Copy)

        def low_part(eng, i, src=None):
            return eng.tensor_tensor(wl[i][:], w[:, i] if src is None else src, wh[i][:].bitcast(F32), ALU.subtract)

        w_first = q[:].rearrange("p i t -> p (i t)").rearrange("p (j k n) -> p j k n", j=2, k=KT)

        def first_loads(sp, sem, small):
            for j in range(2):
                sp.dma_start(w_first[:, j], win[:, :, j * INNER:j * INNER + P]).then_inc(sem, 16)
            load_maps(sp, 0, small)
            load_cols(sp, 0, small)
            return 7 * TILES + 1

        full = xm[:].rearrange("p i t -> p (i t)")[:, 0:4 * 512].rearrange("p (i t) -> p i t", i=4)
        modulate_split(nc, G, 1, B.xnew, G.hT_hi, G.hT_lo, full, first_loads,
                       lambda act: high_part(act, 0, w_first), lambda pool: low_part(pool, 0, w_first))

        with phase(nc, "zero w_in") as (block, s):
            @block.sync
            def _(sp):
                load_w(sp, 0, 1, s["w_in"])
                sp.wait_ge(s["w_in"], 32)

            @block.vector
            def _(dve):
                dve.memset(B.gates[:], 0.0)
                dve.memset(padl[:].rearrange("p a b -> p (a b)"), 0.0)
                dve.memset(padc[:], 0.0)
                dve.memset(WG[:], 0.0).then_inc(s["zero"], 1)

        def head_round(r, more):
            n_w = TILES + (2 if more else 0)
            sems = ("cols_in w_in0 w_in1 hi_ok lo_ok small_in bd_ok bdt_ps bdt_sb fold_ps fold_sb bqk_sb xm_ps xm_sb padded "
                    "z_ps z_sb conv_ok xc_ok q_ps q_sb v_ps v_sb gate_ps gate_sb step stored0 stored1")
            with phase(nc, sems) as (block, s):
                w_in, stored = [s["w_in0"], s["w_in1"]], [s["stored0"], s["stored1"]]

                @block.sync
                def _(sp):
                    def dst(x, t):
                        return x[bass.ds(r * TILES + t, 1)].rearrange("o p t -> p (o t)")

                    for t in range(TILES):
                        if t + 2 < n_w:
                            if t:
                                sp.wait_ge(s["hi_ok"], t)
                                sp.wait_ge(s["lo_ok"], t)
                            load_w(sp, r, t + 2, w_in[t % 2])
                        sp.wait_ge(s["z_sb"], t + 1)
                        sp.dma_start(dst(B.sz_d, t), sz[:, t % 2]).then_inc(stored[t % 2], 16)
                        sp.wait_ge(s["v_sb"], 3 * t + 3)
                        sp.dma_start(B.v_d[bass.ds(r * TILES + t, 1)].rearrange("o p c n -> p (o c) n"), v[:, t % 2]).then_inc(stored[t % 2], 16)
                        sp.wait_ge(s["xc_ok"], t + 1)
                        sp.dma_start(dst(B.k_d, t), xc[:, t % 2]).then_inc(stored[t % 2], 16)
                        sp.wait_ge(s["q_sb"], t + 1)
                        sp.dma_start(dst(B.q_d, t), q[:, t % 2]).then_inc(stored[t % 2], 16)
                    if more:
                        sp.wait_ge(s["conv_ok"], TILES)
                        load_cols(sp, r + 1, s["cols_in"])
                        sp.wait_ge(s["cols_in"], 16)
                        sp.wait_ge(s["small_in"], TILES * 7 * 16)
                        for i in range(2):
                            sp.wait_ge(w_in[i], 32 * (TILES // 2))
                    for i in range(2):
                        sp.wait_ge(stored[i], TILES // 2 * 4 * 16)

                @block.tensor
                def _(pe):
                    def x_part(t):
                        i = t % 2
                        pe.wait_ge(s["bd_ok"], t + 1)
                        if t:
                            pe.wait_ge(s["v_sb"], 3 * t)
                            pe.wait_ge(s["xm_sb"], t)
                            pe.wait_ge(s["padded"], t)
                        for j in range(3):
                            last = pe.transpose(PS[:, 7, j * P:(j + 1) * P], BD[:, i, j], G.c("ident"))
                        last.then_inc(s["bdt_ps"], 1)
                        if t:
                            pe.wait_ge(s["hi_ok"], t)
                            pe.wait_ge(s["lo_ok"], t)
                        project_split(pe, PS, 0, wh[i][:, 0], wl[i][:, 0], G.hT_hi, G.hT_lo, PIECES).then_inc(s["xm_ps"], 1)
                        pe.wait_ge(s["bdt_sb"], t + 1)
                        g = [wg[:, t, j].rearrange("p a b -> p (a b)") for j in range(3)]
                        pe.matmul(PS[:, 7, 0:16], BDT[:, i, 0], g[0], start=True, stop=False)
                        pe.matmul(PS[:, 7, 0:16], BDT[:, i, 1], g[1], start=False, stop=True)
                        pe.matmul(PS[:, 7, 16:32], BDT[:, i, 2], g[2], start=True, stop=True)
                        pe.matmul(PS[:, 7, P:2 * P], BDT[:, i, 0], BDT[:, i, 1], start=True, stop=True).then_inc(s["fold_ps"], 1)

                    def z_part(t):
                        i = t % 2
                        if t:
                            pe.wait_ge(s["q_sb"], t)
                        project_split(pe, PS, 3, wh[i][:, 1], wl[i][:, 1], G.hT_hi, G.hT_lo, [(0, 512), (512, 512)], at=CTX).then_inc(s["z_ps"], 1)
                        pe.wait_ge(s["xm_sb"], t + 1)
                        pe.wait_ge(s["fold_sb"], t + 1)
                        pe.wait_ge(s["bqk_sb"], t + 1)
                        if t:
                            pe.wait_ge(s["gate_sb"], t)
                        for c in range(NCH):
                            last = pe.matmul(PS[:, 5 + c // 4, (c % 4) * P:(c % 4 + 1) * P], xm[:, i, c * CH:(c + 1) * CH], BD[:, i, 2],
                                             start=True, stop=True)
                            if c in (3, 7, 9):
                                last.then_inc(s["v_ps"], 1)

                    def q_part(t):
                        i = t % 2
                        pe.wait_ge(s["xc_ok"], t + 1)
                        pe.wait_ge(s["z_sb"], t + 1)
                        for off in (0, 512):
                            last = pe.matmul(PS[:, 3 + off // 512, :], BQK[:, i], xc[:, i, CTX + off:CTX + off + 512], start=True, stop=True)
                        last.then_inc(s["q_ps"], 1)
                        pe.wait_ge(s["v_sb"], 3 * t + 3)
                        if t + 1 < TILES:
                            pe.wait_ge(s["fold_sb"], t + 2)
                            pe.wait_ge(s["bqk_sb"], t + 2)
                        for off, m in PIECES:
                            pe.matmul(PS[:, 5 + off // 512, 0:m], WG[:, i, 0], xc[:, i, off:off + m], start=True, stop=False)
                            last = pe.matmul(PS[:, 5 + off // 512, 0:m], WG[:, i, 1], xm[:, i, off:off + m], start=False, stop=True)
                        last.then_inc(s["gate_ps"], 1)

                    x_part(0)
                    z_part(0)
                    for t in range(TILES):
                        if t + 1 < TILES:
                            x_part(t + 1)
                        q_part(t)
                        if t + 1 < TILES:
                            z_part(t + 1)

                @block.scalar
                def _(act):
                    def high(t):
                        if t >= 2:
                            act.wait_ge(w_in[t % 2], 32 * (t // 2))
                            act.wait_ge(s["z_ps"], t - 1)
                        high_part(act, t % 2).then_inc(s["hi_ok"], 1)

                    def x_out(t):
                        i = t % 2
                        act.wait_ge(s["xm_ps"], t + 1)
                        if t:
                            act.wait_ge(s["conv_ok"], t)
                        act.activation(padl[:, 1:ROWS + 1, 1:GRID_W + 1], flat(PS, 0)[:, CTX:].rearrange("p (r w) -> p r w", w=GRID_W), ACT.Copy)
                        act.activation(padc[:, 1:CTX + 1], flat(PS, 0)[:, 0:CTX], ACT.Copy).then_inc(s["padded"], 1)
                        if t >= 2:
                            act.wait_ge(s["gate_ps"], t - 1)
                        act.activation(xm[:, i], flat(PS, 0), ACT.Copy).then_inc(s["xm_sb"], 1)

                    def turn(t):
                        act.wait_ge(s["bdt_ps"], t + 1)
                        act.activation(BDT[:, t % 2].rearrange("p a b -> p (a b)"), PS[:, 7, 0:3 * P], ACT.Copy).then_inc(s["bdt_sb"], 1)

                    turn(0)
                    x_out(0)
                    for t in range(TILES):
                        i = t % 2
                        if t + 1 < TILES or more:
                            high(t + 1)
                        act.wait_ge(s["z_ps"], t + 1)
                        if t >= 2:
                            act.wait_ge(stored[i], t // 2 * 4 * 16)
                        act.activation(sz[:, i], flat(PS, 3)[:, 0:SEQ], ACT.Silu).then_inc(s["z_sb"], 1)
                        for j in range(3):
                            m = 4 if j < 2 else 2
                            act.wait_ge(s["v_ps"], 3 * t + j + 1)
                            act.activation(v[:, i, 4 * j:4 * j + m].rearrange("p c n -> p (c n)"), PS[:, 5 + j, 0:m * P], ACT.Copy).then_inc(s["v_sb"], 1)
                        if t + 1 < TILES:
                            turn(t + 1)
                        act.wait_ge(s["conv_ok"], t + 1)
                        act.activation(xc[:, i], acc, ACT.Silu).then_inc(s["xc_ok"], 1)
                        if t + 1 < TILES:
                            x_out(t + 1)
                        act.wait_ge(s["q_ps"], t + 1)
                        act.activation(q[:, i], flat(PS, 3)[:, 0:SEQ], ACT.Copy, scale=float(DH) ** -0.5).then_inc(s["q_sb"], 1)
                        if more and t == TILES - 2:
                            act.wait_ge(s["bd_ok"], TILES)
                            act.wait_ge(s["fold_ps"], TILES)
                            load_maps(act, r + 1, s["small_in"])

                @block.gpsimd
                def _(pool):
                    for t in range(1, TILES + more):
                        pool.wait_ge(s["hi_ok"], t)
                        if t >= 2:
                            pool.wait_ge(s["z_ps"], t - 1)
                        low_part(pool, t % 2).then_inc(s["lo_ok"], 1)

                @block.vector
                def _(dve):
                    step = Steps(dve, s["step"])

                    def maps(t):
                        if t >= 2:
                            dve.wait_ge(s["v_ps"], 3 * (t - 1))
                        for j in range(3):
                            last = dve.tensor_tensor(BD[:, t % 2, j].rearrange("p (a b) -> p a b", b=4), wqkv[:, t, j:j + 1, :].broadcast_to([P, 32, 4]),
                                                     G.c("block4").rearrange("p (a b) -> p a b", b=4), ALU.mult)
                        last.then_inc(s["bd_ok"], 1)

                    def folds(t):
                        dve.wait_ge(s["fold_ps"], t + 1)
                        if t >= 2:
                            dve.wait_ge(s["gate_ps"], t - 1)
                        for j in range(2):
                            dst = WG[:, t % 2, j].rearrange("p (a b) -> p a b", b=32)[:, :, 0:4]
                            last = dve.tensor_copy(dst, PS[:, 7, 16 * j:16 * j + 16].rearrange("p (a b) -> p a b", b=4))
                        last.then_inc(s["fold_sb"], 1)
                        dve.tensor_copy(BQK[:, t % 2], PS[:, 7, P:2 * P]).then_inc(s["bqk_sb"], 1)

                    maps(0)
                    folds(0)
                    for t in range(TILES):
                        if t + 1 < TILES:
                            maps(t + 1)
                        dve.wait_ge(s["padded"], t + 1)
                        if t:
                            dve.wait_ge(s["xc_ok"], t)
                        col = [cols[:, t, j:j + 1] for j in range(TILE_PARAMS)]
                        lat = acc[:, CTX:].rearrange("p (r w) -> p r w", w=GRID_W)
                        step.add(dve.tensor_scalar(lat, padl[:, 0:ROWS, 0:GRID_W], col[0], col[9], ALU.mult, ALU.add))
                        step.link(dve.tensor_scalar(acc[:, 0:CTX], padc[:, 0:CTX], col[3], col[9], ALU.mult, ALU.add))
                        for tap in range(1, 9):
                            a, b = tap // 3, tap % 3
                            if tap in (4, 5):
                                step.add(dve.scalar_tensor_tensor(acc[:, 0:CTX], padc[:, b:b + CTX], col[tap], acc[:, 0:CTX], ALU.mult, ALU.add))
                            ins = dve.scalar_tensor_tensor(lat, padl[:, a:a + ROWS, b:b + GRID_W], col[tap], lat, ALU.mult, ALU.add)
                            if tap == 8:
                                ins.then_inc(s["conv_ok"], 1)
                            else:
                                step.link(ins)
                        if t + 1 < TILES:
                            folds(t + 1)
                        dve.wait_ge(s["gate_ps"], t + 1)
                        if t:
                            dve.wait_ge(s["gate_sb"], t)
                        dve.tensor_tensor(B.gates[:], flat(PS, 5), B.gates[:], ALU.add).then_inc(s["gate_sb"], 1)

        with nc.Fori(0, HEADS1 - 1) as r:
            head_round(r, True)
        head_round(HEADS1 - 1, False)


def mlstm_gates(nc, A, G, B):
    with ExitStack() as ctx:
        def sb(n, s):
            return ctx.enter_context(nc.sbuf_tensor(n, s, F32))
        bias = sb("gate_bias", [P, 1])
        x, l = sb("gate_x", [P, T]), sb("gate_l", [P, T])
        F_, a, M, m = [sb(n, [P, T]) for n in ("gate_F", "gate_a", "gate_M", "gate_m")]
        unit = sb("unit", [P, T])
        colsb = sb("gate_cols", [P, 2, NCH, HEADS1, 2])
        PS = G.PS
        with phase(nc, "zero bias_in x_ok l_ok step rows_ok turned0 turned1 cols_ok stored act_step") as (block, s):
            @block.sync
            def _(sp):
                sp.wait_ge(s["zero"], 1)
                for j, n in enumerate(("ml_bi_f", "ml_bf_f", "ml_bi_b", "ml_bf_b")):
                    sp.dma_start(bias[32 * j:32 * j + 4], A.p[n][0].rearrange("(p o) -> p o", o=1)).then_inc(s["bias_in"], 16)
                sp.wait_ge(s["rows_ok"], 1)
                for d in range(2):
                    sp.dma_start(B.M_d[:, d], M[64 * d:64 * d + 4, CTX:]).then_inc(s["stored"], 16)
                sp.wait_ge(s["cols_ok"], 2)
                for h in range(HEADS1):
                    sp.dma_start(B.cols_d[h], colsb[:, :, :, h]).then_inc(s["stored"], 16)
                sp.wait_ge(s["stored"], 6 * 16)

            @block.scalar
            def _(act):
                step = Steps(act, s["act_step"])
                act.wait_ge(s["x_ok"], 1)
                step.link(act.activation(l[:], x[:], ACT.Abs))
                step.link(act.activation(l[:], l[:], ACT.Exp, scale=-1.0))
                act.activation(l[:], l[:], ACT.Ln, bias=G.c("ones")[:, 0:1]).then_inc(s["l_ok"], 1)

            @block.vector
            def _(dve):
                step = Steps(dve, s["step"])
                dve.memset(bias[:], 0.0).then_inc(s["zero"], 1)
                step.add(dve.memset(unit[:], 1.0))
                step.add(dve.memset(a[:], 0.0))
                step.add(dve.memset(M[:], 0.0))
                step.add(dve.memset(m[:], 0.0))
                step.link(dve.memset(F_[:], 0.0))
                dve.wait_ge(s["bias_in"], 64)
                step.publish(dve.tensor_scalar(x[:], B.gates[:], bias[:], None, ALU.add), s["x_ok"], 1)
                dve.wait_ge(s["l_ok"], 1)
                step.link(dve.scalar_tensor_tensor(l[:], x[:], 0.0, l[:], ALU.min, ALU.subtract))
                for d in range(2):
                    r, f = slice(64 * d, 64 * d + 4), slice(64 * d + 32, 64 * d + 36)

                    def scan(out, in0, in1, first, op0, op1):
                        for lo, hi, prev in ((0, CTX, None), (CTX, T, CTX - 1 if d == 0 else 0)):
                            ini = first if prev is None else out[:, prev:prev + 1]
                            v = [z[:, lo:hi] if d == 0 else z[:, lo:hi][:, ::-1] for z in (out, in0, in1)]
                            step.link(dve.tensor_tensor_scan(v[0], v[1], v[2], ini, op0, op1))

                    step.link(dve.tensor_copy(m[r], l[f]))
                    scan(F_[r], unit[r], m[r], 0.0, ALU.mult, ALU.add)
                    step.link(dve.tensor_tensor(a[r], x[r], F_[r], ALU.subtract))
                    scan(M[r], a[r], a[r], -3e38, ALU.max, ALU.max)
                    step.link(dve.scalar_tensor_tensor(m[r], F_[r], -1.0, M[r], ALU.mult, ALU.subtract))
                step.publish(dve.tensor_scalar(M[:], M[:], -1.0, None, ALU.mult), s["rows_ok"], 1)
                for j, t in enumerate((s["turned0"], s["turned1"])):
                    for n in range(3):
                        cnt = min(4, NCH - 4 * n)
                        dve.wait_ge(t, n + 1)
                        for d in range(2):
                            src = PS[:, 4 * j + n, 0:cnt * P].rearrange("p (c r) -> p c r", r=P)[:, :, 64 * d:64 * d + 4]
                            last = dve.tensor_copy(colsb[:, d, 4 * n:4 * n + cnt, :, j], src)
                    last.then_inc(s["cols_ok"], 1)

            @block.tensor
            def _(pe):
                pe.wait_ge(s["rows_ok"], 1)
                for j, (src, t) in enumerate(((a, s["turned0"]), (m, s["turned1"]))):
                    for n in range(3):
                        for c in range(4 * n, min(4 * n + 4, NCH)):
                            last = pe.transpose(PS[:, 4 * j + n, (c % 4) * P:(c % 4 + 1) * P], src[:, c * CH:(c + 1) * CH], G.c("ident"))
                        last.then_inc(t, 1)


TQ = SEQ // P
VCOL = [0, P, 2 * P + 2, 3 * P + 2]
SEEN = NCH + CTXCH + 1


def mlstm_heads(nc, A, G, B):
    def uses(d, c):
        return [j for j in range(NCH) if j < CTXCH or (j <= c if d == 0 else j >= c)]

    def slot(d, c, j):
        return j if d == 0 else c + 1 + (j if j < CTXCH else CTXCH + j - c)

    groups = [(0, 4), (4, 4), (8, 2)]
    with ExitStack() as ctx:
        def sb(n, s, t=F32):
            return ctx.enter_context(nc.sbuf_tensor(n, s, t))
        Q, K = sb("Q", [P, 4, SEQ]), sb("K1", [P, 4, T])
        vraw = sb("v_raw", [P, 2, NCH, P])
        VH, VL = sb("V_hi", [P, NCH, 4 * P + 2], F32R), sb("V_lo", [P, NCH, 4 * P + 2], F32R)
        cols, pcol = sb("head_cols", [P, 2, NCH, 2]), sb("head_params", [P, 4, TILE_PARAMS])
        Mrow = sb("M_row", [P, 2, SEQ])
        sx, sz = sb("sx_in", [P, 4, SEQ]), sb("sz_in", [P, 4, SEQ])
        W = sb("weights", [P, 2, SEEN, P])
        WH = [sb(f"weights_hi{i}", [P, SEEN, P], F32R) for i in range(2)]
        WL = [sb(f"weights_lo{i}", [P, SEEN, P], F32R) for i in range(2)]
        dg = sb("diag_arg", [P, 2, 2, P])
        H = sb("H", [P, TQ, DH])
        floor = sb("floor", [P, 2, NCH])
        den = sb("den", [P, 2, 2])
        st, mv, rs = sb("h_stats", [P, 2, 6]), sb("h_mv", [P, TQ, 2]), sb("h_rstd", [P, 2, TQ])
        eps = sb("eps_h", [P, 1])
        PS = G.PS

        def load_qk(sp, h, sem):
            for kt in range(4):
                sp.dma_start(K[:, kt], B.k_d[bass.ds(h * 4 + kt, 1)].rearrange("o p t -> p (o t)")).then_inc(sem, 16)
                sp.dma_start(Q[:, kt], B.q_d[bass.ds(h * 4 + kt, 1)].rearrange("o p t -> p (o t)")).then_inc(sem, 16)

        def load_rows(sp, h, sem):
            sp.dma_start(Mrow[:].rearrange("p d t -> p (d t)"),
                         B.M_d[bass.ds(h, 1)].rearrange("o d t -> o (d t)").broadcast_to([P, 2 * SEQ])).then_inc(sem, 16)
            sp.dma_start(cols[:], B.cols_d[bass.ds(h, 1)].rearrange("o p d c j -> p (o d) c j")).then_inc(sem, 16)

        with phase(nc, "ones_ok in_ok") as (block, s):
            @block.vector
            def _(dve):
                ones = G.c("ones")[:, 0:2 * NCH].rearrange("p (c n) -> p c n", n=2)
                dve.tensor_copy(VH[:, :, 2 * P:2 * P + 2], ones)
                dve.tensor_tensor(VL[:, :, 2 * P:2 * P + 2], ones, ones, ALU.subtract)
                dve.memset(eps[:], EPS_LN).then_inc(s["ones_ok"], 1)

            @block.sync
            def _(sp):
                load_rows(sp, 0, s["in_ok"])
                load_qk(sp, 0, s["in_ok"])
                sp.wait_ge(s["in_ok"], 10 * 16)

        def head_round(h, more):
            sems = ("cols_in qk_in v_in0 v_in1 v_hi v_lo w_hi w_lo row_in skip_in scored weighted d_ok diag_ok floor_ok av_ps av_sb mean_ok root normed "
                    "turned skip_ok y_half y_ok step stored taken")
            with phase(nc, sems) as (block, s):
                v_in = [s["v_in0"], s["v_in1"]]

                @block.sync
                def _(sp):
                    sp.dma_start(pcol[:], A.cols1_d[bass.ds(h * 4, 4)].rearrange("k p j -> p k j")).then_inc(s["cols_in"], 16)
                    for kt in range(4):
                        if kt >= 2:
                            sp.wait_ge(s["v_hi"], kt - 1)
                            sp.wait_ge(s["v_lo"], kt - 1)
                        sp.dma_start(vraw[:, kt % 2], B.v_d[bass.ds(h * 4 + kt, 1)].rearrange("o p c n -> p (o c) n")).then_inc(v_in[kt % 2], 16)
                    sp.dma_start(sz[:], B.sz_d[bass.ds(h * 4, 4)].rearrange("k p t -> p k t")).then_inc(s["skip_in"], 16)
                    if more:
                        sp.wait_ge(s["scored"], 3 * TQ)
                        sp.wait_ge(s["skip_ok"], 4)
                        load_qk(sp, h + 1, s["qk_in"])
                    for kt in range(4):
                        sp.wait_ge(s["y_ok"], 4 + kt + 1)
                        sp.dma_start(B.y_d[bass.ds(h * 4 + kt, 1)].rearrange("o p t -> p (o t)"), sx[:, kt]).then_inc(s["stored"], 16)
                    if more:
                        sp.wait_ge(s["row_in"], 32)
                        sp.wait_ge(s["qk_in"], 128)
                    sp.wait_ge(s["stored"], 64)

                @block.tensor
                def _(pe):
                    def scores(i):
                        for g, (j0, m) in enumerate(groups):
                            n = 3 * i + g
                            if n >= 4:
                                pe.wait_ge(s["weighted"], n - 3)
                            for j in range(j0, j0 + m):
                                for kt in range(4):
                                    last = pe.matmul(PS[:, 4 + n % 4, (j - j0) * P:(j - j0 + 1) * P], K[:, kt, j * P:(j + 1) * P],
                                                     Q[:, kt, i * P:(i + 1) * P], start=(kt == 0), stop=(kt == 3))
                            last.then_inc(s["scored"], 1)

                    def turn(half):
                        pe.wait_ge(s["normed"], 4 * half + 4)
                        for kt in range(4):
                            if half:
                                pe.wait_ge(s["y_half"], kt + 1)
                            for i in range(4):
                                last = pe.transpose(PS[:, 4 + kt, i * P:(i + 1) * P], H[:, 4 * half + i, kt * P:(kt + 1) * P], G.c("ident"))
                            last.then_inc(s["turned"], 1)

                    scores(0)
                    pe.wait_ge(s["v_hi"], 4)
                    pe.wait_ge(s["v_lo"], 4)
                    for i in range(TQ):
                        if i + 1 < TQ:
                            scores(i + 1)
                        if i == TQ - 1:
                            pe.wait_ge(s["weighted"], 3 * TQ)
                            turn(0)
                        pe.wait_ge(s["w_hi"], i + 1)
                        pe.wait_ge(s["w_lo"], i + 1)
                        if i:
                            pe.wait_ge(s["av_sb"], i)
                        for d in range(2):
                            seen = uses(d, i + CTXCH)
                            for j in seen:
                                wh, wl = (x[i % 2][:, slot(d, i + CTXCH, j)] for x in (WH, WL))
                                for half, q in enumerate((slice(0, 2 * P + 2), slice(2 * P + 2, 4 * P + 2))):
                                    out = PS[:, 2 * d + half, 0:q.stop - q.start]
                                    pe.matmul(out, wh, VH[:, j, q], start=(j == seen[0]), stop=False)
                                    pe.matmul(out, wh, VL[:, j, q], start=False, stop=False)
                                    last = pe.matmul(out, wl, VH[:, j, q], start=False, stop=(j == seen[-1]))
                        last.then_inc(s["av_ps"], 1)
                    turn(1)

                @block.scalar
                def _(act):
                    def root(half):
                        act.wait_ge(s["mean_ok"], 4 * half + 4)
                        t = slice(4 * half, 4 * half + 4)
                        act.activation(rs[:, 0, t], mv[:, t, 1], ACT.Sqrt, bias=eps[:]).then_inc(s["root"], 1)

                    act.activation(floor[:], cols[:, :, :, 1], ACT.Exp).then_inc(s["floor_ok"], 1)
                    def decay(i):
                        c = i + CTXCH
                        if i >= 2:
                            act.wait_ge(s["w_lo"], i - 1)
                        act.wait_ge(s["diag_ok"], 2 * i + 2)
                        for d in range(2):
                            for j in uses(d, c):
                                arg = dg[:, i % 2, d] if j == c else Mrow[:, d, i * P:(i + 1) * P]
                                last = act.activation(W[:, i % 2, slot(d, c, j)], arg, ACT.Exp, bias=cols[:, d, j, 0:1])
                        last.then_inc(s["d_ok"], 1)

                    def high(i):
                        act.wait_ge(s["weighted"], 3 * i + 3)
                        if i >= 2:
                            act.wait_ge(s["av_ps"], i - 1)
                        act.activation(WH[i % 2][:], W[:, i % 2], ACT.Copy).then_inc(s["w_hi"], 1)

                    decay(0)
                    for kt in range(4):
                        act.wait_ge(v_in[kt % 2], 16 * (kt // 2 + 1))
                        act.activation(VH[:, :, VCOL[kt]:VCOL[kt] + P], vraw[:, kt % 2], ACT.Copy).then_inc(s["v_hi"], 1)
                    for i in range(TQ - 1):
                        decay(i + 1)
                        high(i)
                    root(0)
                    if more:
                        act.wait_ge(s["floor_ok"], 1)
                        act.wait_ge(s["d_ok"], TQ)
                        load_rows(act, h + 1, s["row_in"])
                    high(TQ - 1)
                    root(1)

                @block.gpsimd
                def _(pool):
                    for i in range(TQ):
                        pool.wait_ge(s["w_hi"], i + 1)
                        if i >= 2:
                            pool.wait_ge(s["av_ps"], i - 1)
                        pool.tensor_tensor(WL[i % 2][:], W[:, i % 2], WH[i % 2][:].bitcast(F32), ALU.subtract).then_inc(s["w_lo"], 1)

                @block.vector
                def _(dve):
                    step = Steps(dve, s["step"])

                    def diag(i):
                        if i >= 2:
                            dve.wait_ge(s["d_ok"], i - 1)
                        for d in range(2):
                            dve.tensor_tensor(dg[:, i % 2, d], G.c("neg")[:, d * P:(d + 1) * P], Mrow[:, d, i * P:(i + 1) * P],
                                              ALU.add).then_inc(s["diag_ok"], 1)

                    dve.wait_ge(s["floor_ok"], 1)
                    diag(0)
                    dve.wait_ge(s["cols_in"], 16)
                    for kt in range(4):
                        dve.tensor_scalar(sx[:, kt], K[:, kt, CTX:], pcol[:, kt, 11:12], None, ALU.mult).then_inc(s["skip_ok"], 1)
                    def weigh(i):
                        c = i + CTXCH
                        dve.wait_ge(s["d_ok"], i + 1)
                        for g, (j0, m) in enumerate(groups):
                            n = 3 * i + g
                            dve.wait_ge(s["scored"], n + 1)
                            for d in range(2):
                                js = [j for j in uses(d, c) if j0 <= j < j0 + m]
                                runs = []
                                for j in js:
                                    if runs and runs[-1][1] == j:
                                        runs[-1][1] = j + 1
                                    else:
                                        runs.append([j, j + 1])
                                for a, b in runs:
                                    w = W[:, i % 2, slot(d, c, a):slot(d, c, a) + b - a]
                                    last = dve.tensor_tensor(w, PS[:, 4 + n % 4, (a - j0) * P:(b - j0) * P].rearrange("p (j t) -> p j t", t=P), w, ALU.mult)
                            last.then_inc(s["weighted"], 1)

                    def collect(i):
                        c = i + CTXCH
                        dve.wait_ge(s["av_ps"], i + 1)
                        for d in range(2):
                            step.add(dve.scalar_tensor_tensor(den[:, d, 0:1], PS[:, 2 * d, 2 * P:2 * P + 1], -1.0, floor[:, d, c:c + 1],
                                                              ALU.mult, ALU.max))
                        step.wait()
                        for d in range(2):
                            step.add(dve.tensor_tensor(den[:, d, 0:1], PS[:, 2 * d, 2 * P:2 * P + 1], den[:, d, 0:1], ALU.max))
                        step.wait()
                        for d in range(2):
                            step.add(dve.reciprocal(den[:, d, 1:2], den[:, d, 0:1]))
                        step.wait()
                        for half in range(2):
                            step.add(dve.tensor_scalar(H[:, i, 2 * P * half:2 * P * half + 2 * P], PS[:, half, 0:2 * P], den[:, 0, 1:2], None, ALU.mult))
                        step.wait()
                        for half in range(2):
                            hh = H[:, i, 2 * P * half:2 * P * half + 2 * P]
                            ins = dve.scalar_tensor_tensor(hh, PS[:, 2 + half, 0:2 * P], den[:, 1, 1:2], hh, ALU.mult, ALU.add)
                            if half:
                                step.publish(ins, s["av_sb"], i + 1)
                            else:
                                step.add(ins)
                        step.link(dve.bn_stats(st[:, i % 2], H[:, i]))
                        dve.bn_aggr(mv[:, i], st[:, i % 2]).then_inc(s["mean_ok"], 1)

                    def normalize(half):
                        t = slice(4 * half, 4 * half + 4)
                        dve.wait_ge(s["root"], half + 1)
                        step.link(dve.reciprocal(rs[:, 0, t], rs[:, 0, t]))
                        step.link(dve.scalar_tensor_tensor(rs[:, 1, t], mv[:, t, 0], -1.0, rs[:, 0, t], ALU.mult, ALU.mult))
                        for i in range(4 * half, 4 * half + 4):
                            dve.tensor_scalar(H[:, i], H[:, i], rs[:, 0, i:i + 1], rs[:, 1, i:i + 1], ALU.mult, ALU.add).then_inc(s["normed"], 1)

                    def finish(half):
                        t = slice(4 * P * half, 4 * P * (half + 1))
                        for kt in range(4):
                            dve.wait_ge(s["turned"], 4 * half + kt + 1)
                            dve.scalar_tensor_tensor(sx[:, kt, t], PS[:, 4 + kt, :], pcol[:, kt, 10:11], sx[:, kt, t],
                                                     ALU.mult, ALU.add).then_inc(s["y_half"], 1)
                        for kt in range(4):
                            dve.wait_ge(s["y_half"], 4 * half + kt + 1)
                            dve.tensor_tensor(sx[:, kt, t], sx[:, kt, t], sz[:, kt, t], ALU.mult).then_inc(s["y_ok"], 1)

                    diag(1)
                    for kt in range(4):
                        q = slice(VCOL[kt], VCOL[kt] + P)
                        dve.wait_ge(s["v_hi"], kt + 1)
                        dve.tensor_tensor(VL[:, :, q], vraw[:, kt % 2], VH[:, :, q].bitcast(F32), ALU.subtract).then_inc(s["v_lo"], 1)
                    weigh(0)
                    for i in range(TQ):
                        if i + 1 < TQ:
                            weigh(i + 1)
                        if i + 2 < TQ:
                            diag(i + 2)
                        if i == TQ - 2:
                            normalize(0)
                        if i == TQ - 1:
                            dve.wait_ge(s["skip_in"], 16)
                            dve.wait_ge(s["skip_ok"], 4)
                            finish(0)
                        collect(i)
                    normalize(1)
                    finish(1)

        with nc.Fori(0, HEADS1 - 1) as h:
            head_round(h, True)
        head_round(HEADS1 - 1, False)


def build(nc, inputs, out):
    A = Names()
    A.p = inputs
    A.x, A.ctx, A.mod_w, A.consts = inputs["x"], inputs["ctx"], inputs["mod_w"], inputs["consts"]

    def scratch(name, shape):
        return nc.dram_tensor(name, shape, F32, kind="Internal").ap()

    A.gates_d = scratch("gates_d", (3, P, D))
    A.cols0_d = scratch("cols0_d", (4, P, NPAIR))
    A.cols1_d = scratch("cols1_d", (NT1, P, TILE_PARAMS))
    A.lg_d = scratch("lg_d", (32, T))
    A.yT_d = scratch("yT_d", (KT, P, T))
    A.x1_d = scratch("x1_d", (NCH, P, D))
    at, ends = const_layout()
    with ExitStack() as ctx:
        def sb(n, s):
            return ctx.enter_context(nc.sbuf_tensor(n, s, F32))
        G = Names()
        G.count = 0
        G.PS = ctx.enter_context(nc.psum_tensor("PS", [P, 8, 512], F32))
        G.ends = ends
        G.cst = sb("cst", [P, ends[0]])

        def const(name):
            a, b = at[name]
            if b <= ends[0]:
                return G.cst[:, a:b]
            if b <= ends[1]:
                return G.cst0[:, a - ends[0]:b - ends[0]]
            return G.cst_rwkv[:, a - ends[1]:b - ends[1]]

        G.c = const
        G.vc = sb("vc", [P, P])
        G.modc = sb("modc", [P, 2, 16, 2])
        B = Names()
        with nc.sbuf_tensor("hT", [P, KT, T], F32) as hT, nc.sbuf_tensor("rt", [P, 2, T], F32) as rt:
            G.hT = hT
            w_lr = rt[:].rearrange("p d t -> p (d t)")[:, 0:KT * (32 + 256)].rearrange("p (k n) -> p k n", k=KT)
            G.ahead = rt[:, 1]
            with nc.sbuf_tensor("xnat", [P, NCH, D], F32) as xnat:
                setup_phase(nc, A, G, xnat, w_lr)
                modulate_phase(nc, A, G, 0, xnat, hT)
            with nc.sbuf_tensor("cst0", [P, ends[1] - ends[0]], F32) as G.cst0:
                layer0(nc, A, G, w_lr, rt)
        with ExitStack() as c1:
            xnew = c1.enter_context(nc.sbuf_tensor("xnew", [P, NCH, D], F32))

            def x_of(t):
                return (A.ctx if t < CTXCH else A.x)[0, (t % CTXCH if t < CTXCH else t - CTXCH) * P:][:P]
            out_phase(nc, A, G, 0, A.yT_d, A.p["e_w_out"][0], KT, list(range(NCH)), x_of, xnew, lambda t: A.x1_d[t])
            G.hT_hi, G.hT_lo = (c1.enter_context(nc.sbuf_tensor(n, [P, KT, T], F32R)) for n in ("hT_hi", "hT_lo"))
            B.xnew = xnew
            layer1_inputs(nc, A, G, B, scratch)
        mlstm_heads(nc, A, G, B)
        with nc.sbuf_tensor("xlast", [P, 2, D], F32) as xlast:
            out_phase(nc, A, G, 1, B.y_d, A.p["o_w_out"][0], NT1, list(range(CTXCH, NCH)), lambda t: A.x1_d[t], xlast,
                      lambda t: out[0, (t - CTXCH) * P:(t - CTXCH + 1) * P, :])


def layer1_inputs(nc, A, G, B, scratch):
    B.q_d, B.k_d = scratch("q_d", (NT1, P, SEQ)), scratch("k_d", (NT1, P, T))
    B.v_d = scratch("v_d", (NT1, P, NCH, P))
    B.sz_d = scratch("sz_d", (NT1, P, SEQ))
    B.y_d = scratch("y1_d", (NT1, P, SEQ))
    B.M_d, B.cols_d = scratch("M_d", (HEADS1, 2, SEQ)), scratch("hcols_d", (HEADS1, P, 2, NCH, 2))
    with nc.sbuf_tensor("gates1", [P, T], F32) as gates:
        B.gates = gates
        mlstm_inputs(nc, A, G, B)
        mlstm_gates(nc, A, G, B)


def layer0(nc, A, G, w_lr, rt):
    with ExitStack() as c2:
        def sb2(n, s):
            return c2.enter_context(nc.sbuf_tensor(n, s, F32))
        B = Names()
        G.cst_rwkv = sb2("cst_rwkv", [P, G.ends[2] - G.ends[1]])
        B.LW, B.LA = sb2("LW", [P, T]), sb2("LA", [P, T])
        lowrank_phase(nc, A, G, w_lr, B.LW, B.LA)
        with ExitStack() as c3:
            def sb3(n, s):
                return c3.enter_context(nc.sbuf_tensor(n, s, F32))
            B.cols = sb3("pair_cols", [P, NPAIR])
            B.rt = rt
            B.at, B.bt, B.kt = (sb3(n, [P, 2, T]) for n in ("at", "bt", "kt"))
            B.V, B.sG, B.bonus = (sb3(n, [P, T]) for n in ("V", "sG", "bonus"))
            B.PL = sb3("PL", [P, 2, NCH])
            B.mus, B.keep = sb3("mus", [P, 4, 4]), sb3("keep_mu", [P, 4])

            def pair(p, next_at):
                rwkv_prep(nc, A, G, B, p)
                with ExitStack() as c4:
                    def sb4(n, s):
                        return c4.enter_context(nc.sbuf_tensor(fresh(G, n), s, F32))
                    B.QT = sb4("QT", [P, NCH, 2, P])
                    B.GT, B.HS = sb4("GT", [P, NCH, 2, 64]), sb4("HS", [P, NCH, 2, 64])
                    B.Y = sb4("Y_rwkv", [P, T])
                    B.gate = sb4("gate_rwkv", [P, T])
                    rwkv_chunks(nc, A, G, B)
                    rwkv_finish(nc, A, G, B, p, next_at)

            with nc.Fori(0, 3) as p:
                pair(p, p * P + (RK + P))
            pair(3, GQ)
    with ExitStack() as c2:
        def sb2(n, s):
            return c2.enter_context(nc.sbuf_tensor(n, s, F32))
        B = Names()
        B.q, B.k = sb2("gla_q", [P, 2, T]), sb2("gla_k", [P, 2, T])
        B.b, B.qd, B.sG = sb2("gla_b", [P, 2, T]), sb2("gla_qd", [P, 2, T]), sb2("gla_sG", [P, 2, T])
        B.V = sb2("gla_V", [P, NCH, 2 * P])
        B.KN, B.A = sb2("gla_KN", [P, 2, NCH, P]), sb2("gla_A", [P, NCH, 2, P])
        B.tot = sb2("gla_tot", [P, 2, NCH])
        for g in range(2):
            gla_prep(nc, A, G, B, g)
            gla_scores(nc, A, G, B)
            gla_out(nc, A, G, B, g, GQ + P if g == 0 else None)


_INS = ['x', 'c', 'ctx', 'c_ctx', 'mod_w', 'mod_b', 'ln_g', 'ln_b', 'e_w_in', 'e_w_out', 'gla_wa2_f',
        'gla_ba_f', 'gla_wa2_b', 'gla_ba_b', 'gla_norm_g', 'rwkv_mu', 'rwkv_w0_f', 'rwkv_ww2_f',
        'rwkv_w0_b', 'rwkv_ww2_b', 'rwkv_a0_f', 'rwkv_wa2_f', 'rwkv_a0_b', 'rwkv_wa2_b', 'rwkv_k_k',
        'rwkv_k_a', 'rwkv_r_k', 'rwkv_gn_g', 'rwkv_gn_b', 'o_w_in', 'o_w_out', 'ml_conv_w', 'ml_conv_b',
        'ml_wq', 'ml_wk', 'ml_wv', 'ml_wi_f', 'ml_bi_f', 'ml_wf_f', 'ml_bf_f', 'ml_wi_b', 'ml_bi_b',
        'ml_wf_b', 'ml_bf_b', 'ml_norm_g', 'ml_skip']


def kernel(**inputs):
    import concourse.bacc as bacc
    from concourse.bass_utils import run_bass_kernel_spmd

    nc = bacc.Bacc("TRN2", target_bir_lowering=False, num_devices=1)
    arrays, args = {}, {}
    for name in _INS + ["consts"]:
        a = np.concatenate(list(constants().values()), 1) if name == "consts" else inputs[name]
        a = np.ascontiguousarray(a)
        arrays[f"in_{name}_dram"] = a
        args[name] = nc.dram_tensor(f"in_{name}_dram", a.shape, mybir.dt.from_np(a.dtype), kind="ExternalInput").ap()
    out = nc.dram_tensor("out_0_dram", (1, SEQ, D), F32, kind="ExternalOutput").ap()
    build(nc, args, out)
    r = run_bass_kernel_spmd(nc, [arrays], core_ids=[0])
    return r.results[0]["out_0_dram"]
```
